# Optimizing a Trainium2 kernel written in Bass

```python
import jax, jax.numpy as jnp
from jax import lax
import numpy as np

D_MODEL = 1024
BATCH = 1
SEQ = 512
DEPTH = 1
DEC_BATCH = 8
DEC_SEQ = 16
PAST_LEN = 1024

CHUNK = 64
HEAD_DIM = 64
ATT_SCALE = HEAD_DIM ** -0.5
FOX_HEADS = 8
FOX_QBLK = 128
SWA_HEADS = 8
SWA_KV_HEADS = 2
SWA_GROUP = SWA_HEADS // SWA_KV_HEADS
WINDOW = 128
WINDOW_CHUNKS = WINDOW // CHUNK
N_EXPERTS = 64
TOP_K = 8
N_GROUPS = 8
TOPK_GROUPS = 4
D_EXPERT = 256
D_SHARED = 256
ROUTED_SCALE = 2.5
EXPERT_BLOCK = 256
RMS_EPS = 1e-6
NEG_INF = -1e30

FOX_W = FOX_HEADS * HEAD_DIM
SWA_QW = SWA_HEADS * HEAD_DIM
SWA_KW = SWA_KV_HEADS * HEAD_DIM
IN_SPLIT_SIZES = (FOX_W, FOX_W, FOX_W, FOX_HEADS, SWA_QW, SWA_KW, SWA_KW, D_MODEL, D_MODEL)
IN_SPLITS = tuple(int(v) for v in np.cumsum(IN_SPLIT_SIZES)[:-1])
D_IN = sum(IN_SPLIT_SIZES)

kernel_name = 'hybrid_fox_swa_moe_streaming_step'

def rmsnorm(x, g):
    xf = x.astype(jnp.float32)
    y = xf * lax.rsqrt(jnp.mean(xf * xf, axis=-1, keepdims=True) + RMS_EPS)
    return (y * g.astype(jnp.float32)).astype(x.dtype)

def alibi_slopes(n):
    return jnp.asarray([2.0 ** (-8.0 * (i + 1) / n) for i in range(n)], dtype=jnp.float32)

def ada_mod(c, w_ada, b_ada):
    m = jax.nn.silu(c) @ w_ada + b_ada
    return [t[:, None, :] for t in jnp.split(m, 6, axis=-1)]

def modulate(x, g, shift, scale):
    return rmsnorm(x, g) * (1 + scale) + shift

def sink_softmax(s, sink):
    m = jnp.maximum(jnp.max(s, axis=-1, keepdims=True), sink)
    e = jnp.exp(s - m)
    return e / (jnp.sum(e, axis=-1, keepdims=True) + jnp.exp(sink - m))

def mixer_inputs(h, w_in, b_f):
    B, S, _ = h.shape
    z = h @ w_in
    qa, ka, va, fa, qb, kb, vb, ga, gb = jnp.split(z, IN_SPLITS, axis=-1)
    heads = lambda t, n: t.reshape(B, S, n, HEAD_DIM)
    logf = jax.nn.log_sigmoid(fa.astype(jnp.float32) + b_f.astype(jnp.float32))
    return (heads(qa, FOX_HEADS), heads(ka, FOX_HEADS), heads(va, FOX_HEADS), logf,
            heads(qb, SWA_HEADS), heads(kb, SWA_KV_HEADS), heads(vb, SWA_KV_HEADS), ga, gb)

def mixer_output(oa, ob, ga, gb, w_ba, w_bb, w_out):
    ya = oa @ w_ba
    yb = ob @ w_bb
    return (jax.nn.sigmoid(ga) * ya + jax.nn.sigmoid(gb) * yb) @ w_out

def fox_prompt(q, k, v, fcum):
    B, S, H, Dh = q.shape
    nqb = S // FOX_QBLK
    qb = q.reshape(B, nqb, FOX_QBLK, H, Dh).swapaxes(0, 1)
    fq = fcum.reshape(B, nqb, FOX_QBLK, H).swapaxes(0, 1)
    fk = fcum.transpose(0, 2, 1)
    kpos = jnp.arange(S)

    def block(args):
        q_i, fq_i, i = args
        s = jnp.einsum('bqhd,bkhd->bhqk', q_i, k, preferred_element_type=jnp.float32) * ATT_SCALE
        s = s + fq_i.transpose(0, 2, 1)[..., None] - fk[:, :, None, :]
        qpos = i * FOX_QBLK + jnp.arange(FOX_QBLK)
        s = jnp.where(kpos[None, :] <= qpos[:, None], s, NEG_INF)
        p = jax.nn.softmax(s, axis=-1)
        return jnp.einsum('bhqk,bkhd->bqhd', p.astype(v.dtype), v)

    o = lax.map(block, (qb, fq, jnp.arange(nqb)))
    return o.swapaxes(0, 1).reshape(B, S, H * Dh)

def fox_sample(q, k_new, v_new, logf_new, ck, cv, clogf):
    B, N, H, Dh = q.shape
    L = ck.shape[1]
    k = jnp.concatenate([ck, k_new.astype(ck.dtype)], axis=1)
    v = jnp.concatenate([cv, v_new.astype(cv.dtype)], axis=1)
    clf = clogf.astype(jnp.float32)
    logf = jnp.concatenate([clf, logf_new], axis=1)
    fk = jnp.cumsum(logf, axis=1) - jnp.sum(clf, axis=1, keepdims=True)
    fq = fk[:, L:]
    s = jnp.einsum('bqhd,bkhd->bhqk', q, k, preferred_element_type=jnp.float32) * ATT_SCALE
    s = s + fq.transpose(0, 2, 1)[..., None] - fk.transpose(0, 2, 1)[:, :, None, :]
    kidx = jnp.arange(L + N)
    qidx = L + jnp.arange(N)
    s = jnp.where(kidx[None, :] <= qidx[:, None], s, NEG_INF)
    p = jax.nn.softmax(s, axis=-1)
    o = jnp.einsum('bhqk,bkhd->bqhd', p.astype(v.dtype), v)
    return o.reshape(B, N, H * Dh)

def swa_prompt(q, k, v, sinks, slopes):
    B, S, H, Dh = q.shape
    NC = S // CHUNK
    KB = (WINDOW_CHUNKS + 1) * CHUNK
    qc = q.reshape(B, NC, CHUNK, SWA_KV_HEADS, SWA_GROUP, Dh)
    pad = ((0, 0), (WINDOW_CHUNKS * CHUNK, 0), (0, 0), (0, 0))
    kp = jnp.pad(k, pad).reshape(B, NC + WINDOW_CHUNKS, CHUNK, SWA_KV_HEADS, Dh)
    vp = jnp.pad(v, pad).reshape(B, NC + WINDOW_CHUNKS, CHUNK, SWA_KV_HEADS, Dh)
    kband = jnp.concatenate([kp[:, i:i + NC] for i in range(WINDOW_CHUNKS + 1)], axis=2)
    vband = jnp.concatenate([vp[:, i:i + NC] for i in range(WINDOW_CHUNKS + 1)], axis=2)
    s = jnp.einsum('bcqhgd,bckhd->bchgqk', qc, kband, preferred_element_type=jnp.float32) * ATT_SCALE
    cidx = jnp.arange(NC)
    qpos = (cidx * CHUNK)[:, None] + jnp.arange(CHUNK)[None, :]
    kpos = ((cidx - WINDOW_CHUNKS) * CHUNK)[:, None] + jnp.arange(KB)[None, :]
    dist = jnp.abs(qpos[:, :, None] - kpos[:, None, :]).astype(jnp.float32)
    sl = slopes.reshape(SWA_KV_HEADS, SWA_GROUP)
    s = s - sl[None, None, :, :, None, None] * dist[None, :, None, None, :, :]
    s = jnp.where((kpos >= 0)[None, :, None, None, None, :], s, NEG_INF)
    sk = sinks.astype(jnp.float32).reshape(SWA_KV_HEADS, SWA_GROUP)[None, None, :, :, None, None]
    p = sink_softmax(s, sk)
    o = jnp.einsum('bchgqk,bckhd->bcqhgd', p.astype(vband.dtype), vband)
    return o.reshape(B, S, H * Dh)

def swa_sample(q, k_new, v_new, ck, cv, sinks, slopes):
    B, N, H, Dh = q.shape
    W = ck.shape[1]
    k = jnp.concatenate([ck, k_new.astype(ck.dtype)], axis=1)
    v = jnp.concatenate([cv, v_new.astype(cv.dtype)], axis=1)
    qg = q.reshape(B, N, SWA_KV_HEADS, SWA_GROUP, Dh)
    s = jnp.einsum('bqhgd,bkhd->bhgqk', qg, k, preferred_element_type=jnp.float32) * ATT_SCALE
    dist = jnp.abs((W + jnp.arange(N))[:, None] - jnp.arange(W + N)[None, :]).astype(jnp.float32)
    sl = slopes.reshape(SWA_KV_HEADS, SWA_GROUP)
    s = s - sl[None, :, :, None, None] * dist[None, None, None]
    sk = sinks.astype(jnp.float32).reshape(SWA_KV_HEADS, SWA_GROUP)[None, :, :, None, None]
    p = sink_softmax(s, sk)
    o = jnp.einsum('bhgqk,bkhd->bqhgd', p.astype(v.dtype), v)
    return o.reshape(B, N, H * Dh), k[:, -W:], v[:, -W:]

def swiglu(x, wg, wu, wd):
    return (jax.nn.silu(x @ wg) * (x @ wu)) @ wd

def moe(x, w_router, router_bias, w_gate, w_up, w_down, w_sh_gate, w_sh_up, w_sh_down):
    T, D = x.shape
    scores = jax.nn.sigmoid((x @ w_router).astype(jnp.float32))
    sel = scores + router_bias.astype(jnp.float32)
    grp = sel.reshape(T, N_GROUPS, N_EXPERTS // N_GROUPS)
    grp_score = jnp.sum(lax.top_k(grp, 2)[0], axis=-1)
    _, gidx = lax.top_k(grp_score, TOPK_GROUPS)
    gmask = jnp.any(gidx[..., None] == jnp.arange(N_GROUPS), axis=1)
    emask = jnp.repeat(gmask, N_EXPERTS // N_GROUPS, axis=1)
    _, eidx = lax.top_k(jnp.where(emask, sel, NEG_INF), TOP_K)
    gw = jnp.take_along_axis(scores, eidx, axis=1)
    gw = gw / jnp.sum(gw, axis=-1, keepdims=True) * ROUTED_SCALE
    A = T * TOP_K
    flat_e = eidx.reshape(-1)
    flat_t = jnp.repeat(jnp.arange(T, dtype=jnp.int32), TOP_K)
    flat_w = gw.reshape(-1)
    order = jnp.argsort(flat_e)
    se, st, sw = flat_e[order], flat_t[order], flat_w[order]
    counts = jnp.bincount(flat_e, length=N_EXPERTS)
    padded = (counts + EXPERT_BLOCK - 1) // EXPERT_BLOCK * EXPERT_BLOCK
    start = jnp.cumsum(counts) - counts
    pend = jnp.cumsum(padded)
    pstart = pend - padded
    dest = pstart[se] + jnp.arange(A) - start[se]
    n_blocks = -(-A // EXPERT_BLOCK) + N_EXPERTS
    P = n_blocks * EXPERT_BLOCK
    row_tok = jnp.full((P,), T, dtype=jnp.int32).at[dest].set(st)
    row_w = jnp.zeros((P,), jnp.float32).at[dest].set(sw)
    blk_e = jnp.minimum(jnp.searchsorted(pend, jnp.arange(n_blocks) * EXPERT_BLOCK, side='right'),
                        N_EXPERTS - 1)
    x_ext = jnp.concatenate([x, jnp.zeros((1, D), x.dtype)], axis=0)

    def body(b, acc):
        tok = lax.dynamic_slice_in_dim(row_tok, b * EXPERT_BLOCK, EXPERT_BLOCK)
        rw = lax.dynamic_slice_in_dim(row_w, b * EXPERT_BLOCK, EXPERT_BLOCK)
        e = blk_e[b]
        yb = swiglu(x_ext[tok], w_gate[e], w_up[e], w_down[e]).astype(jnp.float32)
        return acc.at[tok].add(yb * rw[:, None])

    acc = lax.fori_loop(0, n_blocks, body, jnp.zeros((T + 1, D), jnp.float32))
    shared = swiglu(x, w_sh_gate, w_sh_up, w_sh_down).astype(jnp.float32)
    return (acc[:T] + shared).astype(x.dtype)

def setup_inputs(seed: int = 0) -> dict:
    key = jax.random.key(seed)
    ks = jax.random.split(key, 32)
    f32 = jnp.float32
    rn = lambda k, shape: jax.random.normal(k, shape, f32)
    w = lambda k, shape, fan_in: rn(k, shape) * fan_in ** -0.5
    swa_rows = min(WINDOW, PAST_LEN)
    return {
        'x_prompt': rn(ks[0], (BATCH, SEQ, D_MODEL)),
        'x_sample': rn(ks[1], (DEC_BATCH, DEC_SEQ, D_MODEL)),
        'cache_fox_k': rn(ks[2], (DEPTH, DEC_BATCH, PAST_LEN, FOX_HEADS, HEAD_DIM)),
        'cache_fox_v': rn(ks[3], (DEPTH, DEC_BATCH, PAST_LEN, FOX_HEADS, HEAD_DIM)),
        'cache_fox_logf': jax.nn.log_sigmoid(3.0 + 0.5 * rn(ks[4], (DEPTH, DEC_BATCH, PAST_LEN, FOX_HEADS))),
        'cache_swa_k': rn(ks[5], (DEPTH, DEC_BATCH, swa_rows, SWA_KV_HEADS, HEAD_DIM)),
        'cache_swa_v': rn(ks[6], (DEPTH, DEC_BATCH, swa_rows, SWA_KV_HEADS, HEAD_DIM)),
        'c_prompt': rn(ks[7], (BATCH, D_MODEL)),
        'c_sample': rn(ks[8], (DEC_BATCH, D_MODEL)),
        'w_ada': 0.5 * w(ks[9], (DEPTH, D_MODEL, 6 * D_MODEL), D_MODEL),
        'b_ada': 0.02 * rn(ks[10], (DEPTH, 6 * D_MODEL)),
        'norm1_g': 1.0 + 0.1 * rn(ks[11], (DEPTH, D_MODEL)),
        'w_in': w(ks[12], (DEPTH, D_MODEL, D_IN), D_MODEL),
        'fox_b_f': 3.0 + 0.5 * rn(ks[13], (DEPTH, FOX_HEADS)),
        'w_branch_a': w(ks[14], (DEPTH, FOX_W, D_MODEL), FOX_W),
        'w_branch_b': w(ks[15], (DEPTH, SWA_QW, D_MODEL), SWA_QW),
        'w_out': w(ks[16], (DEPTH, D_MODEL, D_MODEL), D_MODEL),
        'swa_sinks': 0.5 * rn(ks[17], (DEPTH, SWA_HEADS)),
        'norm2_g': 1.0 + 0.1 * rn(ks[18], (DEPTH, D_MODEL)),
        'w_router': w(ks[19], (DEPTH, D_MODEL, N_EXPERTS), D_MODEL),
        'router_bias': 0.01 * rn(ks[20], (DEPTH, N_EXPERTS)),
        'w_exp_gate': w(ks[21], (DEPTH, N_EXPERTS, D_MODEL, D_EXPERT), D_MODEL),
        'w_exp_up': w(ks[22], (DEPTH, N_EXPERTS, D_MODEL, D_EXPERT), D_MODEL),
        'w_exp_down': w(ks[23], (DEPTH, N_EXPERTS, D_EXPERT, D_MODEL), D_EXPERT),
        'w_sh_gate': w(ks[24], (DEPTH, D_MODEL, D_SHARED), D_MODEL),
        'w_sh_up': w(ks[25], (DEPTH, D_MODEL, D_SHARED), D_MODEL),
        'w_sh_down': w(ks[26], (DEPTH, D_SHARED, D_MODEL), D_SHARED),
        'final_g': 1.0 + 0.1 * rn(ks[27], (D_MODEL,)),
    }

def reference(x_prompt, x_sample, cache_fox_k, cache_fox_v, cache_fox_logf, cache_swa_k, cache_swa_v,
              c_prompt, c_sample, w_ada, b_ada, norm1_g, w_in, fox_b_f, w_branch_a, w_branch_b, w_out,
              swa_sinks, norm2_g, w_router, router_bias, w_exp_gate, w_exp_up, w_exp_down,
              w_sh_gate, w_sh_up, w_sh_down, final_g):
    slopes = alibi_slopes(SWA_HEADS)
    xp, xs = x_prompt, x_sample
    B, S, D = xp.shape
    DB, N, _ = xs.shape
    rows_p = min(WINDOW, S)
    fkp, fvp, flp, skp, svp = [], [], [], [], []
    fks, fvs, fls, sks, svs = [], [], [], [], []
    for l in range(DEPTH):
        mp = ada_mod(c_prompt, w_ada[l], b_ada[l])
        ms = ada_mod(c_sample, w_ada[l], b_ada[l])
        hp = modulate(xp, norm1_g[l], mp[0], mp[1])
        qa, ka, va, lf, qb, kb, vb, ga, gb = mixer_inputs(hp, w_in[l], fox_b_f[l])
        oa = fox_prompt(qa, ka, va, jnp.cumsum(lf, axis=1))
        ob = swa_prompt(qb, kb, vb, swa_sinks[l], slopes)
        xp = xp + mp[2] * mixer_output(oa, ob, ga, gb, w_branch_a[l], w_branch_b[l], w_out[l])
        fkp.append(ka); fvp.append(va); flp.append(lf)
        skp.append(kb[:, S - rows_p:]); svp.append(vb[:, S - rows_p:])
        hs = modulate(xs, norm1_g[l], ms[0], ms[1])
        qa, ka, va, lf, qb, kb, vb, ga, gb = mixer_inputs(hs, w_in[l], fox_b_f[l])
        oa = fox_sample(qa, ka, va, lf, cache_fox_k[l], cache_fox_v[l], cache_fox_logf[l])
        ob, swk, swv = swa_sample(qb, kb, vb, cache_swa_k[l], cache_swa_v[l], swa_sinks[l], slopes)
        xs = xs + ms[2] * mixer_output(oa, ob, ga, gb, w_branch_a[l], w_branch_b[l], w_out[l])
        fks.append(ka); fvs.append(va); fls.append(lf); sks.append(swk); svs.append(swv)
        hp2 = modulate(xp, norm2_g[l], mp[3], mp[4]).reshape(B * S, D)
        hs2 = modulate(xs, norm2_g[l], ms[3], ms[4]).reshape(DB * N, D)
        y = moe(jnp.concatenate([hp2, hs2], axis=0), w_router[l], router_bias[l], w_exp_gate[l],
                w_exp_up[l], w_exp_down[l], w_sh_gate[l], w_sh_up[l], w_sh_down[l])
        xp = xp + mp[5] * y[:B * S].reshape(B, S, D)
        xs = xs + ms[5] * y[B * S:].reshape(DB, N, D)
    y_prompt = rmsnorm(xp, final_g)
    y_sample = rmsnorm(xs, final_g)
    return (y_prompt, y_sample,
            jnp.stack(fkp), jnp.stack(fvp), jnp.stack(flp), jnp.stack(skp), jnp.stack(svp),
            jnp.stack(fks), jnp.stack(fvs), jnp.stack(fls), jnp.stack(sks), jnp.stack(svs))


_drawn_inputs = setup_inputs


def setup_inputs(seed=0):
    import zlib

    import numpy as np

    out = dict(_drawn_inputs(seed))
    spreads = {}
    factors = {'cache_fox_logf': 43.995, 'swa_sinks': 8.0}
    for name, (base, spread) in spreads.items():
        noise = np.random.default_rng([zlib.crc32(name.encode()), seed]).standard_normal(out[name].shape)
        drawn = base * np.exp(spread * noise) if base else spread * noise
        out[name] = __import__('jax').numpy.asarray(drawn.astype(out[name].dtype))
    for name, factor in factors.items():
        out[name] = (out[name] * factor).astype(out[name].dtype)
    return out
```

```python
from contextlib import ExitStack

import concourse.bass as bass
from concourse import mybir

F32 = mybir.dt.float32
I32 = mybir.dt.int32
U32 = mybir.dt.uint32
ALU = mybir.AluOpType
ACT = mybir.ActivationFunctionType
AX = mybir.AxisListType.X

P = 128
D = 1024
KC = D // P
SEQ, DB, DN, PAST = 512, 8, 16, 1024
TOK = SEQ + DB * DN
NT = TOK // P
PT = SEQ // P
H, HD = 8, 64
HW = H * HD
KVH = 2
KW = KVH * HD
GROUP = H // KVH
SINKW = 128
NE, TOPK, NG, TOPG = 64, 8, 8, 4
FE = 256
ROUTED_SCALE = 2.5
EPS = 1e-6
NEG = -1e30
ATT_SCALE = HD ** -0.5
PAIRS = (TOK * TOPK // P + NE + 1) // 2 + 1
SLOTS = 2 * PAIRS
JC = PAST // P
NM = 6 * D
O_Q, O_K, O_V, O_F = 0, HW, 2 * HW, 3 * HW
O_QB = 3 * HW + H
O_KB = O_QB + HW
O_GA = O_KB + 2 * KW
O_GB = O_GA + D
CONST = {}
_at = 0
for _name, _n in (("ident", P), ("tri_incl", P), ("tri_strict", P), ("suffix", P), ("ones", P), ("causal", P),
                  ("same", P), ("swa_dist", 2 * P), ("others", P), ("fox_new", DN), ("swa_old", P), ("swa_new", DN),
                  ("headmask", HW), ("groupmask", KW), ("fold16", DN), ("fold64", GROUP * DN),
                  ("ties", NG * NG), ("iota64", NE), ("pairs2", PAIRS), ("pcol", 1)):
    CONST[_name] = (_at, _n)
    _at += _n
NCONST = _at


def constants(np):
    c = np.zeros((P, NCONST), np.float32)
    p = np.arange(P)

    def put(name, a):
        at, n = CONST[name]
        c[:, at:at + n] = np.broadcast_to(a, (P, n))

    put("ident", np.eye(P))
    put("tri_incl", p[:, None] <= p[None])
    put("tri_strict", p[:, None] < p[None])
    put("suffix", p[:, None] > p[None])
    put("ones", np.ones((P, P)))
    put("causal", np.where(p[None] <= p[:, None], 0.0, NEG))
    b, n = p // DN, p % DN
    put("same", -((b[:, None] == b[None]) & (n[:, None] <= n[None])).astype(np.float32))
    key = np.arange(2 * P) - P
    d = np.abs(p[:, None] - key[None]).astype(np.float32)
    ok = (key[None] // 64 >= p[:, None] // 64 - 2) & (key[None] // 64 <= p[:, None] // 64)
    put("swa_dist", np.where(ok, d, 3e32))
    h, q = p // DN, p % DN
    slope = 2.0 ** (-8.0 * (h + 1) / H)
    k = np.arange(DN)
    put("others", np.where((p[:, None] < DB * H) & (b[None] != p[:, None] // H), NEG, 0.0))
    put("fox_new", np.where(k[None] <= q[:, None], 0.0, NEG))
    put("swa_old", -slope[:, None] * (SINKW + q[:, None] - p[None]))
    put("swa_new", -slope[:, None] * np.abs(q[:, None] - k[None]))
    put("headmask", h[:, None] == np.arange(HW)[None] // HD)
    put("groupmask", h[:, None] // GROUP == np.arange(KW)[None] // HD)
    put("fold16", q[:, None] == np.arange(DN)[None])
    i = np.arange(GROUP * DN)
    put("fold64", (h[:, None] % GROUP == i[None] // DN) & (q[:, None] == i[None] % DN))
    g = np.arange(NG)
    put("ties", (g[None] < g[:, None]).reshape(1, -1))
    put("iota64", np.arange(NE)[None])
    put("pairs2", 2 * (1 + np.arange(PAIRS))[None])
    put("pcol", p[:, None])
    return c


class Steps:

    def __init__(self, eng, sem):
        self.eng, self.sem, self.base, self.n = eng, sem, 0, 0

    def link(self, ins):
        self.n += 1
        ins.then_inc(self.sem, 1)
        self.eng.wait_ge(self.sem, self.base + self.n)

    def resume(self, eng):
        self.eng = eng
        return self

    def loop(self, base):
        self.base, self.n = base, 0


def cdiv(a, b):
    return -(-a // b)


def build(nc, a, o):
    with ExitStack() as ctx:
        def sem(name):
            return ctx.enter_context(nc.semaphore(name))

        def scratch(name, shape, dt=F32):
            return nc.dram_tensor(name, shape, dt, kind="Internal").ap()

        S = {}
        ps = ctx.enter_context(nc.psum_tensor("ps", [P, 8, 512], F32))
        mod_d = scratch("mod_d", [1 + DB, NM])
        h2_d = scratch("h2_d", [TOK, D])
        acc_d = scratch("acc_d", [TOK + P, D])
        tab_d = scratch("tab_d", [SLOTS * P, 2], U32)

        sizes = dict(wst=9 * DB * H, const=NCONST, x=NT * D, hT=KC * TOK, Q=NT * D, ring=4 * KC * 512,
                     qbT=GROUP * TOK, kbT=TOK, v=NT * HW, kvb=NT * 2 * KW, oaT=4 * TOK, obT=4 * TOK,
                     work=4 * D, biasT=PAST + P, logf=NT * H + JC * DB * H, small=336)
        R = {}
        for name, n in sizes.items():
            R[name] = ctx.enter_context(nc.sbuf_tensor("r_" + name, [P, n], F32))

        def C(name, rows=P):
            at, n = CONST[name]
            return R["const"][0:rows, at:at + n]

        env = dict(nc=nc, a=a, o=o, ps=ps, R=R, C=C, sem=sem, mod_d=mod_d, h2_d=h2_d, acc_d=acc_d,
                   tab_d=tab_d, S=S)
        env["counts"] = ctx.enter_context(nc.sbuf_tensor("counts", [P, 1 + P], I32))
        env["table"] = R["biasT"][:, 0:2 * SLOTS].bitcast(U32)
        env["kv"] = [sem("k_cache_even"), sem("k_cache_odd"), sem("v_cache_even"), sem("v_cache_odd")]
        env["dve_steps"] = Steps(None, sem("dve_steps"))
        for stage in (project_stage, prompt_stage, sample_stage, mix_stage, expert_stage, final_stage):
            stage(env)


def carve(region, *shapes):
    out, at = [], 0
    for shape in shapes:
        n = 1
        for s in shape:
            n *= s
        v = region[:, at:at + n]
        if len(shape) == 2:
            v = v.rearrange("p (x y) -> p x y", y=shape[1])
        elif len(shape) == 3:
            v = v.rearrange("p (x y z) -> p x y z", y=shape[1], z=shape[2])
        out.append(v)
        at += n
    return out if len(out) > 1 else out[0]


def project_stage(env):
    nc, a, o, ps, R, C, sem = (env[k] for k in ("nc", "a", "o", "ps", "R", "C", "sem"))
    mod_d = env["mod_d"]
    x = carve(R["x"], (NT, D))
    hT = carve(R["hT"], (KC, TOK))
    hrow = carve(R["Q"], (NT, D))
    qT, kT = carve(R["Q"], (4, TOK), (4, TOK))
    qbT = carve(R["qbT"], (GROUP, TOK))
    kbT = R["kbT"]
    v = carve(R["v"], (NT, HW))
    kvb = carve(R["kvb"], (NT, 2 * KW))
    ring = [R["ring"][:, s * 4096:(s + 1) * 4096] for s in range(4)]
    modp = carve(R["work"], (2, D))
    mods = carve(R["work"][:, 2 * D:], (2, D))
    logf = carve(R["logf"], (NT, H))
    clogf = R["logf"][:, NT * H:].rearrange("p (b j h) -> p b (j h)", b=DB, h=H)
    m_sb = carve(R["oaT"], (2, D))[0:1 + DB, :, :]
    b_sb = carve(R["obT"], (2, D))[0:1 + DB, :, :]
    c_sb = R["kvb"][0:1 + DB, 0:D]
    g1_sb = R["v"][0:1 + DB, 0:D]
    g2_sb = R["v"][0:1 + DB, D:2 * D]
    sg_sb = R["qbT"][0:1 + DB, 0:D]
    cT = carve(R["biasT"], (KC, 1 + DB))
    stat, rstd, bf, lt = carve(R["small"], (NT,), (NT,), (H,), (5, NT * H))
    kst = carve(R["oaT"], (2, HW))
    sq = carve(R["obT"], (D,), )

    s_const, s_c, s_g = sem("a_const"), sem("a_c_rows"), sem("a_norm_gains")
    s_x = sem("a_x_rows")
    s_clf = env["S"]["cached_logf"] = sem("cached_logf")
    s_bada = [sem("a_bias_part0"), sem("a_bias_part1")]
    s_w = [sem(f"a_w_slot{i}") for i in range(4)]
    s_mout = [sem("a_mod_stored0"), sem("a_mod_stored1")]
    s_mod = sem("a_mod_loaded")
    s_sig, s_silu, s_cT, s_cTc = sem("a_sigmoid_c"), sem("a_silu_c"), sem("a_cT_psum"), sem("a_cT_sbuf")
    s_ada, s_left, s_m = sem("a_ada_psum"), sem("a_ada_left_psum"), sem("a_scale_rows")
    s_sq, s_var, s_rt = sem("a_sumsq"), sem("a_variance"), sem("a_root")
    s_h, s_tr = sem("a_h_rows"), sem("a_h_transposed")
    s_hTa, s_hTv = sem("a_hT_by_act"), sem("a_hT_by_dve")
    s_mm, s_ea, s_ev = sem("a_proj_psum"), sem("a_proj_by_act"), sem("a_proj_by_dve")
    s_lf, s_exp, s_ln = sem("a_logit"), sem("a_exp_logit"), sem("a_ln")
    s_o = sem("a_outputs")
    s_ko = [sem("a_k_rows_stored0"), sem("a_k_rows_stored1")]

    w_in = a["w_in"][0].rearrange("(k p) n -> p k n", p=P)
    w_ada = a["w_ada"][0].rearrange("(k p) n -> p k n", p=P)
    pieces = [(w_ada[:, :, 512 * n:512 * (n + 1)], 512) for n in range(NM // 512)]
    NA = len(pieces)
    pieces += [(w_in[:, :, O_Q:O_Q + 512], 512), (w_in[:, :, O_K:O_K + 512], 512),
               (w_in[:, :, O_V:O_V + 512], 512), (w_in[:, :, O_F:O_F + H], H),
               (w_in[:, :, O_KB:O_KB + 2 * KW], 2 * KW), (w_in[:, :, O_QB:O_QB + 512], 512)]
    W_Q, W_K, W_V, W_F, W_KV, W_QB = range(NA, NA + 6)

    def wslot(n):
        return carve(ring[n % 4], (KC, pieces[n][1]))

    wqb = carve(ring[W_V % 4], (KC, 512))
    s_perm = sem("a_w_qb_reordered")

    jobs = []
    for c in range(4):
        jobs += [("q", c, 0), ("q", c, 1)]
    for c in range(4):
        jobs += [("k", c, 0), ("k", c, 1)]
    for t in range(NT):
        jobs += [("v", t, 0)]
    for t in range(NT):
        jobs += [("f", t, 0)]
    for t in range(NT):
        jobs += [("kv", t, 0)]
    for c in range(4):
        jobs += [("qb", c, 0), ("qb", c, 1)]
    for t in range(NT):
        jobs += [("kbT", t, 0)]
    for t in range(NT):
        jobs += [("krow", t, 0)]
    job_no = {j: n for n, j in enumerate(jobs)}
    by_act = [n % 2 == 0 and j[0] != "f" for n, j in enumerate(jobs)]
    done_a = [sum(by_act[:n + 1]) for n in range(len(jobs))]
    done_v = [n + 1 - done_a[n] for n in range(len(jobs))]
    PB = 6

    def job_done(eng, n):
        if by_act[n]:
            eng.wait_ge(s_ea, done_a[n])
        else:
            eng.wait_ge(s_ev, done_v[n])

    def last_use(n):
        if n < NA:
            return s_ada, n + 1
        kind = {W_Q: "q", W_K: "k", W_V: "v", W_F: "f", W_KV: "kv", W_QB: "qb"}[n]
        return s_mm, max(m for m, j in enumerate(jobs) if j[0] == kind) + 1

    def evacuate(eng, n, j):
        kind, i, part = j
        bank = ps[:, n % PB, :]
        if kind in ("q", "k", "qb"):
            dst = {"q": qT, "k": kT, "qb": qbT}[kind][:, i, 0:SEQ] if part == 0 else \
                {"q": qT, "k": kT, "qb": qbT}[kind][:, i, SEQ:TOK]
            src = bank if part == 0 else bank[:, 0:P]
            if kind == "k":
                return nc.scalar.copy(dst, src) if by_act[n] else nc.vector.tensor_copy(dst, src)
            if by_act[n]:
                return nc.scalar.mul(dst, src, ATT_SCALE)
            return nc.vector.tensor_scalar(dst, src, ATT_SCALE, None, ALU.mult)
        if kind == "krow" and i < 2:
            eng.wait_ge(s_mout[0], 48)
            eng.wait_ge(s_mout[1], 48)
        if kind == "krow" and i >= 2:
            eng.wait_ge(s_ko[i % 2], 16 * (i // 2))
        if kind == "f":
            return nc.vector.tensor_tensor(lt[:, 0, i * H:(i + 1) * H], bank[:, 0:H], bf, ALU.add)
        dst, src = {"v": (v[:, i, :], bank), "kv": (kvb[:, i, :], bank[:, 0:2 * KW]),
                    "kbT": (kbT[:, i * P:(i + 1) * P], bank[:, 0:P]), "krow": (kst[:, i % 2, :], bank)}[kind]
        return nc.scalar.copy(dst, src) if by_act[n] else nc.vector.tensor_copy(dst, src)

    with nc.Block() as block:
        @block.sync
        def _(sp):
            sp.dma_start(c_sb[0:1, :], a["c_prompt"]).then_inc(s_c, 16)
            sp.dma_start(c_sb[1:1 + DB, :], a["c_sample"]).then_inc(s_c, 16)
            sp.dma_start(R["const"][:, :], a["const"]).then_inc(s_const, 16)
            for part in range(2):
                sp.dma_start(b_sb[:, part, :], a["b_ada"][:, part * D:(part + 1) * D]
                             .to_broadcast([1 + DB, D])).then_inc(s_bada[part], 16)
            for n in range(NA + 6):
                if n >= 4:
                    s, val = last_use(n - 4)
                    sp.wait_ge(s, val)
                if n == W_F:
                    with nc.allow_non_contiguous_dma(reason="eight columns of forget logits"):
                        sp.dma_start(wslot(n), pieces[n][0]).then_inc(s_w[n % 4], 16)
                else:
                    sp.dma_start(wslot(n), pieces[n][0]).then_inc(s_w[n % 4], 16)
            for t in range(NT):
                job_done(sp, job_no[("v", t, 0)])
            sp.dma_start(o[3].rearrange("l b (t p) h d -> p (l b t) (h d)", p=P), v[:, 0:PT, :]).then_inc(s_o, 16)
            sp.dma_start(o[8].rearrange("l b n h d -> (l b n) (h d)"), v[:, PT, :]).then_inc(s_o, 16)
            sp.wait_ge(s_lf, 2)
            sp.dma_start(o[4].rearrange("l b (t p) h -> p (l b t) h", p=P), logf[:, 0:PT, :]).then_inc(s_o, 16)
            sp.dma_start(o[9].rearrange("l b n h -> (l b n) h"), logf[:, PT, :]).then_inc(s_o, 16)
            for t in range(NT):
                job_done(sp, job_no[("kv", t, 0)])
            for half, (po, so, cache) in enumerate(((o[5], o[10], a["cache_swa_k"]), (o[6], o[11], a["cache_swa_v"]))):
                cols = slice(half * KW, (half + 1) * KW)
                sp.dma_start(po.rearrange("l b p h d -> (l b p) (h d)"), kvb[:, PT - 1, cols]).then_inc(s_o, 16)
                win, old = so[0].rearrange("b s h d -> b s (h d)"), cache[0].rearrange("b s h d -> b s (h d)")
                sp.dma_start(win[:, 0:SINKW - DN, :], old[:, DN:SINKW, :]).then_inc(s_o, 16)
                for b in range(DB):
                    sp.dma_start(win[b, SINKW - DN:SINKW, :], kvb[b * DN:(b + 1) * DN, PT, cols]).then_inc(s_o, 16)
            kp = o[2].rearrange("l b (t p) h d -> (l b t) p (h d)", p=P)
            ks = o[7].rearrange("l b n h d -> (l b n) (h d)")
            for t in range(NT):
                job_done(sp, job_no[("krow", t, 0)])
                sp.dma_start(kp[t] if t < PT else ks, kst[:, t % 2, :]).then_inc(s_ko[t % 2], 16)
            sp.wait_ge(s_ko[0], 48)
            sp.wait_ge(s_ko[1], 32)
            sp.wait_ge(s_o, 16 * (4 + 2 * (2 + DB)))

        @block.scalar
        def _(act):
            act.dma_start(x[:, 0:PT, :], a["x_prompt"][0].rearrange("(t p) d -> p t d", p=P)).then_inc(s_x, 16)
            act.dma_start(x[:, PT, :], a["x_sample"].rearrange("b n d -> (b n) d")).then_inc(s_x, 16)
            act.dma_start(g1_sb, a["norm1_g"].to_broadcast([1 + DB, D])).then_inc(s_g, 16)
            act.dma_start(g2_sb, a["norm2_g"].to_broadcast([1 + DB, D])).then_inc(s_g, 16)
            act.dma_start(clogf, a["cache_fox_logf"][0].rearrange("b (p j) h -> p b (j h)", j=JC)).then_inc(s_clf, 16)
            act.dma_start(bf, a["fox_b_f"].to_broadcast([P, H])).then_inc(s_g, 16)
            act.wait_ge(s_c, 32)
            nc.scalar.activation(sg_sb, c_sb, ACT.Sigmoid).then_inc(s_sig, 1)
            act.wait_ge(s_x, 32)
            sq_v = R["qbT"][:, D:2 * D]
            for t in range(NT):
                if t:
                    act.wait_ge(s_sq, t)
                nc.scalar.activation(sq_v, x[:, t, :], ACT.Square, accum_out=stat[:, t:t + 1]).then_inc(s_sq, 1)
            act.wait_ge(s_var, 1)
            nc.scalar.activation(rstd, stat, ACT.Sqrt).then_inc(s_rt, 1)
            for part in range(6):
                if part in (1, 4):
                    act.wait_ge(s_m, 1 if part == 1 else 2)
                else:
                    act.wait_ge(s_left, 2 * part + 2)
                act.dma_start(mod_d[:, part * D:(part + 1) * D], m_sb[:, part % 2, :]).then_inc(s_mout[part % 2], 16)
                if part + 2 < 6:
                    act.dma_start(b_sb[:, part % 2, :], a["b_ada"][:, (part + 2) * D:(part + 3) * D]
                                  .to_broadcast([1 + DB, D])).then_inc(s_bada[part % 2], 16)
                if part == 1:
                    act.wait_ge(s_mout[0], 16)
                    act.wait_ge(s_mout[1], 16)
                    load_mod(act, mod_d, R["work"][:, 0:2 * D], R["work"][:, 2 * D:4 * D], 0, 2, s_mod)
            for n in range(0, 2 * NT, 2):
                act.wait_ge(s_tr, n + 1)
                t, g = n // 2, n % 2
                nc.scalar.copy(hT[:, 4 * g:4 * g + 4, t * P:(t + 1) * P],
                               ps[:, n % 4, :].rearrange("p (k t) -> p k t", t=P)).then_inc(s_hTa, 1)
            for n, j in enumerate(jobs):
                if by_act[n]:
                    act.wait_ge(s_mm, n + 1)
                    evacuate(act, n, j).then_inc(s_ea, 1)
                if j == ("f", NT - 1, 0):
                    act.wait_ge(s_lf, 1)
                    nc.scalar.activation(lt[:, 1, :], lt[:, 1, :], ACT.Exp, scale=-1.0).then_inc(s_exp, 1)
                    act.wait_ge(s_exp, 2)
                    nc.scalar.activation(lt[:, 3, :], lt[:, 2, :], ACT.Ln).then_inc(s_ln, 1)

        @block.tensor
        def _(pe):
            pe.wait_ge(s_const, 16)
            pe.wait_ge(s_silu, 1)
            for k in range(KC):
                last = nc.tensor.transpose(ps[:, 7, k * 9:(k + 1) * 9], sg_sb[:, k * P:(k + 1) * P],
                                           C("ident", 9)[:, 0:9])
            last.then_inc(s_cT, 1)
            pe.wait_ge(s_cTc, 1)
            for n in range(NA):
                pe.wait_ge(s_w[n % 4], 16 * (n // 4 + 1))
                if n >= 4:
                    pe.wait_ge(s_left, n - 3)
                for k in range(KC):
                    last = nc.tensor.matmul(ps[0:9, n % 4, :], cT[:, k, :], wslot(n)[:, k, :],
                                            start=(k == 0), stop=(k == KC - 1))
                last.then_inc(s_ada, 1)
            for n in range(2 * NT):
                t, g = n // 2, n % 2
                pe.wait_ge(s_h, t + 1)
                if n >= 4:
                    pe.wait_ge(s_hTa if n % 2 == 0 else s_hTv, (n - 4) // 2 + 1)
                else:
                    pe.wait_ge(s_left, NA - 3 + n)
                for k in range(4):
                    last = nc.tensor.transpose(ps[:, n % 4, k * P:(k + 1) * P],
                                               hrow[:, t, (4 * g + k) * P:(4 * g + k + 1) * P], C("ident"))
                last.then_inc(s_tr, 1)
            pe.wait_ge(s_hTa, NT)
            pe.wait_ge(s_hTv, NT)
            need = {"q": W_Q, "k": W_K, "v": W_V, "f": W_F, "kv": W_KV, "qb": W_QB}
            for n, (kind, i, part) in enumerate(jobs):
                if kind == "qb" and i == 0 and part == 0:
                    pe.wait_ge(s_perm, KVH)
                elif kind in need and i == 0 and part == 0:
                    m = need[kind]
                    pe.wait_ge(s_w[m % 4], 16 * (m // 4 + 1))
                if n >= PB:
                    job_done(pe, n - PB)
                bank = ps[:, n % PB, :]
                if kind in ("q", "k", "qb"):
                    w = wslot(need[kind])
                    out, cols = (bank, slice(0, SEQ)) if part == 0 else (bank[:, 0:P], slice(SEQ, TOK))
                    for k in range(KC):
                        lhsT = (wqb if kind == "qb" else w)[:, k, i * P:(i + 1) * P]
                        last = nc.tensor.matmul(out, lhsT, hT[:, k, cols], start=(k == 0), stop=(k == KC - 1))
                elif kind in ("v", "f", "kv"):
                    w = wslot(need[kind])
                    for k in range(KC):
                        last = nc.tensor.matmul(bank[:, 0:pieces[need[kind]][1]], hT[:, k, i * P:(i + 1) * P],
                                                w[:, k, :], start=(k == 0), stop=(k == KC - 1))
                elif kind == "kbT":
                    job_done(pe, job_no[("kv", i, 0)])
                    last = nc.tensor.transpose(bank[:, 0:P], kvb[:, i, 0:KW], C("ident"))
                else:
                    if i == 0:
                        job_done(pe, job_no[("k", 3, 0)])
                        job_done(pe, job_no[("k", 3, 1)])
                    for c in range(4):
                        last = nc.tensor.transpose(bank[:, c * P:(c + 1) * P], kT[:, c, i * P:(i + 1) * P], C("ident"))
                last.then_inc(s_mm, 1)

        @block.vector
        def _(dve):
            st = env["dve_steps"].resume(dve)
            dve.wait_ge(s_sig, 1)
            nc.vector.tensor_tensor(sg_sb, sg_sb, c_sb, ALU.mult).then_inc(s_silu, 1)
            dve.wait_ge(s_cT, 1)
            nc.vector.tensor_copy(cT, ps[:, 7, 0:KC * 9].rearrange("p (k m) -> p k m", m=9)).then_inc(s_cTc, 1)
            dve.wait_ge(s_sq, NT)
            nc.vector.tensor_scalar(stat, stat, 1.0 / D, EPS, ALU.mult, ALU.add).then_inc(s_var, 1)
            dve.wait_ge(s_rt, 1)
            st.link(nc.vector.reciprocal(rstd, rstd))
            dve.wait_ge(s_g, 48)

            def rows(t):
                mod = modp if t < PT else mods
                st.link(nc.vector.scalar_tensor_tensor(hrow[:, t, :], x[:, t, :], rstd[:, t:t + 1], mod[:, 1, :],
                                                       ALU.mult, ALU.mult))
                nc.vector.tensor_tensor(hrow[:, t, :], hrow[:, t, :], mod[:, 0, :], ALU.add).then_inc(s_h, 1)

            for part in range(6):
                if part >= 2:
                    dve.wait_ge(s_mout[part % 2], 16 * (part // 2))
                dve.wait_ge(s_bada[part % 2], 16 * (part // 2 + 1))
                for half in range(2):
                    n = 2 * part + half
                    dve.wait_ge(s_ada, n + 1)
                    ins = nc.vector.tensor_tensor(m_sb[:, part % 2, half * 512:(half + 1) * 512], ps[0:9, n % 4, :],
                                                  b_sb[:, part % 2, half * 512:(half + 1) * 512], ALU.add)
                    ins.then_inc(s_left, 1)
                if part in (1, 4):
                    dve.wait_ge(s_left, 2 * part + 2)
                    nc.vector.scalar_tensor_tensor(m_sb[:, part % 2, :], m_sb[:, part % 2, :], 1.0,
                                                   g1_sb if part == 1 else g2_sb, ALU.add, ALU.mult).then_inc(s_m, 1)
                if part == 3:
                    dve.wait_ge(s_mod, 32)
                if part >= 3:
                    rows(part - 3)
            rows(3)
            rows(4)
            for n in range(1, 2 * NT, 2):
                dve.wait_ge(s_tr, n + 1)
                t, g = n // 2, n % 2
                nc.vector.tensor_copy(hT[:, 4 * g:4 * g + 4, t * P:(t + 1) * P],
                                      ps[:, n % 4, :].rearrange("p (k t) -> p k t", t=P)).then_inc(s_hTv, 1)
            for n, j in enumerate(jobs):
                if not by_act[n]:
                    dve.wait_ge(s_mm, n + 1)
                    evacuate(dve, n, j).then_inc(s_ev, 1)
                if j == ("f", NT - 1, 0):
                    z, u, w, lnw, e = (lt[:, r, :] for r in range(5))
                    dve.wait_ge(s_ev, done_v[n])
                    st.link(nc.vector.tensor_scalar(u, z, -1.0, None, ALU.mult))
                    nc.vector.tensor_tensor(u, u, z, ALU.max).then_inc(s_lf, 1)
                    dve.wait_ge(s_exp, 1)
                    nc.vector.tensor_scalar(w, u, 1.0, None, ALU.add).then_inc(s_exp, 1)
                    dve.wait_ge(s_ln, 1)
                    st.link(nc.vector.tensor_scalar(w, w, -1.0, None, ALU.add))
                    st.link(nc.vector.tensor_scalar(e, w, 0.0, None, ALU.is_equal))
                    st.link(nc.vector.tensor_tensor(w, w, e, ALU.add))
                    st.link(nc.vector.tensor_tensor(lnw, lnw, e, ALU.add))
                    st.link(nc.vector.reciprocal(w, w))
                    st.link(nc.vector.tensor_tensor(u, u, lnw, ALU.mult))
                    st.link(nc.vector.tensor_tensor(u, u, w, ALU.mult))
                    st.link(nc.vector.tensor_scalar(z, z, 0.0, None, ALU.min))
                    nc.vector.tensor_tensor(R["logf"][:, 0:NT * H], z, u, ALU.subtract).then_inc(s_lf, 1)

        @block.gpsimd
        def _(pool):
            def reorder():
                pool.wait_ge(s_w[W_QB % 4], 16 * (W_QB // 4 + 1))
                pool.wait_ge(*last_use(W_V))
                for g in range(KVH):
                    src = wslot(W_QB).rearrange("p k (g i d) -> p k g i d", g=KVH, d=HD)[:, :, g]
                    nc.gpsimd.tensor_copy(wqb.rearrange("p k (i g d) -> p k i g d", g=KVH, d=HD)[:, :, :, g],
                                          src).then_inc(s_perm, 1)

            reorder()


def load_mod(eng, mod_d, modp, mods, part, n, s_mod):
    eng.dma_start(modp, mod_d[0:1, part * D:(part + n) * D].to_broadcast([P, n * D])).then_inc(s_mod, 16)
    eng.dma_start(mods, mod_d[1:1 + DB, None, part * D:(part + n) * D].to_broadcast([DB, DN, n * D])).then_inc(s_mod, 16)


def prompt_stage(env):
    nc, a, ps, R, C, sem, S = (env[k] for k in ("nc", "a", "ps", "R", "C", "sem", "S"))
    qT, kT = carve(R["Q"], (4, TOK), (4, TOK))
    qbT, kbT = carve(R["qbT"], (GROUP, TOK)), R["kbT"]
    v, kvb = carve(R["v"], (NT, HW)), carve(R["kvb"], (NT, 2 * KW))
    oaT, obT = carve(R["oaT"], (4, TOK)), carve(R["obT"], (GROUP, TOK))
    logf = carve(R["logf"], (NT, H))
    nfk = R["biasT"][0:H, 0:SEQ]
    prob, probT = carve(R["work"], (3, 512), (2, 512))
    U = 2 * H * PT
    units = [("fox", h, i) for h in range(H) for i in range(PT)] + \
            [("swa", h, i) for h in range(H) for i in range(PT)]
    mx, nm, rs, es, ri, sinks = carve(R["small"], (U,), (U,), (U,), (U,), (U,), (H,))
    s_sink, s_cum, s_nfk = sem("b_sinks"), sem("b_cumsum_psum"), sem("b_neg_cumsum")
    s_s, s_nm, s_e, s_es = sem("b_scores"), sem("b_neg_max"), sem("b_exp"), sem("b_exp_sink")
    s_p, s_t, s_pt = sem("b_prob"), sem("b_prob_transposed"), sem("b_probT")
    s_pv, s_o = sem("b_pv"), sem("b_o_out")

    def width(kind, i):
        return (i + 1) * P if kind == "fox" else P * min(i + 1, 2)

    swa_before = [sum(u[0] == "swa" for u in units[:n]) for n in range(U)]

    with nc.Block() as block:
        @block.sync
        def _(sp):
            sp.dma_start(sinks, a["swa_sinks"].to_broadcast([P, H])).then_inc(s_sink, 16)
            for b in range(2):
                for half in range(2):
                    half_cache(sp, env, b, b, half)

        @block.tensor
        def _(pe):
            for i in range(PT):
                for j in range(i + 1):
                    last = nc.tensor.matmul(ps[0:H, 7, i * P:(i + 1) * P], logf[:, j, :],
                                            C("tri_incl") if j == i else C("ones"), start=(j == 0), stop=(j == i))
            last.then_inc(s_cum, 1)

            def scores(n):
                kind, h, i = units[n]
                if n >= 3:
                    if kind == "swa" or units[n - 3][0] == "fox":
                        pe.wait_ge(s_e, n - 2)
                if n == 0:
                    pe.wait_ge(s_nfk, 1)
                w = width(kind, i)
                out = ps[:, n % 3, 0:w]
                if kind == "fox":
                    part = slice(HD * (h % 2), HD * (h % 2) + HD)
                    nc.tensor.matmul(out, C("ident", H)[:, h:h + 1].to_broadcast([H, P]), nfk[:, 0:w],
                                     start=True, stop=False)
                    ins = nc.tensor.matmul(out, qT[part, h // 2, i * P:(i + 1) * P], kT[part, h // 2, 0:w],
                                           start=False, stop=True)
                else:
                    g = h // GROUP
                    part = slice(HD * g, HD * g + HD)
                    ins = nc.tensor.matmul(out, qbT[part, h % GROUP, i * P:(i + 1) * P],
                                           kbT[part, (i + 1) * P - w:(i + 1) * P], start=True, stop=True)
                ins.then_inc(s_s, 1)

            def turn(n):
                kind, h, i = units[n]
                pe.wait_ge(s_p, n + 1)
                if n >= 2:
                    pe.wait_ge(s_pt, n - 1)
                for j in range(width(kind, i) // P):
                    last = nc.tensor.transpose(ps[:, 3 + n % 2, j * P:(j + 1) * P], prob[:, n % 3, j * P:(j + 1) * P],
                                               C("ident"))
                last.then_inc(s_t, 1)

            def values(n):
                kind, h, i = units[n]
                pe.wait_ge(s_pt, n + 1)
                if n >= 2:
                    pe.wait_ge(s_o, n - 1)
                r = h % 2 if kind == "fox" else h // GROUP
                out = ps[HD * r:HD * r + HD, 5 + n % 2, 0:P]
                nb = width(kind, i) // P
                for j in range(nb):
                    if kind == "fox":
                        lhsT = v[:, j, h * HD:(h + 1) * HD]
                    else:
                        lhsT = kvb[:, i + 1 - nb + j, KW + r * HD:KW + (r + 1) * HD]
                    ins = nc.tensor.matmul(out, lhsT, probT[:, n % 2, j * P:(j + 1) * P],
                                           start=(j == 0), stop=(j == nb - 1))
                ins.then_inc(s_pv, 1)

            for n in range(U + 3):
                if n < U:
                    scores(n)
                if 2 <= n < U + 2:
                    turn(n - 2)
                if n >= 3:
                    values(n - 3)

        @block.vector
        def _(dve):
            st = env["dve_steps"].resume(dve)
            dve.wait_ge(S["cached_logf"], 16)
            clogf = R["logf"][:, NT * H:].rearrange("p (b j h) -> p b j h", b=DB, h=H)
            wst = R["wst"].rearrange("p (j b h) -> p j b h", j=9, h=H)
            st.link(nc.vector.tensor_copy(wst[:, JC], logf[:, PT:PT + 1, :].to_broadcast([P, DB, H])))
            st.link(nc.vector.tensor_copy(wst[:, JC - 2], clogf[:, :, JC - 1, :]))
            for j in range(JC - 3, -1, -1):
                st.link(nc.vector.tensor_tensor(wst[:, j], wst[:, j + 1], clogf[:, :, j + 1, :], ALU.add))
            st.link(nc.vector.tensor_tensor(wst[:, JC - 1], wst[:, 0], clogf[:, :, 0, :], ALU.add))
            dve.wait_ge(s_cum, 1)
            nc.vector.tensor_scalar(nfk, ps[0:H, 7, :], -1.0, None, ALU.mult).then_inc(s_nfk, 1)
            dve.wait_ge(s_sink, 16)

            def maxima(n):
                kind, h, i = units[n]
                w = width(kind, i)
                dve.wait_ge(s_s, n + 1)
                if kind == "fox":
                    own = ps[:, n % 3, w - P:w]
                    st.link(nc.vector.tensor_tensor(own, own, C("causal"), ALU.add))
                    nc.vector.tensor_reduce(nm[:, n:n + 1], ps[:, n % 3, 0:w], AX, ALU.max, negate=True).then_inc(s_nm, 1)
                    return
                slope = 2.0 ** (-8.0 * (h + 1) / H)
                if n >= 3:
                    dve.wait_ge(s_t, n - 2)
                st.link(nc.vector.scalar_tensor_tensor(prob[:, n % 3, 0:w], C("swa_dist")[:, 2 * P - w:], -slope,
                                                       ps[:, n % 3, 0:w], ALU.mult, ALU.add))
                st.link(nc.vector.tensor_reduce(mx[:, n:n + 1], prob[:, n % 3, 0:w], AX, ALU.max))
                nc.vector.tensor_scalar(nm[:, n:n + 1], mx[:, n:n + 1], sinks[:, h:h + 1], -1.0,
                                        ALU.max, ALU.mult).then_inc(s_nm, 1)

            def normalise(n):
                kind, h, i = units[n]
                w = width(kind, i)
                dve.wait_ge(s_e, n + 1)
                if kind == "swa":
                    dve.wait_ge(s_es, swa_before[n] + 1)
                    st.link(nc.vector.tensor_tensor(rs[:, n:n + 1], rs[:, n:n + 1], es[:, n:n + 1], ALU.add))
                st.link(nc.vector.reciprocal(ri[:, n:n + 1], rs[:, n:n + 1]))
                nc.vector.tensor_scalar(prob[:, n % 3, 0:w], prob[:, n % 3, 0:w], ri[:, n:n + 1], None,
                                        ALU.mult).then_inc(s_p, 1)

            def out(n):
                kind, h, i = units[n]
                r = h % 2 if kind == "fox" else h // GROUP
                part = slice(HD * r, HD * r + HD)
                dst = oaT[part, h // 2, :] if kind == "fox" else obT[part, h % GROUP, :]
                dve.wait_ge(s_pv, n + 1)
                nc.vector.tensor_copy(dst[:, i * P:(i + 1) * P], ps[part, 5 + n % 2, 0:P]).then_inc(s_o, 1)

            for n in range(U + 3):
                if n < U:
                    maxima(n)
                if 1 <= n < U + 1:
                    normalise(n - 1)
                if n >= 3:
                    out(n - 3)

        @block.scalar
        def _(act):
            act.wait_ge(s_sink, 16)
            for n in range(U + 2):
                if n < U:
                    kind, h, i = units[n]
                    w = width(kind, i)
                    act.wait_ge(s_nm, n + 1)
                    if kind == "fox" and n >= 3:
                        act.wait_ge(s_t, n - 2)
                    src = ps[:, n % 3, 0:w] if kind == "fox" else prob[:, n % 3, 0:w]
                    nc.scalar.activation(prob[:, n % 3, 0:w], src, ACT.Exp, bias=nm[:, n:n + 1],
                                         accum_out=rs[:, n:n + 1]).then_inc(s_e, 1)
                    if kind == "swa":
                        nc.scalar.activation(es[:, n:n + 1], sinks[:, h:h + 1], ACT.Exp,
                                             bias=nm[:, n:n + 1]).then_inc(s_es, 1)
                if n >= 2:
                    kind, h, i = units[n - 2]
                    act.wait_ge(s_t, n - 1)
                    if n >= 4:
                        act.wait_ge(s_pv, n - 3)
                    w = width(kind, i)
                    nc.scalar.copy(probT[:, n % 2, 0:w], ps[:, 3 + n % 2, 0:w]).then_inc(s_pt, 1)


def sample_stage(env):
    nc, a, ps, R, C, sem, S, kv = (env[k] for k in ("nc", "a", "ps", "R", "C", "sem", "S", "kv"))
    qT, kT = carve(R["Q"], (4, TOK), (4, TOK))
    qbT, kbT = carve(R["qbT"], (GROUP, TOK)), R["kbT"]
    v, kvb = carve(R["v"], (NT, HW)), carve(R["kvb"], (NT, 2 * KW))
    oaT, obT = carve(R["oaT"], (4, TOK)), carve(R["obT"], (GROUP, TOK))
    logf = carve(R["logf"], (NT, H))
    wst = R["wst"].rearrange("p (j c) -> p j c", j=9)
    biasT = R["biasT"]
    NKEY = PAST + P
    kc, q_fox, q_swa, pick = carve(R["x"], (4, PAST), (4 * 160,), (P,), (P,))
    prob, probT, om, omb, sb_s, pbT, skT, skv0, skv1 = carve(
        R["work"], (NKEY,), (9, P), (HW,), (KW,), (2 * P,), (2, P), (P,), (2, KW), (2, KW))
    skv = [skv0, skv1]
    ring = [R["ring"][:, s * 4096:(s + 1) * 4096].rearrange("p (j n) -> p j n", j=JC) for s in range(4)]
    nmf, rsf, rif, mxb, nmb, rsb, esb, rib, sink = carve(R["small"], *[(1,)] * 9)
    s_sink, s_z, s_bias, s_biasT = sem("c_sink"), sem("c_zeros"), sem("c_bias_psum"), sem("c_bias_rows")
    s_skv = [sem("c_swa_cache_even"), sem("c_swa_cache_odd")]
    s_q = sem("c_queries")
    s_s, s_sb, s_nm, s_nmb = sem("c_scores"), sem("c_swa_scores"), sem("c_neg_max"), sem("c_swa_neg_max")
    s_e, s_eb = sem("c_exp"), sem("c_swa_exp")
    s_tr = [sem("c_turned_bank0"), sem("c_turned_bank1")]
    s_fr = [sem("c_copied_by_act"), sem("c_copied_by_dve")]
    s_pv, s_pvb, s_om, s_omb = sem("c_pv"), sem("c_swa_pv"), sem("c_o_masked"), sem("c_swa_o_masked")
    s_f, s_fb, s_oa, s_ob = sem("c_folded"), sem("c_swa_folded"), sem("c_o_out"), sem("c_swa_o_out")
    s_v = sem("c_dve_steps")

    class Turn:
        def __init__(self, i, u, r, last):
            j = 13 * u + r - (8 if last else 0)
            self.bank = j % 2
            self.before = i * 13 + 4 + j // 2

        def enter(self, pe):
            pe.wait_ge(s_fr[self.bank], self.before)

        def ready(self, eng):
            eng.wait_ge(s_tr[self.bank], self.before + 1)

        def copied(self, eng):
            eng.wait_ge(s_fr[self.bank], self.before + 1)

    def copy_out(bank, dst, src):
        ins = nc.scalar.copy(dst, src) if bank == 0 else nc.vector.tensor_copy(dst, src)
        ins.then_inc(s_fr[bank], 1)

    def key_cols(j):
        return kc[:, :, j * P:(j + 1) * P]

    def four(bank):
        return ps[:, bank, :].rearrange("p (c t) -> p c t", t=P)

    def copies(eng, bank, i, u, last, rs):
        for r in rs:
            t = Turn(i, u, r, last)
            if t.bank != bank:
                continue
            t.ready(eng)
            if r < 8:
                copy_out(bank, key_cols(r), four(bank))
            elif r == 8:
                copy_out(bank, skT, ps[:, bank, 0:P])
            elif r < 12:
                n = min(4, 9 - 4 * (r - 9))
                copy_out(bank, probT[:, 4 * (r - 9):4 * (r - 9) + n, :],
                         ps[:, bank, 0:n * P].rearrange("p (c t) -> p c t", t=P))
            else:
                copy_out(bank, pbT, ps[:, bank, 0:2 * P].rearrange("p (c t) -> p c t", t=P))

    def steps(eng, body):
        for u in range(2):
            body(0, u, first=True)
        with eng.Fori(1, DB // 2 - 1) as i:
            for u in range(2):
                body(i, u)
        for u in range(2):
            body(DB // 2 - 1, u, last=(u == 1))

    with nc.Block() as block:
        @block.sync
        def _(sp):
            with nc.allow_non_contiguous_dma(reason="a sink for each of 128 (head, query) rows"):
                sp.dma_start(sink, a["swa_sinks"].rearrange("l h -> (l h)")[:, None, None].to_broadcast([H, DN, 1])
                             ).then_inc(s_sink, 16)

            def small(i, u):
                for half, name in enumerate(("cache_swa_k", "cache_swa_v")):
                    rows = a[name][0].rearrange("b s h d -> b s (h d)")
                    b = 2 * i + u
                    src = rows[b] if isinstance(b, int) else rows[bass.ds(b, 1)].rearrange("a p n -> p (a n)")
                    sp.dma_start(skv[u][:, half, :], src).then_inc(s_skv[u], 16)

            for u in range(2):
                small(0, u)
            with sp.Fori(1, DB // 2) as i:
                for u in range(2):
                    b = 2 * i + u
                    sp.wait_ge(s_s, b - 1)
                    half_cache(sp, env, b, u, 0)
                    sp.wait_ge(s_pvb, b - 1)
                    small(i, u)
                    sp.wait_ge(s_pv, b - 1)
                    half_cache(sp, env, b, u, 1)

        @block.tensor
        def _(pe):
            for j in range(JC):
                out = ps[0:DB * H, 2 + j // 4, (j % 4) * P:(j % 4 + 1) * P]
                last = nc.tensor.matmul(out, wst[:, JC - 1, :], C("suffix"), start=True, stop=(j == JC - 1))
                if j < JC - 1:
                    last = nc.tensor.matmul(out, wst[:, j, :], C("ident"), start=False, stop=True)
            last = nc.tensor.matmul(ps[0:DB * H, 4, 0:P], wst[:, JC, :], C("same"), start=True, stop=True)
            last.then_inc(s_bias, 1)
            pe.wait_ge(kv[0], 16)
            for r in range(8):
                if r >= 2:
                    pe.wait_ge(s_fr[r % 2], r // 2)
                for c in range(4):
                    last = nc.tensor.transpose(ps[:, r % 2, c * P:(c + 1) * P], ring[0][:, r, c * P:(c + 1) * P],
                                               C("ident"))
                last.then_inc(s_tr[r % 2], 1)
            pe.wait_ge(s_biasT, 1)
            pe.wait_ge(s_z, 4)

            def body(i, u, first=False, last=False):
                b = 2 * i + u
                pe.wait_ge(s_q, b + 1)
                if first and u == 0:
                    for x in range(2):
                        pe.wait_ge(s_fr[x], 4)
                else:
                    for r in (6, 7):
                        prev = Turn(i if u else i - 1, 1 - u, r, False)
                        prev.copied(pe)
                if not (first and u == 0):
                    pe.wait_ge(s_e, b)
                for half in range(2):
                    out, cols = ps[:, 2 + half, :], slice(half * 512, half * 512 + 512)
                    nc.tensor.matmul(out, pick, biasT[:, cols], start=True, stop=False)
                    for c in range(4):
                        nc.tensor.matmul(out, q_fox[:, c * P:(c + 1) * P], kc[:, c, cols], start=False, stop=(c == 3))
                out = ps[:, 4, 0:P]
                nc.tensor.matmul(out, pick, biasT[:, PAST:NKEY], start=True, stop=False)
                for c in range(4):
                    ins = nc.tensor.matmul(out, q_fox[:, c * P:(c + 1) * P], kT[:, c, SEQ:TOK], start=False, stop=(c == 3))
                ins.then_inc(s_s, 1)
                if not last:
                    nu = 1 - u
                    pe.wait_ge(kv[nu], 16 * ((i + 1) if u == 0 else (i + 2)))
                    for r in range(8):
                        t = Turn(i, u, r, False)
                        t.enter(pe)
                        for c in range(4):
                            ins = nc.tensor.transpose(ps[:, t.bank, c * P:(c + 1) * P],
                                                      ring[nu][:, r, c * P:(c + 1) * P], C("ident"))
                        ins.then_inc(s_tr[t.bank], 1)
                t = Turn(i, u, 8, last)
                t.enter(pe)
                pe.wait_ge(s_skv[u], 32 * (i + 1))
                nc.tensor.transpose(ps[:, t.bank, 0:P], skv[u][:, 0, :], C("ident")).then_inc(s_tr[t.bank], 1)
                t.copied(pe)
                if not (first and u == 0):
                    pe.wait_ge(s_nmb, b)
                nc.tensor.matmul(ps[:, 7, 0:P], q_swa, skT, start=True, stop=True)
                nc.tensor.matmul(ps[:, 7, P:2 * P], pick, C("others"), start=True, stop=False)
                nc.tensor.matmul(ps[:, 7, P:2 * P], q_swa, kbT[:, SEQ:TOK], start=False, stop=True).then_inc(s_sb, 1)
                pe.wait_ge(s_e, b + 1)
                for r in range(9, 12):
                    t = Turn(i, u, r, last)
                    t.enter(pe)
                    for c in range(min(4, 9 - 4 * (r - 9))):
                        k = 4 * (r - 9) + c
                        ins = nc.tensor.transpose(ps[:, t.bank, c * P:(c + 1) * P], prob[:, k * P:(k + 1) * P], C("ident"))
                    ins.then_inc(s_tr[t.bank], 1)
                t = Turn(i, u, 12, last)
                t.enter(pe)
                pe.wait_ge(s_eb, b + 1)
                for c in range(2):
                    ins = nc.tensor.transpose(ps[:, t.bank, c * P:(c + 1) * P], sb_s[:, c * P:(c + 1) * P], C("ident"))
                ins.then_inc(s_tr[t.bank], 1)
                if not (first and u == 0):
                    pe.wait_ge(s_oa, b)
                    pe.wait_ge(s_ob, b)
                for r in (10, 11):
                    Turn(i, u, r, last).copied(pe)
                pe.wait_ge(kv[2 + u], 16 * (i + 1))
                for k in range(9):
                    rhs = ring[2 + u][:, k, :] if k < JC else v[:, PT, :]
                    ins = nc.tensor.matmul(ps[:, 5, :], probT[:, k, :], rhs, start=(k == 0), stop=(k == 8))
                ins.then_inc(s_pv, 1)
                t.copied(pe)
                nc.tensor.matmul(ps[:, 6, 0:KW], pbT[:, 0, :], skv[u][:, 1, :], start=True, stop=False)
                nc.tensor.matmul(ps[:, 6, 0:KW], pbT[:, 1, :], kvb[:, PT, KW:2 * KW], start=False, stop=True).then_inc(s_pvb, 1)
                pe.wait_ge(s_om, b + 1)
                for c in range(4):
                    ins = nc.tensor.matmul(ps[:, 5, c * DN:(c + 1) * DN], om[:, c * P:(c + 1) * P], C("fold16"),
                                           start=True, stop=True)
                ins.then_inc(s_f, 1)
                pe.wait_ge(s_omb, b + 1)
                nc.tensor.matmul(ps[:, 6, 0:GROUP * DN], omb, C("fold64"), start=True, stop=True).then_inc(s_fb, 1)

            steps(pe, body)

        def at_request(ap, b):
            return ap[:, :, b * DN:(b + 1) * DN] if isinstance(b, int) else ap[:, :, bass.ds(b * DN, DN)]

        @block.vector
        def _(dve):
            st = Steps(dve, s_v)
            nc.vector.memset(q_fox, 0.0).then_inc(s_z, 1)
            nc.vector.memset(q_swa, 0.0).then_inc(s_z, 1)
            nc.vector.memset(pick, 0.0).then_inc(s_z, 1)
            nc.vector.memset(biasT[DB * H:P, :], 0.0).then_inc(s_z, 1)
            dve.wait_ge(s_bias, 1)
            st.link(nc.vector.tensor_copy(biasT[0:DB * H, 0:PAST], ps[0:DB * H, 2:4, :].rearrange("p a b -> p (a b)")))
            nc.vector.tensor_tensor(biasT[0:DB * H, PAST:NKEY], ps[0:DB * H, 4, 0:P], C("others", DB * H),
                                    ALU.add).then_inc(s_biasT, 1)
            dve.wait_ge(s_z, 4)

            def queries(b):
                diag = q_fox.rearrange("p (c w) -> p c w", w=160)
                for r in range(2):
                    part = slice(HD * r, HD * r + HD)
                    nc.vector.tensor_copy(diag[part, :, r * DN:(r + 1) * DN], at_request(qT[part, :, SEQ:TOK], b))
                    nc.vector.tensor_copy(q_swa[part, r * GROUP * DN:(r + 1) * GROUP * DN].rearrange("p (i n) -> p i n", n=DN),
                                          at_request(qbT[part, :, SEQ:TOK], b))
                heads = C("ident", DB * H)
                heads = heads[:, b * H:(b + 1) * H] if isinstance(b, int) else heads[:, bass.ds(b * H, H)]
                nc.vector.tensor_copy(pick[0:DB * H, :].rearrange("p (h n) -> p h n", n=DN),
                                      heads.unsqueeze(2).to_broadcast([DB * H, H, DN])).then_inc(s_q, 1)

            queries(0)
            for r in range(1, 8, 2):
                dve.wait_ge(s_tr[1], r // 2 + 1)
                copy_out(1, key_cols(r), four(1))
            per = 9

            def body(i, u, first=False, last=False):
                b = 2 * i + u

                def per_request(ap):
                    return ap.rearrange("p (b n) -> p b n", n=DN)

                def all_requests(name):
                    return C(name).unsqueeze(1).to_broadcast([P, DB, DN])

                dve.wait_ge(s_s, b + 1)
                st.link(nc.vector.tensor_tensor(per_request(ps[:, 4, 0:P]), per_request(ps[:, 4, 0:P]),
                                                all_requests("fox_new"), ALU.add))
                nc.vector.tensor_reduce(nmf, ps[:, 2:5, :].rearrange("p a b -> p (a b)")[:, 0:NKEY], AX, ALU.max,
                                        negate=True).then_inc(s_nm, 1)
                if not last:
                    copies(dve, 1, i, u, last, range(8))
                copies(dve, 1, i, u, last, [8])
                dve.wait_ge(s_sb, b + 1)
                st.link(nc.vector.tensor_tensor(sb_s[:, 0:P], ps[:, 7, 0:P], C("swa_old"), ALU.add))
                st.link(nc.vector.tensor_tensor(per_request(sb_s[:, P:2 * P]), per_request(ps[:, 7, P:2 * P]),
                                                all_requests("swa_new"), ALU.add))
                st.link(nc.vector.tensor_reduce(mxb, sb_s, AX, ALU.max))
                nc.vector.tensor_scalar(nmb, mxb, sink, -1.0, ALU.max, ALU.mult).then_inc(s_nmb, 1)
                if not last:
                    queries(b + 1)
                dve.wait_ge(s_e, b + 1)
                st.link(nc.vector.reciprocal(rif, rsf))
                copies(dve, 1, i, u, last, range(9, 12))
                dve.wait_ge(s_eb, 2 * b + 2) if False else dve.wait_ge(s_eb, b + 1)
                st.link(nc.vector.tensor_tensor(rsb, rsb, esb, ALU.add))
                st.link(nc.vector.reciprocal(rib, rsb))
                copies(dve, 1, i, u, last, [12])
                dve.wait_ge(s_pv, b + 1)
                nc.vector.scalar_tensor_tensor(om, ps[:, 5, :], rif, C("headmask"), ALU.mult, ALU.mult).then_inc(s_om, 1)
                dve.wait_ge(s_pvb, b + 1)
                nc.vector.scalar_tensor_tensor(omb, ps[:, 6, 0:KW], rib, C("groupmask"), ALU.mult, ALU.mult).then_inc(s_omb, 1)
                dve.wait_ge(s_fb, b + 1)
                nc.vector.tensor_copy(at_request(obT[:, :, SEQ:TOK], b),
                                      ps[:, 6, 0:GROUP * DN].rearrange("p (i n) -> p i n", n=DN)).then_inc(s_ob, 1)

            base = st.n
            count = []

            def counted(i, u, first=False, last=False):
                if u == 0 or not isinstance(i, int):
                    pass
                st.loop((2 * i + u) * 7 + base)
                body(i, u, first, last)
                assert st.n == 7, st.n

            dve.wait_ge(s_sink, 16)
            steps(dve, counted)

        @block.scalar
        def _(act):
            for r in range(0, 8, 2):
                act.wait_ge(s_tr[0], r // 2 + 1)
                copy_out(0, key_cols(r), four(0))
            act.wait_ge(s_sink, 16)

            def body(i, u, first=False, last=False):
                b = 2 * i + u
                if not last:
                    act.wait_ge(s_s, b + 1)
                    copies(act, 0, i, u, last, range(4))
                act.wait_ge(s_nm, b + 1)
                nc.scalar.activation(prob, ps[:, 2:5, :].rearrange("p a b -> p (a b)")[:, 0:NKEY], ACT.Exp,
                                     bias=nmf, accum_out=rsf).then_inc(s_e, 1)
                if not last:
                    copies(act, 0, i, u, last, range(4, 8))
                copies(act, 0, i, u, last, [8])
                act.wait_ge(s_nmb, b + 1)
                nc.scalar.activation(esb, sink, ACT.Exp, bias=nmb)
                nc.scalar.activation(sb_s, sb_s, ACT.Exp, bias=nmb, accum_out=rsb).then_inc(s_eb, 1)
                copies(act, 0, i, u, last, range(9, 13))
                act.wait_ge(s_f, b + 1)
                nc.scalar.copy(at_request(oaT[:, :, SEQ:TOK], b),
                               ps[:, 5, 0:4 * DN].rearrange("p (i n) -> p i n", n=DN)).then_inc(s_oa, 1)

            steps(act, body)


def half_cache(eng, env, b, u, half):
    a, R, kv = env["a"], env["R"], env["kv"]
    rows = a[("cache_fox_k", "cache_fox_v")[half]][0].rearrange("b (p j) h d -> b p (j h d)", j=JC)
    slot = 2 * half + u
    src = rows[b] if isinstance(b, int) else rows[bass.ds(b, 1)].rearrange("a p n -> p (a n)")
    eng.dma_start(R["ring"][:, slot * 4096:(slot + 1) * 4096], src).then_inc(kv[slot], 16)


def mix_stage(env):
    nc, a, ps, R, C, sem = (env[k] for k in ("nc", "a", "ps", "R", "C", "sem"))
    mod_d, h2_d, acc_d, tab_d = env["mod_d"], env["h2_d"], env["acc_d"], env["tab_d"]
    hT = carve(R["hT"], (KC, TOK))
    h2row = carve(R["hT"], (NT, D))
    oaT, obT = carve(R["oaT"], (4, TOK)), carve(R["obT"], (GROUP, TOK))
    mixT = carve(R["Q"], (KC, TOK))
    x = carve(R["x"], (NT, D))
    ring = R["ring"]
    sub = [carve(ring[:, s * D:(s + 1) * D], (KC, P)) for s in range(8)]
    wa, wb = carve(ring[:, 8192:12288], (4, D)), carve(ring[:, 12288:16384], (GROUP, D))
    wo = [carve(ring[:, s * 4096:(s + 1) * 4096], (KC, 512)) for s in range(2)]
    h2T = carve(ring[:, 8192:], (KC, TOK))
    wsg = carve(ring[:, 0:4096], (2, KC, FE))
    wsd = carve(ring[:, 4096:6144], (2, D))
    sgate, prod = carve(R["work"], (2 * 2, TOK), (2, TOK))
    gate1 = carve(R["v"], (2, D))
    shift2 = [R["work"][:, 0:D], R["work"][:, 2 * D:3 * D]]
    scale2 = [R["work"][:, D:2 * D], R["work"][:, 3 * D:4 * D]]
    wr, br = carve(R["biasT"], (KC, NE), (NE,))
    tmpx = carve(R["obT"], (2, 512))
    tmpr = carve(R["oaT"], (2, D))
    stat, sums = carve(R["small"], (NT,), (2 * NT,))
    squares = R["qbT"][:, 2 * D:2 * D + 512]
    hs, hTs, sgs = (carve(R["wst"], (2, FE)), carve(R["kbT"], (2, FE)), carve(R["kvb"][:, 768:], (2, FE)))
    ysb = carve(R["v"], (2, D))
    sc, sel, gt, chosen, dest, selm, left = carve(R["oaT"], *[(NT, NE)] * 7)
    nblk, pend, pst = carve(R["kvb"], (NE,), (NE,), (NE,))
    (top2, gs, gtr, eqr, rank, top8, idxf, destk, gk) = carve(
        R["obT"][:, D:], (NG, 8), (NT, NG), (NG, NG), (NG, NG), (NT, NG), (NT, 8), (NT, TOPK), (NT, TOPK), (NT, TOPK))
    junk, den, blk, one = carve(R["obT"][:, D + 512:], (NE,), (NT,), (1,), (1,))
    idx8 = R["obT"][:, D + 600:D + 640].bitcast(U32).rearrange("p (t k) -> p t k", k=TOPK)
    slot_no = R["obT"][:, D + 640:D + 680].bitcast(U32).rearrange("p (t k) -> p t k", k=TOPK)
    entry = R["obT"][:, D + 680:D + 760].rearrange("p (t k w) -> p t k w", k=TOPK, w=2)
    entry_u = R["obT"][:, D + 680:D + 760].bitcast(U32).rearrange("p (t k w) -> p t k w", k=TOPK, w=2)
    zero_rows = R["kvb"][:, 256:768]
    counts = env["counts"]

    s_wb = sem("d_w_branches")
    s_sub = [sem(f"d_w_gate{c}") for c in range(4)]
    s_wo = [sem("d_w_out0"), sem("d_w_out1")]
    s_x, s_wr, s_mod, s_wsg, s_wsd = sem("d_x_and_gate1"), sem("d_router_and_gate2"), sem("d_mod2"), sem("d_w_sh_gu"), sem("d_w_sh_down")
    s_mm, s_sig, s_mul, s_mix = sem("d_branch_psum"), sem("d_sigmoid"), sem("d_gated"), sem("d_mixed")
    s_out, s_x1, s_sq, s_var, s_rt = sem("d_out_psum"), sem("d_x1"), sem("d_sumsq"), sem("d_variance"), sem("d_root")
    s_h2, s_h2d = sem("d_h2_rows"), sem("d_h2_stored")
    s_t, s_ta, s_tv = sem("d_turned"), sem("d_h2T_by_act"), sem("d_h2T_by_dve")
    s_lg, s_sc, s_m, s_pos = sem("d_logits"), sem("d_scores"), sem("d_chosen"), sem("d_positions")
    s_gu, s_sg, s_hs, s_ht, s_hc = sem("d_sh_gu"), sem("d_sh_sigmoid"), sem("d_sh_hidden"), sem("d_sh_turned"), sem("d_sh_hT")
    s_y, s_ye, s_yd = sem("d_sh_y"), sem("d_sh_y_rows"), [sem("d_sh_stored0"), sem("d_sh_stored1")]
    s_blk, s_bt = sem("d_block_column"), sem("d_block_row")
    s_sp, s_tab, s_ent, s_scat = sem("d_spare_zeros"), sem("d_table_init"), sem("d_entries"), sem("d_scattered")
    s_tl = sem("d_table_loaded")
    w_in = a["w_in"][0].rearrange("(k p) n -> p k n", p=P)

    with nc.Block() as block:
        @block.sync
        def _(sp):
            def gates(c):
                for h, o0 in enumerate((O_GA, O_GB)):
                    sp.dma_start(sub[2 * (c % 4) + h], w_in[:, :, o0 + c * P:o0 + (c + 1) * P]).then_inc(s_sub[c % 4], 16)

            gates(0)
            sp.dma_start(wa, a["w_branch_a"][0].rearrange("(k p) n -> p k n", p=P)).then_inc(s_wb, 16)
            for g in range(KVH):
                sp.dma_start(wb[g * HD:(g + 1) * HD], a["w_branch_b"][0].rearrange("(g i d) n -> g d i n", g=KVH, d=HD)[g]
                             ).then_inc(s_wb, 16)
            for c in range(1, 4):
                gates(c)
            for c in range(4, KC):
                sp.wait_ge(s_mm, 4 * (c - 4) + 2)
                gates(c)
            w_out = a["w_out"][0].rearrange("(k p) n -> p k n", p=P)
            sp.wait_ge(s_mm, 4 * 5 + 2)
            sp.dma_start(wo[0], w_out[:, :, 0:512]).then_inc(s_wo[0], 16)
            sp.wait_ge(s_mm, 4 * 7 + 2)
            sp.dma_start(wo[1], w_out[:, :, 512:D]).then_inc(s_wo[1], 16)
            sp.wait_ge(s_mix, KC)
            load_mod(sp, mod_d, R["work"][:, 0:2 * D], R["work"][:, 2 * D:4 * D], 3, 2, s_mod)
            sp.dma_start(tab_d, a["empty_table"]).then_inc(s_tab, 16)
            sp.wait_ge(s_out, NT)
            for h, name in enumerate(("w_sh_gate", "w_sh_up")):
                sp.dma_start(wsg[:, h], a[name][0].rearrange("(p k) f -> p k f", k=KC)).then_inc(s_wsg, 16)
            sp.wait_ge(s_out, 2 * NT)
            sp.dma_start(wsd, a["w_sh_down"][0].rearrange("(p j) n -> p j n", j=2)).then_inc(s_wsd, 16)
            for t in range(NT):
                sp.wait_ge(s_h2, t + 1)
                sp.dma_start(h2_d[t * P:(t + 1) * P, :], h2row[:, t, :]).then_inc(s_h2d, 16)
            sp.wait_ge(s_sp, 1)
            for half in range(2):
                sp.dma_start(acc_d[TOK:TOK + P, half * 512:(half + 1) * 512], zero_rows).then_inc(s_h2d, 16)
            for t in range(NT):
                sp.wait_ge(s_ye, 2 * t + 2)
                sp.dma_start(acc_d[t * P:(t + 1) * P, :], ysb[:, t % 2, :]).then_inc(s_yd[t % 2], 16)
            sp.wait_ge(s_yd[0], 48)
            sp.wait_ge(s_yd[1], 32)
            sp.wait_ge(s_h2d, 16 * (NT + 2))

        @block.tensor
        def _(pe):
            for c in range(KC):
                pe.wait_ge(s_sub[c % 4], 32 * (c // 4 + 1))
                if c == 0:
                    pe.wait_ge(s_wb, 48)
                if c >= 2:
                    pe.wait_ge(s_mul, 4 * (c - 1))
                if c >= 1:
                    pe.wait_ge(s_sig, 3 * (c - 1) + 2)
                extra = ps[:, (5 * c + 4) % 8, :]
                for r in range(4):
                    n = KC if r < 2 else 4
                    for part in range(2):
                        out = ps[:, (5 * c + r) % 8, :] if part == 0 else extra[:, r * P:(r + 1) * P]
                        cols = slice(0, SEQ) if part == 0 else slice(SEQ, TOK)
                        for k in range(n):
                            if r < 2:
                                lhsT, rhs = sub[2 * (c % 4) + r][:, k, :], hT[:, k, cols]
                            elif r == 2:
                                lhsT, rhs = wa[:, k, c * P:(c + 1) * P], oaT[:, k, cols]
                            else:
                                lhsT, rhs = wb[:, k, c * P:(c + 1) * P], obT[:, k, cols]
                            last = nc.tensor.matmul(out, lhsT, rhs, start=(k == 0), stop=(k == n - 1))
                    last.then_inc(s_mm, 1)
            pe.wait_ge(s_mix, KC)

            def turn(t):
                pe.wait_ge(s_h2, t + 1)
                for g in range(2):
                    n = 2 * t + g
                    if n >= 2:
                        pe.wait_ge(s_ta if g == 0 else s_tv, t)
                    for k in range(4):
                        last = nc.tensor.transpose(ps[:, 4 + g, k * P:(k + 1) * P],
                                                   h2row[:, t, (4 * g + k) * P:(4 * g + k + 1) * P], C("ident"))
                    last.then_inc(s_t, 1)

            for n in range(2 * NT):
                half, t = n // NT, n % NT
                if t == 0:
                    pe.wait_ge(s_wo[half], 16)
                if n >= 4:
                    pe.wait_ge(s_x1, n - 3)
                for k in range(KC):
                    last = nc.tensor.matmul(ps[:, n % 4, :], mixT[:, k, t * P:(t + 1) * P], wo[half][:, k, :],
                                            start=(k == 0), stop=(k == KC - 1))
                last.then_inc(s_out, 1)
                if half == 1 and t >= 1:
                    turn(t - 1)
            turn(NT - 1)
            pe.wait_ge(s_wr, 64)
            pe.wait_ge(s_ta, NT)
            pe.wait_ge(s_tv, NT)
            for t in range(NT):
                for k in range(KC):
                    last = nc.tensor.matmul(ps[:, 6, t * NE:(t + 1) * NE], h2T[:, k, t * P:(t + 1) * P], wr[:, k, :],
                                            start=(k == 0), stop=(k == KC - 1))
            last.then_inc(s_lg, 1)
            pe.wait_ge(s_x1, 2 * NT)
            pe.wait_ge(s_wsg, 32)
            for t in range(NT):
                for k in range(KC):
                    last = nc.tensor.matmul(ps[:, t, :], h2T[:, k, t * P:(t + 1) * P], wsg[:, :, k, :],
                                            start=(k == 0), stop=(k == KC - 1))
                last.then_inc(s_gu, 1)
            pe.wait_ge(s_m, 1)
            for t in range(NT):
                for j in range(t + 1):
                    nc.tensor.matmul(ps[:, 7, t * NE:(t + 1) * NE], C("tri_strict") if j == t else C("ones"),
                                     chosen[:, j, :], start=(j == 0), stop=(j == t))
            for j in range(NT):
                last = nc.tensor.matmul(ps[:, 7, NT * NE:(NT + 1) * NE], C("ones"), chosen[:, j, :],
                                        start=(j == 0), stop=(j == NT - 1))
            last.then_inc(s_pos, 1)
            for t in range(NT):
                pe.wait_ge(s_hs, t + 1)
                if t == 0:
                    pe.wait_ge(s_sc, 1)
                if t >= 2:
                    pe.wait_ge(s_hc, t - 1)
                for j in range(2):
                    last = nc.tensor.transpose(ps[:, 5 + t % 2, j * P:(j + 1) * P], hs[:, t % 2, j * P:(j + 1) * P],
                                               C("ident"))
                last.then_inc(s_ht, 1)
                pe.wait_ge(s_hc, t + 1)
                pe.wait_ge(s_wsd, 16)
                for half in range(2):
                    n = 2 * t + half
                    if n < 4:
                        pe.wait_ge(s_hs, n + 1)
                    else:
                        pe.wait_ge(s_ye, n - 3)
                    for j in range(2):
                        last = nc.tensor.matmul(ps[:, n % 4, :], hTs[:, t % 2, j * P:(j + 1) * P],
                                                wsd[:, j, half * 512:(half + 1) * 512], start=(j == 0), stop=(j == 1))
                    last.then_inc(s_y, 1)
            pe.wait_ge(s_blk, 1)
            nc.tensor.matmul(ps[0:1, 4, 0:P], blk, C("ident"), start=True, stop=True).then_inc(s_bt, 1)

        @block.scalar
        def _(act):
            act.dma_start(gate1[:, 0, :], mod_d[0:1, 2 * D:3 * D].to_broadcast([P, D])).then_inc(s_x, 16)
            act.dma_start(gate1[:, 1, :], mod_d[1:1 + DB, None, 2 * D:3 * D].to_broadcast([DB, DN, D])).then_inc(s_x, 16)
            act.dma_start(x[:, 0:PT, :], a["x_prompt"][0].rearrange("(t p) d -> p t d", p=P)).then_inc(s_x, 16)
            act.dma_start(x[:, PT, :], a["x_sample"].rearrange("b n d -> (b n) d")).then_inc(s_x, 16)
            act.dma_start(wr, a["w_router"][0].rearrange("(p k) n -> p k n", k=KC)).then_inc(s_wr, 16)
            act.dma_start(br, a["router_bias"].to_broadcast([P, NE])).then_inc(s_wr, 16)
            gate2 = carve(R["qbT"], (2, D))
            act.dma_start(gate2[:, 0, :], mod_d[0:1, 5 * D:6 * D].to_broadcast([P, D])).then_inc(s_wr, 16)
            act.dma_start(gate2[:, 1, :], mod_d[1:1 + DB, None, 5 * D:6 * D].to_broadcast([DB, DN, D])).then_inc(s_wr, 16)
            for c in range(KC):
                u = c % 2
                if c >= 2:
                    act.wait_ge(s_mul, 4 * (c - 1))
                for r in range(2):
                    act.wait_ge(s_mm, 4 * c + r + 1)
                    nc.scalar.activation(sgate[:, 2 * u + r, 0:SEQ], ps[:, (5 * c + r) % 8, :], ACT.Sigmoid).then_inc(s_sig, 1)
                act.wait_ge(s_mm, 4 * c + 4)
                nc.scalar.activation(sgate[:, 2 * u:2 * u + 2, SEQ:TOK],
                                     ps[:, (5 * c + 4) % 8, 0:2 * P].rearrange("p (r t) -> p r t", t=P),
                                     ACT.Sigmoid).then_inc(s_sig, 1)

            def turned(t):
                act.wait_ge(s_t, 2 * t + 1)
                nc.scalar.copy(h2T[:, 0:4, t * P:(t + 1) * P], ps[:, 4, :].rearrange("p (k t) -> p k t", t=P)).then_inc(s_ta, 1)

            for t in range(NT):
                act.wait_ge(s_x1, NT + t + 1)
                for half in range(2):
                    if 2 * t + half:
                        act.wait_ge(s_sq, 2 * t + half)
                    nc.scalar.activation(squares, x[:, t, half * 512:(half + 1) * 512], ACT.Square,
                                         accum_out=sums[:, 2 * t + half:2 * t + half + 1]).then_inc(s_sq, 1)
                act.wait_ge(s_var, t + 1)
                nc.scalar.activation(stat[:, t:t + 1], stat[:, t:t + 1], ACT.Sqrt).then_inc(s_rt, 1)
                if t >= 1:
                    turned(t - 1)
            turned(NT - 1)
            act.wait_ge(s_lg, 1)
            nc.scalar.activation(sc, ps[:, 6, 0:NT * NE].rearrange("p (t e) -> p t e", e=NE), ACT.Sigmoid).then_inc(s_sc, 1)

            def sigmoid(t):
                act.wait_ge(s_gu, t + 1)
                if t >= 2:
                    act.wait_ge(s_hs, t - 1)
                nc.scalar.activation(sgs[:, t % 2, :], ps[:, t, 0:FE], ACT.Sigmoid).then_inc(s_sg, 1)

            def hidden(t):
                act.wait_ge(s_ht, t + 1)
                nc.scalar.copy(hTs[:, t % 2, :], ps[:, 5 + t % 2, 0:FE]).then_inc(s_hc, 1)

            def rows(t):
                for half in range(2):
                    n = 2 * t + half
                    act.wait_ge(s_y, n + 1)
                    if t >= 2 and half == 0:
                        act.wait_ge(s_yd[t % 2], 16 * (t // 2))
                    nc.scalar.copy(ysb[:, t % 2, half * 512:(half + 1) * 512], ps[:, n % 4, :]).then_inc(s_ye, 1)

            for t in range(2):
                sigmoid(t)
            for t in range(NT):
                if t + 2 < NT:
                    sigmoid(t + 2)
                hidden(t)
                rows(t)
            act.wait_ge(s_bt, 1)
            nc.scalar.copy(counts[0:1, 1:1 + P], ps[0:1, 4, 0:P])

        @block.vector
        def _(dve):
            st = env["dve_steps"].resume(dve)
            nc.vector.memset(zero_rows, 0.0).then_inc(s_sp, 1)
            for c in range(KC):
                u = c % 2
                extra = ps[:, (5 * c + 4) % 8, :]
                if c >= 2:
                    dve.wait_ge(s_mix, c - 1)
                for r in range(2):
                    out = mixT[:, c, :] if r == 0 else prod[:, u, :]
                    dve.wait_ge(s_sig, 3 * c + r + 1)
                    dve.wait_ge(s_mm, 4 * c + r + 3)
                    nc.vector.tensor_tensor(out[:, 0:SEQ], sgate[:, 2 * u + r, 0:SEQ], ps[:, (5 * c + 2 + r) % 8, :],
                                            ALU.mult).then_inc(s_mul, 1)
                dve.wait_ge(s_sig, 3 * c + 3)
                for r in range(2):
                    out = mixT[:, c, :] if r == 0 else prod[:, u, :]
                    nc.vector.tensor_tensor(out[:, SEQ:TOK], sgate[:, 2 * u + r, SEQ:TOK],
                                            extra[:, (2 + r) * P:(3 + r) * P], ALU.mult).then_inc(s_mul, 1)
            dve.wait_ge(s_x, 64)

            def turned(t):
                dve.wait_ge(s_t, 2 * t + 2)
                nc.vector.tensor_copy(h2T[:, 4:8, t * P:(t + 1) * P], ps[:, 5, :].rearrange("p (k t) -> p k t", t=P)).then_inc(s_tv, 1)

            for n in range(2 * NT):
                half, t = n // NT, n % NT
                cols = slice(half * 512, half * 512 + 512)
                dve.wait_ge(s_out, n + 1)
                w = int(t == PT)
                st.link(nc.vector.tensor_tensor(tmpx[:, n % 2, :], ps[:, n % 4, :], gate1[:, w, cols], ALU.mult))
                nc.vector.tensor_tensor(x[:, t, cols], x[:, t, cols], tmpx[:, n % 2, :], ALU.add).then_inc(s_x1, 1)
                if half == 0:
                    continue
                if t == 0:
                    dve.wait_ge(s_mod, 32)
                dve.wait_ge(s_sq, 2 * t + 2)
                st.link(nc.vector.tensor_tensor(stat[:, t:t + 1], sums[:, 2 * t:2 * t + 1],
                                                sums[:, 2 * t + 1:2 * t + 2], ALU.add))
                nc.vector.tensor_scalar(stat[:, t:t + 1], stat[:, t:t + 1], 1.0 / D, EPS, ALU.mult, ALU.add).then_inc(s_var, 1)
                dve.wait_ge(s_rt, t + 1)
                st.link(nc.vector.reciprocal(stat[:, t:t + 1], stat[:, t:t + 1]))
                st.link(nc.vector.scalar_tensor_tensor(tmpr[:, t % 2, :], x[:, t, :], stat[:, t:t + 1], scale2[w],
                                                       ALU.mult, ALU.mult))
                nc.vector.tensor_tensor(h2row[:, t, :].rearrange("q (k p) -> q p k", k=KC),
                                        tmpr[:, t % 2, :].rearrange("q (p k) -> q p k", k=KC),
                                        shift2[w].rearrange("q (p k) -> q p k", k=KC), ALU.add).then_inc(s_h2, 1)
                if t >= 1:
                    turned(t - 1)
            turned(NT - 1)

            dve.wait_ge(s_sc, 1)
            dve.wait_ge(s_wr, 64)
            link = st.link
            link(nc.vector.tensor_tensor(sel, sc, br.unsqueeze(1).to_broadcast([P, NT, NE]), ALU.add))
            for t in range(NT):
                for g in range(NG):
                    last = nc.vector.max(top2[:, g, :], sel[:, t, g * 8:(g + 1) * 8])
                    if g == NG - 1:
                        link(last)
                link(nc.vector.tensor_tensor(gs[:, t, :], top2[:, :, 0], top2[:, :, 1], ALU.add))
                mine = gs[:, t, :].unsqueeze(2).to_broadcast([P, NG, NG])
                other = gs[:, t, :].unsqueeze(1).to_broadcast([P, NG, NG])
                link(nc.vector.tensor_tensor(gtr, other, mine, ALU.is_gt))
                link(nc.vector.tensor_tensor(eqr, other, mine, ALU.is_equal))
                link(nc.vector.tensor_tensor(eqr, eqr, C("ties").rearrange("p (g j) -> p g j", j=NG), ALU.mult))
                link(nc.vector.tensor_tensor(gtr, gtr, eqr, ALU.add))
                link(nc.vector.tensor_reduce(rank[:, t, :], gtr, AX, ALU.add))
            link(nc.vector.tensor_scalar(gs, rank, float(TOPG), None, ALU.is_lt))
            link(nc.vector.tensor_scalar(rank, gs, -NEG, NEG, ALU.mult, ALU.add))
            for t in range(NT):
                grp = selm[:, t, :].rearrange("p (g j) -> p g j", j=8)
                link(nc.vector.tensor_tensor(grp, sel[:, t, :].rearrange("p (g j) -> p g j", j=8),
                                             gs[:, t, :].unsqueeze(2).to_broadcast([P, NG, 8]), ALU.mult))
                link(nc.vector.tensor_tensor(grp, grp, rank[:, t, :].unsqueeze(2).to_broadcast([P, NG, 8]), ALU.add))
                link(nc.vector.max(top8[:, t, :], selm[:, t, :]))
                link(nc.vector.match_replace(left[:, t, :], top8[:, t, :], selm[:, t, :], -3e38))
                link(nc.vector.max_index(idx8[:, t, :], top8[:, t, :], selm[:, t, :]))
            nc.vector.tensor_scalar(chosen, left, -2e38, None, ALU.is_lt).then_inc(s_m, 1)
            dve.wait_ge(s_m, 1)

            def hidden(t):
                dve.wait_ge(s_sg, t + 1)
                if t >= 2:
                    dve.wait_ge(s_ht, t - 1)
                link(nc.vector.tensor_tensor(sgs[:, t % 2, :], sgs[:, t % 2, :], ps[:, t, 0:FE], ALU.mult))
                nc.vector.tensor_tensor(hs[:, t % 2, :].rearrange("q (j p) -> q p j", j=2),
                                        sgs[:, t % 2, :].rearrange("q (p j) -> q p j", j=2),
                                        ps[:, t, FE:2 * FE].rearrange("q (p j) -> q p j", j=2), ALU.mult).then_inc(s_hs, 1)

            for t in range(2):
                hidden(t)
            for t in range(NT):
                link(nc.vector.tensor_tensor_reduce(gt[:, t, :], sc[:, t, :], chosen[:, t, :], 1.0, 0.0, ALU.mult,
                                                    ALU.add, den[:, t:t + 1]))
            link(nc.vector.reciprocal(den, den))
            for t in range(NT):
                link(nc.vector.tensor_scalar(gt[:, t, :], gt[:, t, :], den[:, t:t + 1], ROUTED_SCALE, ALU.mult, ALU.mult))
            link(nc.vector.tensor_copy(idxf, idx8))
            hidden(2)
            dve.wait_ge(s_pos, 1)
            pos = ps[:, 7, 0:NT * NE].rearrange("p (t e) -> p t e", e=NE)
            cnt = ps[:, 7, NT * NE:(NT + 1) * NE]
            link(nc.vector.tensor_scalar(nblk, cnt, 0.0, None, ALU.is_gt))
            for j in range(1, NT):
                link(nc.vector.scalar_tensor_tensor(nblk, cnt, float(j * P), nblk, ALU.is_gt, ALU.add))
            link(nc.vector.memset(junk, 0.0))
            link(nc.vector.tensor_tensor_scan(pend, nblk, junk, 0.0, ALU.add, ALU.add))
            link(nc.vector.tensor_tensor(pst, pend, nblk, ALU.subtract))
            link(nc.vector.tensor_scalar(junk, pend, C("pcol"), 0.0, ALU.is_le, ALU.add, accum_out=blk))
            nc.vector.tensor_scalar(blk, blk, float(NE - 1), None, ALU.min).then_inc(s_blk, 1)
            dve.wait_ge(s_blk, 1)
            link(nc.vector.tensor_scalar(left[0:1, 0, 0:PAIRS], C("pairs2", 1), pend[0:1, NE - 1:NE], 0.0, ALU.is_lt,
                                         ALU.add, accum_out=one[0:1, :]))
            nc.vector.tensor_copy(counts[0:1, 0:1], one[0:1, :])
            link(nc.vector.tensor_scalar(left, pos, float(P), None, ALU.is_ge))
            for j in range(2, NT):
                for t in range(NT):
                    link(nc.vector.scalar_tensor_tensor(left[:, t, :], pos[:, t, :], float(j * P), left[:, t, :],
                                                        ALU.is_ge, ALU.add))
            for t in range(NT):
                link(nc.vector.tensor_scalar(dest[:, t, :], pos[:, t, :], float(SLOTS), None, ALU.mult))
                link(nc.vector.scalar_tensor_tensor(dest[:, t, :], left[:, t, :], float(1 - P * SLOTS), dest[:, t, :],
                                                    ALU.mult, ALU.add))
                link(nc.vector.tensor_tensor(dest[:, t, :], dest[:, t, :], pst, ALU.add))
                for k in range(TOPK):
                    link(nc.vector.scalar_tensor_tensor(junk, C("iota64"), idxf[:, t, k:k + 1], dest[:, t, :],
                                                        ALU.is_equal, ALU.mult, accum_out=destk[:, t, k:k + 1]))
                    link(nc.vector.scalar_tensor_tensor(junk, C("iota64"), idxf[:, t, k:k + 1], gt[:, t, :],
                                                        ALU.is_equal, ALU.mult, accum_out=entry[:, t, k, 1:2]))
                link(nc.vector.tensor_copy(slot_no[:, t, :], destk[:, t, :]))
                link(nc.vector.tensor_scalar(gk[:, t, :], C("pcol").to_broadcast([P, TOPK]), float(t * P), None, ALU.add))
                nc.vector.tensor_copy(entry_u[:, t, :, 0], gk[:, t, :]).then_inc(s_ent, 1)
                if t < 2:
                    hidden(t + 3)

        @block.gpsimd
        def _(pool):
            for c in range(KC):
                pool.wait_ge(s_mul, 4 * c + 4)
                nc.gpsimd.tensor_tensor(mixT[:, c, :], mixT[:, c, :], prod[:, c % 2, :], ALU.add).then_inc(s_mix, 1)
            pool.wait_ge(s_tab, 16)
            for t in range(NT):
                pool.wait_ge(s_ent, t + 1)
                for k in range(TOPK):
                    pool.indirect_dma_start(tab_d, bass.IndirectOffsetOnAxis(ap=slot_no[:, t, k:k + 1], axis=0),
                                            entry_u[:, t, k, :], None).then_inc(s_scat, 16)
            pool.wait_ge(s_scat, 16 * NT * TOPK)
            pool.dma_start(env["table"], tab_d.rearrange("(p b) w -> p (b w)", p=P)).then_inc(s_tl, 16)
            pool.wait_ge(s_tl, 16)


def expert_stage(env):
    nc, a, ps, R, C, sem = (env[k] for k in ("nc", "a", "ps", "R", "C", "sem"))
    h2_d, acc_d, counts = env["h2_d"], env["acc_d"], env["counts"]
    table = env["table"].rearrange("p (b w) -> p b w", w=2)
    ring = R["ring"]
    wgu = [carve(ring[:, u * 4096:(u + 1) * 4096], (2, KC, FE)) for u in range(2)]
    wd = [carve(ring[:, 8192 + u * 2048:8192 + (u + 1) * 2048], (2, D)) for u in range(2)]
    yb = carve(ring[:, 12288:14336], (2, D))
    xg = carve(ring[:, 14336:16384], (2, D))
    xT = carve(R["Q"], (2, D))
    hs, hT, sg = carve(R["Q"][:, 2 * D:], (2, FE), (2, FE), (2, FE))
    gidx = R["small"][:, 0:2].bitcast(U32)
    sidx = R["small"][:, 2:4].bitcast(U32)
    s_w = [sem("e_w_gu_even"), sem("e_w_gu_odd")]
    s_wd = [sem("e_w_down_even"), sem("e_w_down_odd")]
    s_z, s_gi, s_si = sem("e_zeros"), sem("e_gather_index"), sem("e_scatter_index")
    s_g = [sem("e_gathered_even"), sem("e_gathered_odd")]
    s_t, s_xa, s_xv = sem("e_turned"), sem("e_xT_by_act"), sem("e_xT_by_dve")
    s_gu, s_sg, s_v, s_hs = sem("e_gu"), sem("e_sigmoid"), sem("e_dve_steps"), sem("e_hidden")
    s_ht, s_hc, s_y, s_ya, s_yv, s_sc = (sem("e_hidden_turned"), sem("e_hT"), sem("e_y"), sem("e_y_by_act"),
                                         sem("e_y_by_dve"), sem("e_scattered"))
    gate_w = [a["w_exp_gate"][0].rearrange("e (p k) f -> e p (k f)", k=KC),
              a["w_exp_up"][0].rearrange("e (p k) f -> e p (k f)", k=KC)]
    down_w = a["w_exp_down"][0].rearrange("e (p j) n -> e p (j n)", j=2)

    def last_pair(eng):
        return eng.value_load(counts[0:1, 0:1], min_val=TOK * TOPK // P // 2 - 1, max_val=PAIRS - 2)

    def at_expert(w, e):
        return w[bass.ds(e, 1)].rearrange("a p n -> p (a n)")

    def pairs(eng, body, m):
        for u in range(2):
            body(0, u, first=True)
        with eng.Fori(1, m + 1) as i:
            for u in range(2):
                body(i, u)

    with nc.Block() as block:
        @block.sync
        def _(sp):
            m = last_pair(sp)

            def body(i, u, first=False):
                b = 2 * i + u
                col = counts[0:1, 1 + b:2 + b] if isinstance(b, int) else counts[0:1, bass.ds(b + 1, 1)]
                e = sp.value_load(col, min_val=0, max_val=NE - 1)
                if not first:
                    sp.wait_ge(s_gu, b - 1)
                for h in range(2):
                    sp.dma_start(wgu[u][:, h].rearrange("p k f -> p (k f)"), at_expert(gate_w[h], e)).then_inc(s_w[u], 16)
                if not first:
                    sp.wait_ge(s_y, b - 1)
                sp.dma_start(wd[u].rearrange("p j n -> p (j n)"), at_expert(down_w, e)).then_inc(s_wd[u], 16)

            pairs(sp, body, m)

        @block.tensor
        def _(pe):
            m = last_pair(pe)

            def turn(i, u):
                pe.wait_ge(s_g[u], 16 * (i + 1))
                for g in range(2):
                    for k in range(4):
                        last = nc.tensor.transpose(ps[:, 2 + g, k * P:(k + 1) * P],
                                                   xg[:, u, (4 * g + k) * P:(4 * g + k + 1) * P], C("ident"))
                    last.then_inc(s_t, 1)

            def turn_hidden(b, u, wait_bank):
                pe.wait_ge(s_hs, b + 1)
                if wait_bank:
                    pe.wait_ge(s_hc, b)
                for j in range(2):
                    last = nc.tensor.transpose(ps[:, 4, j * P:(j + 1) * P], hs[:, u, j * P:(j + 1) * P], C("ident"))
                last.then_inc(s_ht, 1)

            def down(i, u, b, wait_bank):
                pe.wait_ge(s_hc, b + 1)
                pe.wait_ge(s_wd[u], 16 * (i + 1))
                if wait_bank:
                    pe.wait_ge(s_ya, b)
                    pe.wait_ge(s_yv, b)
                for half in range(2):
                    for j in range(2):
                        last = nc.tensor.matmul(ps[:, 5 + half, :], hT[:, u, j * P:(j + 1) * P],
                                                wd[u][:, j, half * 512:(half + 1) * 512], start=(j == 0), stop=(j == 1))
                last.then_inc(s_y, 1)

            def body(i, u, first=False):
                b = 2 * i + u
                pe.wait_ge(s_xa, b + 1)
                pe.wait_ge(s_xv, b + 1)
                pe.wait_ge(s_w[u], 32 * (i + 1))
                if not first:
                    pe.wait_ge(s_hs, b - 1)
                for k in range(KC):
                    last = nc.tensor.matmul(ps[:, u, :], xT[:, u, k * P:(k + 1) * P], wgu[u][:, :, k, :],
                                            start=(k == 0), stop=(k == KC - 1))
                last.then_inc(s_gu, 1)
                before = not (first and u == 0)
                if before:
                    turn_hidden(b - 1, 1 - u, not first)
                turn(i if u == 0 else i + 1, 1 - u)
                if before:
                    down(i if u == 1 else i - 1, 1 - u, b - 1, not first)

            pe.wait_ge(s_z, 2)
            turn(0, 0)
            pairs(pe, body, m)
            turn_hidden(2 * m + 1, 1, True)
            down(m, 1, 2 * m + 1, True)

        @block.scalar
        def _(act):
            m = last_pair(act)

            def tokens(b):
                act.wait_ge(s_t, 2 * b + 1)
                nc.scalar.copy(xT[:, b_u[0], 0:512], ps[:, 2, :]).then_inc(s_xa, 1)

            b_u = [0]

            def rows(b, u, wait_buffer):
                act.wait_ge(s_y, b + 1)
                if wait_buffer:
                    act.wait_ge(s_sc, 16 * (b - 1))
                w = table[:, b, 1:2] if isinstance(b, int) else table[:, bass.ds(b, 1), 1:2].rearrange("p a w -> p (a w)")
                nc.scalar.activation(yb[:, u, 0:512], ps[:, 5, :], ACT.Copy, scale=w.bitcast(F32)).then_inc(s_ya, 1)

            def body(i, u, first=False):
                b = 2 * i + u
                act.wait_ge(s_gu, b + 1)
                nc.scalar.activation(sg[:, u, :], ps[:, u, 0:FE], ACT.Sigmoid).then_inc(s_sg, 1)
                b_u[0] = 1 - u
                tokens(b + 1)
                if not (first and u == 0):
                    rows(b - 1, 1 - u, not first)

            tokens(0)
            pairs(act, body, m)
            rows(2 * m + 1, 1, True)

        @block.vector
        def _(dve):
            m = last_pair(dve)
            st = Steps(dve, s_v)
            nc.vector.memset(xg[:, 0, :], 0.0).then_inc(s_z, 1)
            nc.vector.memset(xg[:, 1, :], 0.0).then_inc(s_z, 1)

            def tokens(b, u):
                dve.wait_ge(s_t, 2 * b + 2)
                nc.vector.tensor_copy(xT[:, u, 512:D], ps[:, 3, :]).then_inc(s_xv, 1)

            def hidden_columns(b, u):
                dve.wait_ge(s_ht, b + 1)
                nc.vector.tensor_copy(hT[:, u, :], ps[:, 4, 0:FE]).then_inc(s_hc, 1)

            def rows(b, u, wait_buffer):
                dve.wait_ge(s_y, b + 1)
                if wait_buffer:
                    dve.wait_ge(s_sc, 16 * (b - 1))
                w = table[:, b, 1:2] if isinstance(b, int) else table[:, bass.ds(b, 1), 1:2].rearrange("p a w -> p (a w)")
                nc.vector.tensor_scalar(yb[:, u, 512:D], ps[:, 6, :], w.bitcast(F32), None, ALU.mult).then_inc(s_yv, 1)

            def body(i, u, first=False):
                b = 2 * i + u
                if not (first and u == 0):
                    hidden_columns(b - 1, 1 - u)
                dve.wait_ge(s_sg, b + 1)
                st.loop(b)
                st.link(nc.vector.tensor_tensor(sg[:, u, :], sg[:, u, :], ps[:, u, 0:FE], ALU.mult))
                nc.vector.tensor_tensor(hs[:, u, :].rearrange("q (j p) -> q p j", j=2),
                                        sg[:, u, :].rearrange("q (p j) -> q p j", j=2),
                                        ps[:, u, FE:2 * FE].rearrange("q (p j) -> q p j", j=2), ALU.mult).then_inc(s_hs, 1)
                tokens(b + 1, 1 - u)
                if not (first and u == 0):
                    rows(b - 1, 1 - u, not first)

            tokens(0, 0)
            pairs(dve, body, m)
            hidden_columns(2 * m + 1, 1)
            rows(2 * m + 1, 1, True)

        @block.gpsimd
        def _(pool):
            m = last_pair(pool)
            pool.wait_ge(s_z, 2)

            limit = pool.to_reg(TOK - 1)

            r_gathered, r_turned, r_rows, r_added = [pool.alloc_register(name) for name in (
                "gathered", "turned", "rows", "added")]

            def held(register, value):
                if isinstance(value, int):
                    return value
                pool.reg_mov(register, value)
                return register

            def index(dst, b, s):
                src = table[:, b, 0:1] if isinstance(b, int) else table[:, bass.ds(b, 1), 0:1].rearrange("p a w -> p (a w)")
                nc.gpsimd.tensor_copy(dst, src).then_inc(s, 1)

            def gather(u, b, reuse):
                done = held(r_gathered, b + 1)
                if reuse:
                    turned = held(r_turned, 2 * (b - 1))
                    pool.wait_ge(s_z, 2)
                    pool.wait_ge(s_t, turned)
                index(gidx[:, u:u + 1], b, s_gi)
                pool.wait_ge(s_z, 2)
                pool.wait_ge(s_gi, done)
                pool.indirect_dma_start(xg[:, u, :], None, h2_d, bass.IndirectOffsetOnAxis(ap=gidx[:, u:u + 1], axis=0),
                                        bounds_check=limit, oob_is_err=False).then_inc(s_g[u], 16)

            def scatter(u, b):
                done, added = held(r_rows, b + 1), held(r_added, 16 * b)
                pool.wait_ge(s_z, 2)
                if not (isinstance(b, int) and b == 0):
                    pool.wait_ge(s_sc, added)
                index(sidx[:, u:u + 1], b, s_si)
                pool.wait_ge(s_z, 2)
                pool.wait_ge(s_si, done)
                pool.wait_ge(s_ya, done)
                pool.wait_ge(s_yv, done)
                pool.indirect_dma_start(acc_d, bass.IndirectOffsetOnAxis(ap=sidx[:, u:u + 1], axis=0), yb[:, u, :], None,
                                        compute_op=ALU.add).then_inc(s_sc, 16)

            def body(i, u, first=False):
                b = 2 * i + u
                gather(u, b + 2, True)
                if not (first and u == 0):
                    scatter(1 - u, b - 1)

            gather(0, 0, False)
            gather(1, 1, False)
            pairs(pool, body, m)
            scatter(1, 2 * m + 1)
            pool.wait_ge(s_z, 2)
            pool.wait_ge(s_g[0], 16 * (m + 2))
            pool.wait_ge(s_z, 2)
            pool.wait_ge(s_g[1], 16 * (m + 2))
            pool.wait_ge(s_z, 2)
            pool.wait_ge(s_sc, 32 * m + 32)


def final_stage(env):
    nc, a, o, ps, R, C, sem = (env[k] for k in ("nc", "a", "o", "ps", "R", "C", "sem"))
    acc_d = env["acc_d"]
    x, gate2 = carve(R["x"], (NT, D)), carve(R["qbT"], (2, D))
    acc = carve(R["hT"], (NT, D))
    gain, sq = carve(R["Q"], (D,), (D,))
    ss = carve(R["small"], (NT,))
    s_a = [sem("f_gain_and_first_rows"), sem("f_other_rows")]
    s_x, s_sq, s_m, s_rt, s_y, s_o = (sem("f_x2"), sem("f_sumsq"),
                                                sem("f_mean"), sem("f_root"), sem("f_rows"), sem("f_stored"))

    with nc.Block() as block:
        @block.sync
        def _(sp):
            for t in range(NT):
                sp.dma_start(acc[:, t, :], acc_d[t * P:(t + 1) * P, :]).then_inc(s_a[min(t, 1)], 16)
            for t in range(NT):
                sp.wait_ge(s_y, t + 1)
                dst = o[0][0, t * P:(t + 1) * P, :] if t < PT else o[1].rearrange("b n d -> (b n) d")
                sp.dma_start(dst, acc[:, t, :]).then_inc(s_o, 16)
            sp.wait_ge(s_o, 16 * NT)

        @block.scalar
        def _(act):
            act.dma_start(gain, a["final_g"][None, :].to_broadcast([P, D])).then_inc(s_a[0], 16)
            for t in range(NT):
                act.wait_ge(s_x, t + 1)
                if t:
                    act.wait_ge(s_sq, t)
                nc.scalar.activation(sq, x[:, t, :], ACT.Square, accum_out=ss[:, t:t + 1]).then_inc(s_sq, 1)
                act.wait_ge(s_m, t + 1)
                nc.scalar.activation(ss[:, t:t + 1], ss[:, t:t + 1], ACT.Sqrt).then_inc(s_rt, 1)

        @block.vector
        def _(dve):
            st = env["dve_steps"].resume(dve)

            def residual(t):
                dve.wait_ge(s_a[min(t, 1)], 64 if t else 32)
                st.link(nc.vector.tensor_tensor(acc[:, t, :], acc[:, t, :], gate2[:, int(t == PT), :], ALU.mult))
                nc.vector.tensor_tensor(x[:, t, :], x[:, t, :], acc[:, t, :], ALU.add).then_inc(s_x, 1)

            residual(0)
            for t in range(NT):
                if t + 1 < NT:
                    residual(t + 1)
                dve.wait_ge(s_sq, t + 1)
                nc.vector.tensor_scalar(ss[:, t:t + 1], ss[:, t:t + 1], 1.0 / D, EPS, ALU.mult, ALU.add).then_inc(s_m, 1)
                dve.wait_ge(s_rt, t + 1)
                st.link(nc.vector.reciprocal(ss[:, t:t + 1], ss[:, t:t + 1]))
                nc.vector.scalar_tensor_tensor(acc[:, t, :], x[:, t, :], ss[:, t:t + 1], gain, ALU.mult,
                                               ALU.mult).then_inc(s_y, 1)


_INS = ['x_prompt', 'x_sample', 'cache_fox_k', 'cache_fox_v', 'cache_fox_logf', 'cache_swa_k', 'cache_swa_v',
        'c_prompt', 'c_sample', 'w_ada', 'b_ada', 'norm1_g', 'w_in', 'fox_b_f', 'w_branch_a', 'w_branch_b',
        'w_out', 'swa_sinks', 'norm2_g', 'w_router', 'router_bias', 'w_exp_gate', 'w_exp_up', 'w_exp_down',
        'w_sh_gate', 'w_sh_up', 'w_sh_down', 'final_g']
OUTS = [(1, SEQ, D), (DB, DN, D),
        (1, 1, SEQ, H, HD), (1, 1, SEQ, H, HD), (1, 1, SEQ, H), (1, 1, SINKW, KVH, HD), (1, 1, SINKW, KVH, HD),
        (1, DB, DN, H, HD), (1, DB, DN, H, HD), (1, DB, DN, H), (1, DB, SINKW, KVH, HD), (1, DB, SINKW, KVH, HD)]


def prepare(inputs, np):
    arrays = {n: np.ascontiguousarray(inputs[n]) for n in _INS}
    arrays["const"] = constants(np)
    empty = np.zeros((SLOTS * P, 2), np.uint32)
    empty[:, 0] = TOK + np.arange(SLOTS * P) // SLOTS
    arrays["empty_table"] = empty
    return arrays


def kernel(**inputs):
    import numpy as _np
    import concourse.bacc as _bacc
    from concourse import mybir as _mybir
    from concourse.bass_utils import run_bass_kernel_spmd as _run

    nc = _bacc.Bacc("TRN2", target_bir_lowering=False, num_devices=1)
    arrays = prepare(inputs, _np)
    a = {n: nc.dram_tensor("in_" + n, v.shape, _mybir.dt.from_np(v.dtype), kind="ExternalInput").ap()
         for n, v in arrays.items()}
    o = [nc.dram_tensor(f"out_{i}", s, _mybir.dt.float32, kind="ExternalOutput").ap() for i, s in enumerate(OUTS)]
    build(nc, a, o)
    r = _run(nc, [{"in_" + n: v for n, v in arrays.items()}], core_ids=[0])
    return tuple(r.results[0][f"out_{i}"] for i in range(len(OUTS)))
```

```python
from contextlib import ExitStack

import concourse.bass as bass
from concourse import mybir

F32 = mybir.dt.float32
F32R = mybir.dt.float32r
I32 = mybir.dt.int32
U32 = mybir.dt.uint32
ALU = mybir.AluOpType
ACT = mybir.ActivationFunctionType
AX = mybir.AxisListType.X

P = 128
D = 1024
KC = D // P
SEQ, DB, DN, PAST = 512, 8, 16, 1024
TOK = SEQ + DB * DN
NT = TOK // P
PT = SEQ // P
H, HD = 8, 64
HW = H * HD
KVH = 2
KW = KVH * HD
GROUP = H // KVH
SINKW = 128
NE, TOPK, NG, TOPG = 64, 8, 8, 4
FE = 256
ROUTED_SCALE = 2.5
EPS = 1e-6
NEG = -1e30
ATT_SCALE = HD ** -0.5
PAIRS = (TOK * TOPK // P + NE + 1) // 2 + 1
SLOTS = 2 * PAIRS
JC = PAST // P
NM = 6 * D
O_Q, O_K, O_V, O_F = 0, HW, 2 * HW, 3 * HW
O_QB = 3 * HW + H
O_KB = O_QB + HW
O_GA = O_KB + 2 * KW
O_GB = O_GA + D
CONST = {}
_at = 0
for _name, _n in (("ident", P), ("tri_incl", P), ("tri_strict", P), ("suffix", P), ("ones", P), ("causal", P),
                  ("same", P), ("swa_dist", 2 * P), ("others", P), ("fox_new", DN), ("swa_old", P), ("swa_new", DN),
                  ("headmask", HW), ("groupmask", KW), ("fold16", DN), ("fold64", GROUP * DN),
                  ("ties", NG * NG), ("iota64", NE), ("pairs2", PAIRS), ("pcol", 1)):
    CONST[_name] = (_at, _n)
    _at += _n
NCONST = _at


def constants(np):
    c = np.zeros((P, NCONST), np.float32)
    p = np.arange(P)

    def put(name, a):
        at, n = CONST[name]
        c[:, at:at + n] = np.broadcast_to(a, (P, n))

    put("ident", np.eye(P))
    put("tri_incl", p[:, None] <= p[None])
    put("tri_strict", p[:, None] < p[None])
    put("suffix", p[:, None] > p[None])
    put("ones", np.ones((P, P)))
    put("causal", np.where(p[None] <= p[:, None], 0.0, NEG))
    b, n = p // DN, p % DN
    put("same", -((b[:, None] == b[None]) & (n[:, None] <= n[None])).astype(np.float32))
    key = np.arange(2 * P) - P
    d = np.abs(p[:, None] - key[None]).astype(np.float32)
    ok = (key[None] // 64 >= p[:, None] // 64 - 2) & (key[None] // 64 <= p[:, None] // 64)
    put("swa_dist", np.where(ok, d, 3e32))
    h, q = p // DN, p % DN
    slope = 2.0 ** (-8.0 * (h + 1) / H)
    k = np.arange(DN)
    put("others", np.where((p[:, None] < DB * H) & (b[None] != p[:, None] // H), NEG, 0.0))
    put("fox_new", np.where(k[None] <= q[:, None], 0.0, NEG))
    put("swa_old", -slope[:, None] * (SINKW + q[:, None] - p[None]))
    put("swa_new", -slope[:, None] * np.abs(q[:, None] - k[None]))
    put("headmask", h[:, None] == np.arange(HW)[None] // HD)
    put("groupmask", h[:, None] // GROUP == np.arange(KW)[None] // HD)
    put("fold16", q[:, None] == np.arange(DN)[None])
    i = np.arange(GROUP * DN)
    put("fold64", (h[:, None] % GROUP == i[None] // DN) & (q[:, None] == i[None] % DN))
    g = np.arange(NG)
    put("ties", (g[None] < g[:, None]).reshape(1, -1))
    put("iota64", np.arange(NE)[None])
    put("pairs2", 2 * (1 + np.arange(PAIRS))[None])
    put("pcol", p[:, None])
    return c


class Steps:

    def __init__(self, eng, sem):
        self.eng, self.sem, self.base, self.n = eng, sem, 0, 0

    def link(self, ins):
        self.n += 1
        ins.then_inc(self.sem, 1)
        self.eng.wait_ge(self.sem, self.base + self.n)

    def resume(self, eng):
        self.eng = eng
        return self

    def loop(self, base):
        self.base, self.n = base, 0


HALF = TOK // 2


def split_product(nc, out, pairs, begin, end):
    last = None
    for n, ((lh, ll), (rh, rl)) in enumerate(pairs):
        for j, (l, r) in enumerate(((lh, rh), (ll, rh), (lh, rl))):
            last = nc.tensor.matmul(out, l, r, start=begin and n == 0 and j == 0,
                                    stop=end and n == len(pairs) - 1 and j == 2)
    return last


def build(nc, a, o):
    with ExitStack() as ctx:
        def sem(name):
            return ctx.enter_context(nc.semaphore(name))

        def scratch(name, shape, dt=F32):
            return nc.dram_tensor(name, shape, dt, kind="Internal").ap()

        S = {}
        ps = ctx.enter_context(nc.psum_tensor("ps", [P, 8, 512], F32))
        mod_d = scratch("mod_d", [1 + DB, NM])
        h2_d = scratch("h2_d", [TOK, D])
        acc_d = scratch("acc_d", [TOK + P, D])
        tab_d = scratch("tab_d", [SLOTS * P, 2], U32)

        sizes = dict(wst=9 * DB * H, const=NCONST, x=NT * D, hT=KC * TOK, Q=NT * D, ring=4 * KC * 512,
                     qbT=GROUP * TOK, kbT=TOK, v=NT * HW, kvb=NT * 2 * KW, oaT=4 * TOK, obT=4 * TOK,
                     work=4 * D, biasT=PAST + P, logf=NT * H + JC * DB * H, small=336)
        R = {}
        RR = {}
        for name, n in sizes.items():
            at = -(-nc.sbuf_base // 32) * 32
            R[name] = ctx.enter_context(nc.sbuf_tensor("r_" + name, [P, n], F32))
            if name in ("x", "hT", "ring", "qbT", "v", "work", "oaT", "obT"):
                RR[name] = nc.alloc_sbuf_tensor_at("rounded_" + name, [P, n], F32R, offset=at)

        def C(name, rows=P):
            at, n = CONST[name]
            return R["const"][0:rows, at:at + n]

        env = dict(nc=nc, a=a, o=o, ps=ps, R=R, RR=RR, C=C, sem=sem, mod_d=mod_d, h2_d=h2_d, acc_d=acc_d,
                   tab_d=tab_d, S=S)
        env["counts"] = ctx.enter_context(nc.sbuf_tensor("counts", [P, 1 + P], I32))
        env["table"] = R["biasT"][:, 0:2 * SLOTS].bitcast(U32)
        env["kv"] = [sem("k_cache_even"), sem("k_cache_odd"), sem("v_cache_even"), sem("v_cache_odd")]
        env["s_outputs"] = sem("outputs_stored")
        env["s_sub"] = [sem(f"d_w_gate{c}") for c in range(4)]
        env["s_branch"] = sem("d_w_branches")
        env["sub"] = [carve(R["ring"][:, s * D:(s + 1) * D], (KC, P)) for s in range(8)]
        env["wa"], env["wb"] = carve(R["ring"][:, 8192:], (4, D), (GROUP, D))
        env["s_sinks"] = sem("sinks_loaded")
        env["s_zeros"] = sem("gather_buffers_zeroed")
        env["s_down"] = [sem("e_w_down_even"), sem("e_w_down_odd")]
        env["wd"] = carve(R["ring"], (2, D), (2, D))
        env["s_gate_up"] = [sem("e_w_gu_even"), sem("e_w_gu_odd")]
        env["wgu"] = [carve(R[name][:, 0:4096], (2, KC, FE)) for name in ("hT", "work")]
        env["dve_steps"] = Steps(None, sem("dve_steps"))
        for stage in (project_stage, prompt_stage, sample_stage, mix_stage, expert_stage, final_stage):
            stage(env)


def carve(region, *shapes):
    out, at = [], 0
    for shape in shapes:
        n = 1
        for s in shape:
            n *= s
        v = region[:, at:at + n]
        if len(shape) == 2:
            v = v.rearrange("p (x y) -> p x y", y=shape[1])
        elif len(shape) == 3:
            v = v.rearrange("p (x y z) -> p x y z", y=shape[1], z=shape[2])
        out.append(v)
        at += n
    return out if len(out) > 1 else out[0]


def project_stage(env):
    nc, a, o, ps, R, C, sem = (env[k] for k in ("nc", "a", "o", "ps", "R", "C", "sem"))
    mod_d, RR = env["mod_d"], env["RR"]
    x = carve(R["x"], (NT, D))
    hT = carve(R["hT"], (KC, TOK))
    hrow = carve(R["Q"], (NT, D))
    qT, kT = carve(R["Q"], (4, TOK), (4, TOK))
    qbT = carve(R["qbT"], (GROUP, TOK))
    kbT = R["kbT"]
    v = carve(R["v"], (NT, HW))
    kvb = carve(R["kvb"], (NT, 2 * KW))
    ring = [R["ring"][:, s * 4096:(s + 1) * 4096] for s in range(4)]
    modp = carve(R["work"], (2, D))
    mods = carve(R["work"][:, 2 * D:], (2, D))
    logf = carve(R["logf"], (NT, H))
    clogf = R["logf"][:, NT * H:].rearrange("p (b j h) -> p b (j h)", b=DB, h=H)
    m_sb = [R["oaT"][0:1 + DB, 0:D], R["biasT"][0:1 + DB, P:P + D]]
    b_sb = carve(R["obT"], (2, D))[0:1 + DB, :, :]
    c_sb = R["kvb"][0:1 + DB, 0:D]
    g1_sb = R["v"][0:1 + DB, 0:D]
    g2_sb = R["v"][0:1 + DB, D:2 * D]
    sg_sb = R["qbT"][0:1 + DB, 0:D]
    cT = carve(R["biasT"], (KC, 1 + DB))
    stat, rstd, bf, lt = carve(R["small"], (NT,), (NT,), (H,), (5, NT * H))
    kst = carve(R["x"], (NT, HW))
    hT_high = carve(RR["x"], (KC, TOK))
    hT_low = [carve(RR["oaT"], (4, TOK)), carve(RR["obT"], (4, TOK))]
    w_high = carve(RR["work"], (KC, 512))
    ring_low = [RR["ring"][:, s * 4096:(s + 1) * 4096] for s in range(4)]

    s_rest = sem("a_const_rest")
    s_const, s_c, s_g = sem("a_const"), sem("a_c_rows"), sem("a_norm_gains")
    s_x = sem("a_x_rows")
    s_clf = env["S"]["cached_logf"] = sem("cached_logf")
    s_bada = [sem("a_bias_part0"), sem("a_bias_part1")]
    s_w = [sem(f"a_w_slot{i}") for i in range(4)]
    s_mout = [sem("a_mod_stored0"), sem("a_mod_stored1")]
    s_mod = sem("a_mod_loaded")
    s_sig, s_silu, s_cT, s_cTc = sem("a_sigmoid_c"), sem("a_silu_c"), sem("a_cT_psum"), sem("a_cT_sbuf")
    s_ada, s_left, s_m = sem("a_ada_psum"), sem("a_ada_left_psum"), sem("a_scale_rows")
    s_sq, s_var, s_rt = sem("a_sumsq"), sem("a_variance"), sem("a_root")
    s_h, s_tr = sem("a_h_rows"), sem("a_h_transposed")
    s_high, s_low = sem("a_high_parts"), sem("a_low_parts")
    s_mm, s_ea, s_ev = sem("a_proj_psum"), sem("a_proj_by_act"), sem("a_proj_by_dve")
    s_lf, s_exp, s_ln = sem("a_logit"), sem("a_exp_logit"), sem("a_ln")
    s_o = env["s_outputs"]

    w_in = a["w_in"][0].rearrange("(k p) n -> p k n", p=P)
    w_ada = a["w_ada"][0].rearrange("(k p) n -> p k n", p=P)
    pieces = [(w_ada[:, :, 512 * n:512 * (n + 1)], 512) for n in range(NM // 512)]
    NA = len(pieces)
    pieces += [(w_in[:, :, O_Q:O_Q + 512], 512), (w_in[:, :, O_K:O_K + 512], 512),
               (w_in[:, :, O_V:O_V + 512], 512), (w_in[:, :, O_KB:O_KB + 2 * KW], 2 * KW + H),
               (w_in[:, :, O_QB:O_QB + 512], 512)]
    W_Q, W_K, W_V, W_KV, W_QB = range(NA, NA + 5)

    def wslot(n):
        return carve(ring[n % 4], (KC, pieces[n][1]))

    def wlow(n):
        return carve(ring_low[n % 4], (KC, pieces[n][1]))

    wqb = carve(ring_low[W_V % 4], (KC, 512))
    s_pool = sem("a_hT_joined_and_w_qb")
    FIRST_HT, FIRST_K = 4, 4 + 2 * NT

    def weight_split(n, c):
        cols = slice(c * P, (c + 1) * P)
        return wslot(n)[:, :, cols], w_high[:, :, cols], wlow(n)[:, :, cols]

    jobs = []
    for c in range(4):
        jobs += [("q", c, 0), ("q", c, 1)]
    for c in range(4):
        jobs += [("k", c, 0), ("k", c, 1)]
    for t in range(NT):
        jobs += [("v", t, 0)]
    for t in range(NT):
        jobs += [("kv", t, 0)]
    for c in range(4):
        jobs += [("qb", c, 0), ("qb", c, 1)]
    for t in range(NT):
        jobs += [("kbT", t, 0)]
    for t in range(NT):
        jobs += [("krow", t, 0)]
    job_no = {j: n for n, j in enumerate(jobs)}
    by_act = [n % 2 == 0 and j[0] != "kv" for n, j in enumerate(jobs)]
    done_a = [sum(by_act[:n + 1]) for n in range(len(jobs))]
    done_v = [n + 1 - done_a[n] for n in range(len(jobs))]
    PB = 6

    def job_done(eng, n):
        if by_act[n]:
            eng.wait_ge(s_ea, done_a[n])
        else:
            eng.wait_ge(s_ev, done_v[n])

    def last_use(n):
        if n < NA:
            return s_ada, n + 1
        kind = {W_Q: "q", W_K: "k", W_V: "v", W_KV: "kv", W_QB: "qb"}[n]
        return s_mm, max(m for m, j in enumerate(jobs) if j[0] == kind) + 1

    def evacuate(eng, n, j):
        kind, i, part = j
        bank = ps[:, n % PB, :]
        if kind in ("q", "k", "qb"):
            dst = {"q": qT, "k": kT, "qb": qbT}[kind][:, i, part * HALF:(part + 1) * HALF]
            src = bank[:, 0:HALF]
            if kind == "k":
                return nc.scalar.copy(dst, src) if by_act[n] else nc.vector.tensor_copy(dst, src)
            if by_act[n]:
                return nc.scalar.mul(dst, src, ATT_SCALE)
            return nc.vector.tensor_scalar(dst, src, ATT_SCALE, None, ALU.mult)
        if kind == "kv":
            nc.vector.tensor_tensor(lt[:, 0, i * H:(i + 1) * H], bank[:, 2 * KW:2 * KW + H], bf, ALU.add)
        dst, src = {"v": (v[:, i, :], bank), "kv": (kvb[:, i, :], bank[:, 0:2 * KW]),
                    "kbT": (kbT[:, i * P:(i + 1) * P], bank[:, 0:P]), "krow": (kst[:, i, :], bank)}[kind]
        return nc.scalar.copy(dst, src) if by_act[n] else nc.vector.tensor_copy(dst, src)

    with nc.Block() as block:
        @block.sync
        def _(sp):
            sp.dma_start(c_sb[0:1, :], a["c_prompt"]).then_inc(s_c, 16)
            sp.dma_start(c_sb[1:1 + DB, :], a["c_sample"]).then_inc(s_c, 16)
            sp.dma_start(R["const"][:, 0:P], a["const"][:, 0:P]).then_inc(s_const, 16)
            for part in range(2):
                sp.dma_start(b_sb[:, part, :], a["b_ada"][:, part * D:(part + 1) * D]
                             .to_broadcast([1 + DB, D])).then_inc(s_bada[part], 16)
            for n in range(NA + 5):
                if n == 4:
                    sp.dma_start(R["const"][:, P:], a["const"][:, P:]).then_inc(s_rest, 16)
                if n >= 4:
                    s, val = last_use(n - 4)
                    sp.wait_ge(s, val)
                if n == W_KV:
                    sp.dma_start(wslot(n)[:, :, 0:2 * KW], pieces[n][0]).then_inc(s_w[n % 4], 16)
                    with nc.allow_non_contiguous_dma(reason="eight columns of forget logits"):
                        sp.dma_start(wslot(n)[:, :, 2 * KW:], w_in[:, :, O_F:O_F + H]).then_inc(s_w[n % 4], 16)
                else:
                    sp.dma_start(wslot(n), pieces[n][0]).then_inc(s_w[n % 4], 16)
            for t in range(NT):
                job_done(sp, job_no[("v", t, 0)])
            sp.dma_start(o[3].rearrange("l b (t p) h d -> p (l b t) (h d)", p=P), v[:, 0:PT, :]).then_inc(s_o, 16)
            sp.dma_start(o[8].rearrange("l b n h d -> (l b n) (h d)"), v[:, PT, :]).then_inc(s_o, 16)
            sp.wait_ge(s_lf, 2)
            sp.dma_start(o[4].rearrange("l b (t p) h -> p (l b t) h", p=P), logf[:, 0:PT, :]).then_inc(s_o, 16)
            sp.dma_start(o[9].rearrange("l b n h -> (l b n) h"), logf[:, PT, :]).then_inc(s_o, 16)
            for t in range(NT):
                job_done(sp, job_no[("kv", t, 0)])
            for half, (po, so, cache) in enumerate(((o[5], o[10], a["cache_swa_k"]), (o[6], o[11], a["cache_swa_v"]))):
                cols = slice(half * KW, (half + 1) * KW)
                sp.dma_start(po.rearrange("l b p h d -> (l b p) (h d)"), kvb[:, PT - 1, cols]).then_inc(s_o, 16)
                win, old = so[0].rearrange("b s h d -> b s (h d)"), cache[0].rearrange("b s h d -> b s (h d)")
                sp.dma_start(win[:, 0:SINKW - DN, :], old[:, DN:SINKW, :]).then_inc(s_o, 16)
                for b in range(DB):
                    sp.dma_start(win[b, SINKW - DN:SINKW, :], kvb[b * DN:(b + 1) * DN, PT, cols]).then_inc(s_o, 16)
            kp = o[2].rearrange("l b (t p) h d -> (l b t) p (h d)", p=P)
            ks = o[7].rearrange("l b n h d -> (l b n) (h d)")
            for t in range(NT):
                job_done(sp, job_no[("krow", t, 0)])
                sp.dma_start(kp[t] if t < PT else ks, kst[:, t, :]).then_inc(s_o, 16)
            sp.wait_ge(s_rest, 16)
            for part in range(2):
                sp.wait_ge(s_mout[part], 48)

        @block.scalar
        def _(act):
            act.wait_ge(s_c, 32)
            nc.scalar.activation(sg_sb, c_sb, ACT.Sigmoid).then_inc(s_sig, 1)
            act.dma_start(x[:, 0:PT, :], a["x_prompt"][0].rearrange("(t p) d -> p t d", p=P)).then_inc(s_x, 16)
            act.dma_start(x[:, PT, :], a["x_sample"].rearrange("b n d -> (b n) d")).then_inc(s_x, 16)
            act.dma_start(g1_sb, a["norm1_g"].to_broadcast([1 + DB, D])).then_inc(s_g, 16)
            act.dma_start(g2_sb, a["norm2_g"].to_broadcast([1 + DB, D])).then_inc(s_g, 16)
            act.dma_start(clogf, a["cache_fox_logf"][0].rearrange("b (p j) h -> p b (j h)", j=JC)).then_inc(s_clf, 16)
            act.dma_start(bf, a["fox_b_f"].to_broadcast([P, H])).then_inc(s_g, 16)
            act.wait_ge(s_x, 32)
            sq_v = R["qbT"][:, D:2 * D]
            for t in range(NT):
                if t:
                    act.wait_ge(s_sq, t)
                nc.scalar.activation(sq_v, x[:, t, :], ACT.Square, accum_out=stat[:, t:t + 1]).then_inc(s_sq, 1)
            act.wait_ge(s_var, 1)
            nc.scalar.activation(rstd, stat, ACT.Sqrt).then_inc(s_rt, 1)
            for part in range(6):
                if part == 5:
                    act.wait_ge(s_h, NT)
                    act.wait_ge(s_w[W_Q % 4], 16 * (W_Q // 4 + 1))
                    for c in range(4):
                        raw, high, _low = weight_split(W_Q, c)
                        nc.scalar.copy(high, raw).then_inc(s_high, 1)
                if part in (1, 4):
                    act.wait_ge(s_m, 1 if part == 1 else 2)
                else:
                    act.wait_ge(s_left, 2 * part + 2)
                act.dma_start(mod_d[:, part * D:(part + 1) * D], m_sb[part % 2]).then_inc(s_mout[part % 2], 16)
                if part + 2 < 6:
                    act.dma_start(b_sb[:, part % 2, :], a["b_ada"][:, (part + 2) * D:(part + 3) * D]
                                  .to_broadcast([1 + DB, D])).then_inc(s_bada[part % 2], 16)
                if part == 1:
                    act.wait_ge(s_mout[0], 16)
                    act.wait_ge(s_mout[1], 16)
                    load_mod(act, mod_d, R["work"][:, 0:2 * D], R["work"][:, 2 * D:4 * D], 0, 2, s_mod)
            for n in range(2 * NT):
                act.wait_ge(s_tr, n + 1)
                t, g = n // 2, n % 2
                nc.scalar.copy(hT_high[:, 4 * g:4 * g + 4, t * P:(t + 1) * P],
                               ps[:, n % 4, :].rearrange("p (k t) -> p k t", t=P)).then_inc(s_high, 1)
            for n, j in enumerate(jobs):
                if by_act[n]:
                    act.wait_ge(s_mm, n + 1)
                    evacuate(act, n, j).then_inc(s_ea, 1)
                if j[0] == "q" and j[2] == 1:
                    act.wait_ge(s_mm, n + 1)
                    if j[1] == 0:
                        act.wait_ge(s_w[W_K % 4], 16 * (W_K // 4 + 1))
                    raw, high, _low = weight_split(W_K, j[1])
                    nc.scalar.copy(high, raw).then_inc(s_high, 1)
                if j == ("kv", NT - 1, 0):
                    act.wait_ge(s_lf, 1)
                    nc.scalar.activation(lt[:, 1, :], lt[:, 1, :], ACT.Exp, scale=-1.0).then_inc(s_exp, 1)
                    act.wait_ge(s_exp, 2)
                    nc.scalar.activation(lt[:, 3, :], lt[:, 2, :], ACT.Ln).then_inc(s_ln, 1)

        @block.tensor
        def _(pe):
            pe.wait_ge(s_const, 16)
            pe.wait_ge(s_silu, 1)
            for k in range(KC):
                last = nc.tensor.transpose(ps[:, 7, k * 9:(k + 1) * 9], sg_sb[:, k * P:(k + 1) * P],
                                           C("ident", 9)[:, 0:9])
            last.then_inc(s_cT, 1)
            pe.wait_ge(s_cTc, 1)
            for n in range(NA):
                pe.wait_ge(s_w[n % 4], 16 * (n // 4 + 1))
                if n >= 4:
                    pe.wait_ge(s_left, n - 3)
                for k in range(KC):
                    last = nc.tensor.matmul(ps[0:9, n % 4, :], cT[:, k, :], wslot(n)[:, k, :],
                                            start=(k == 0), stop=(k == KC - 1))
                last.then_inc(s_ada, 1)
            for n in range(2 * NT):
                t, g = n // 2, n % 2
                pe.wait_ge(s_h, t + 1)
                if n >= 4:
                    pe.wait_ge(s_low, FIRST_HT + n - 3)
                else:
                    pe.wait_ge(s_left, NA - 3 + n)
                for k in range(4):
                    last = nc.tensor.transpose(ps[:, n % 4, k * P:(k + 1) * P],
                                               hrow[:, t, (4 * g + k) * P:(4 * g + k + 1) * P], C("ident"))
                last.then_inc(s_tr, 1)
            need = {"q": W_Q, "k": W_K, "v": W_V, "kv": W_KV, "qb": W_QB}
            for n, (kind, i, part) in enumerate(jobs):
                if kind == "qb" and i == 0 and part == 0:
                    pe.wait_ge(s_pool, 2 + 2 * KVH)
                elif kind in ("q", "k"):
                    if part == 0:
                        pe.wait_ge(s_low, (FIRST_HT + 2 * NT) if kind == "q" else FIRST_K + i + 1)
                elif kind in need and i == 0 and part == 0:
                    m = need[kind]
                    if kind == "v":
                        pe.wait_ge(s_pool, 2)
                    pe.wait_ge(s_w[m % 4], 16 * (m // 4 + (2 if m == W_KV else 1)))
                if n >= PB:
                    job_done(pe, n - PB)
                bank = ps[:, n % PB, :]
                if kind in ("q", "k", "qb"):
                    w = wqb if kind == "qb" else wlow(need[kind])
                    cols, wcols = slice(part * HALF, (part + 1) * HALF), slice(i * P, (i + 1) * P)
                    last = split_product(nc, bank[:, 0:HALF], [
                        ((w_high[:, k, wcols], w[:, k, wcols]), (hT_high[:, k, cols], hT_low[k // 4][:, k % 4, cols]))
                        for k in range(KC)], True, True)
                elif kind in ("v", "kv"):
                    w = wslot(need[kind])
                    for k in range(KC):
                        last = nc.tensor.matmul(bank[:, 0:pieces[need[kind]][1]], hT[:, k, i * P:(i + 1) * P],
                                                w[:, k, :], start=(k == 0), stop=(k == KC - 1))
                elif kind == "kbT":
                    job_done(pe, job_no[("kv", i, 0)])
                    last = nc.tensor.transpose(bank[:, 0:P], kvb[:, i, 0:KW], C("ident"))
                else:
                    if i == 0:
                        job_done(pe, job_no[("k", 3, 0)])
                        job_done(pe, job_no[("k", 3, 1)])
                    for c in range(4):
                        last = nc.tensor.transpose(bank[:, c * P:(c + 1) * P], kT[:, c, i * P:(i + 1) * P], C("ident"))
                last.then_inc(s_mm, 1)

        @block.vector
        def _(dve):
            st = env["dve_steps"].resume(dve)
            dve.wait_ge(s_sig, 1)
            nc.vector.tensor_tensor(sg_sb, sg_sb, c_sb, ALU.mult).then_inc(s_silu, 1)
            dve.wait_ge(s_cT, 1)
            nc.vector.tensor_copy(cT, ps[:, 7, 0:KC * 9].rearrange("p (k m) -> p k m", m=9)).then_inc(s_cTc, 1)
            dve.wait_ge(s_sq, NT)
            nc.vector.tensor_scalar(stat, stat, 1.0 / D, EPS, ALU.mult, ALU.add).then_inc(s_var, 1)
            dve.wait_ge(s_rt, 1)
            st.link(nc.vector.reciprocal(rstd, rstd))
            dve.wait_ge(s_g, 48)

            def rows(t):
                mod = modp if t < PT else mods
                st.link(nc.vector.scalar_tensor_tensor(hrow[:, t, :], x[:, t, :], rstd[:, t:t + 1], mod[:, 1, :],
                                                       ALU.mult, ALU.mult))
                nc.vector.tensor_tensor(hrow[:, t, :], hrow[:, t, :], mod[:, 0, :], ALU.add).then_inc(s_h, 1)

            for part in range(6):
                if part == 5:
                    rows(3)
                    rows(4)
                    for c in range(4):
                        raw, high, low = weight_split(W_Q, c)
                        dve.wait_ge(s_high, c + 1)
                        nc.vector.tensor_tensor(low, raw, high.bitcast(F32), ALU.subtract).then_inc(s_low, 1)
                if part >= 2:
                    dve.wait_ge(s_mout[part % 2], 16 * (part // 2))
                dve.wait_ge(s_bada[part % 2], 16 * (part // 2 + 1))
                for half in range(2):
                    n = 2 * part + half
                    dve.wait_ge(s_ada, n + 1)
                    ins = nc.vector.tensor_tensor(m_sb[part % 2][:, half * 512:(half + 1) * 512], ps[0:9, n % 4, :],
                                                  b_sb[:, part % 2, half * 512:(half + 1) * 512], ALU.add)
                    ins.then_inc(s_left, 1)
                if part in (1, 4):
                    dve.wait_ge(s_left, 2 * part + 2)
                    nc.vector.scalar_tensor_tensor(m_sb[part % 2], m_sb[part % 2], 1.0,
                                                   g1_sb if part == 1 else g2_sb, ALU.add, ALU.mult).then_inc(s_m, 1)
                if part == 3:
                    dve.wait_ge(s_mod, 32)
                if part == 3:
                    rows(0)
                if part == 4:
                    rows(1)
                    rows(2)
            dve.wait_ge(s_mout[0], 48)
            for n in range(2 * NT):
                dve.wait_ge(s_high, FIRST_HT + n + 1)
                t, g = n // 2, n % 2
                cols = slice(t * P, (t + 1) * P)
                nc.vector.tensor_tensor(hT_low[g][:, :, cols], ps[:, n % 4, :].rearrange("p (k t) -> p k t", t=P),
                                        hT_high[:, 4 * g:4 * g + 4, cols].bitcast(F32), ALU.subtract).then_inc(s_low, 1)
            for n, j in enumerate(jobs):
                if not by_act[n]:
                    dve.wait_ge(s_mm, n + 1)
                    evacuate(dve, n, j).then_inc(s_ev, 1)
                if j[0] == "q" and j[2] == 1:
                    raw, high, low = weight_split(W_K, j[1])
                    dve.wait_ge(s_high, FIRST_K + j[1] + 1)
                    nc.vector.tensor_tensor(low, raw, high.bitcast(F32), ALU.subtract).then_inc(s_low, 1)
                if j == ("kv", NT - 1, 0):
                    z, u, w, lnw, e = (lt[:, r, :] for r in range(5))
                    dve.wait_ge(s_ev, done_v[n])
                    st.link(nc.vector.tensor_scalar(u, z, -1.0, None, ALU.mult))
                    nc.vector.tensor_tensor(u, u, z, ALU.max).then_inc(s_lf, 1)
                    dve.wait_ge(s_exp, 1)
                    nc.vector.tensor_scalar(w, u, 1.0, None, ALU.add).then_inc(s_exp, 1)
                    dve.wait_ge(s_ln, 1)
                    st.link(nc.vector.tensor_scalar(w, w, -1.0, None, ALU.add))
                    st.link(nc.vector.tensor_scalar(e, w, 0.0, None, ALU.is_equal))
                    st.link(nc.vector.tensor_tensor(w, w, e, ALU.add))
                    st.link(nc.vector.tensor_tensor(lnw, lnw, e, ALU.add))
                    st.link(nc.vector.reciprocal(w, w))
                    st.link(nc.vector.tensor_tensor(u, u, lnw, ALU.mult))
                    st.link(nc.vector.tensor_tensor(u, u, w, ALU.mult))
                    st.link(nc.vector.tensor_scalar(z, z, 0.0, None, ALU.min))
                    nc.vector.tensor_tensor(R["logf"][:, 0:NT * H], z, u, ALU.subtract).then_inc(s_lf, 1)

        @block.gpsimd
        def _(pool):
            for g in range(2):
                pool.wait_ge(s_low, FIRST_HT + 2 * NT)
                nc.gpsimd.tensor_tensor(hT[:, 4 * g:4 * g + 4, :], hT_high[:, 4 * g:4 * g + 4, :].bitcast(F32),
                                        hT_low[g].bitcast(F32),
                                        ALU.add).then_inc(s_pool, 1)
            pool.wait_ge(s_w[W_QB % 4], 16 * (W_QB // 4 + 1))
            pool.wait_ge(*last_use(W_K))
            halves = []
            for g in range(KVH):
                halves.append([wslot(W_QB).rearrange("p k (g i d) -> p k g i d", g=KVH, d=HD)[:, :, g]] +
                              [w.rearrange("p k (i g d) -> p k i g d", g=KVH, d=HD)[:, :, :, g] for w in (w_high, wqb)])
            for src, high, low in halves:
                nc.gpsimd.tensor_copy(high, src).then_inc(s_pool, 1)
            pool.wait_ge(*last_use(W_V))
            for g, (src, high, low) in enumerate(halves):
                pool.wait_ge(s_pool, 2 + g + 1)
                nc.gpsimd.tensor_tensor(low, src, high.bitcast(F32), ALU.subtract).then_inc(s_pool, 1)


def load_mod(eng, mod_d, modp, mods, part, n, s_mod):
    eng.dma_start(modp, mod_d[0:1, part * D:(part + n) * D].to_broadcast([P, n * D])).then_inc(s_mod, 16)
    eng.dma_start(mods, mod_d[1:1 + DB, None, part * D:(part + n) * D].to_broadcast([DB, DN, n * D])).then_inc(s_mod, 16)


def prompt_stage(env):
    nc, a, ps, R, C, sem, S = (env[k] for k in ("nc", "a", "ps", "R", "C", "sem", "S"))
    qT, kT = carve(R["Q"], (4, TOK), (4, TOK))
    qbT, kbT = carve(R["qbT"], (GROUP, TOK)), R["kbT"]
    v, kvb = carve(R["v"], (NT, HW)), carve(R["kvb"], (NT, 2 * KW))
    oaT, obT = carve(R["oaT"], (4, TOK)), carve(R["obT"], (GROUP, TOK))
    logf = carve(R["logf"], (NT, H))
    nfk = R["biasT"][0:H, 0:SEQ]
    prob, probT = carve(R["work"], (3, 512), (2, 512))
    U = 2 * H * PT
    units = [("fox", h, i) for h in range(H) for i in range(PT)] + \
            [("swa", h, i) for h in range(H) for i in range(PT)]
    mx, nm, rs, es, ri, sinks = carve(R["small"], (U,), (U,), (U,), (U,), (U,), (H,))
    s_sink, s_cum, s_nfk = env["s_sinks"], sem("b_cumsum_psum"), sem("b_neg_cumsum")
    s_s, s_nm, s_e, s_es = sem("b_scores"), sem("b_neg_max"), sem("b_exp"), sem("b_exp_sink")
    s_p, s_t, s_pt = sem("b_prob"), sem("b_prob_transposed"), sem("b_probT")
    s_pv, s_o = sem("b_pv"), sem("b_o_out")

    def width(kind, i):
        return (i + 1) * P if kind == "fox" else P * min(i + 1, 2)

    swa_before = [sum(u[0] == "swa" for u in units[:n]) for n in range(U)]

    with nc.Block() as block:
        @block.sync
        def _(sp):
            sp.dma_start(sinks, a["swa_sinks"].to_broadcast([P, H])).then_inc(s_sink, 16)
            for b in range(2):
                for half in range(2):
                    half_cache(sp, env, b, b, half)
            sp.wait_ge(env["s_outputs"], 16 * (4 + NT + 2 * (2 + DB)))

        @block.tensor
        def _(pe):
            for i in range(PT):
                for j in range(i + 1):
                    last = nc.tensor.matmul(ps[0:H, 7, i * P:(i + 1) * P], logf[:, j, :],
                                            C("tri_incl") if j == i else C("ones"), start=(j == 0), stop=(j == i))
            last.then_inc(s_cum, 1)

            def scores(n):
                kind, h, i = units[n]
                if n >= 3:
                    if kind == "swa" or units[n - 3][0] == "fox":
                        pe.wait_ge(s_e, n - 2)
                if n == 0:
                    pe.wait_ge(s_nfk, 1)
                w = width(kind, i)
                out = ps[:, n % 3, 0:w]
                if kind == "fox":
                    part = slice(HD * (h % 2), HD * (h % 2) + HD)
                    nc.tensor.matmul(out, C("ident", H)[:, h:h + 1].to_broadcast([H, P]), nfk[:, 0:w],
                                     start=True, stop=False)
                    ins = nc.tensor.matmul(out, qT[part, h // 2, i * P:(i + 1) * P], kT[part, h // 2, 0:w],
                                           start=False, stop=True)
                else:
                    g = h // GROUP
                    part = slice(HD * g, HD * g + HD)
                    ins = nc.tensor.matmul(out, qbT[part, h % GROUP, i * P:(i + 1) * P],
                                           kbT[part, (i + 1) * P - w:(i + 1) * P], start=True, stop=True)
                ins.then_inc(s_s, 1)

            def turn(n):
                kind, h, i = units[n]
                pe.wait_ge(s_p, n + 1)
                if n >= 2:
                    pe.wait_ge(s_pt, n - 1)
                for j in range(width(kind, i) // P):
                    last = nc.tensor.transpose(ps[:, 3 + n % 2, j * P:(j + 1) * P], prob[:, n % 3, j * P:(j + 1) * P],
                                               C("ident"))
                last.then_inc(s_t, 1)

            def values(n):
                kind, h, i = units[n]
                pe.wait_ge(s_pt, n + 1)
                if n >= 2:
                    pe.wait_ge(s_o, n - 1)
                r = h % 2 if kind == "fox" else h // GROUP
                out = ps[HD * r:HD * r + HD, 5 + n % 2, 0:P]
                nb = width(kind, i) // P
                for j in range(nb):
                    if kind == "fox":
                        lhsT = v[:, j, h * HD:(h + 1) * HD]
                    else:
                        lhsT = kvb[:, i + 1 - nb + j, KW + r * HD:KW + (r + 1) * HD]
                    ins = nc.tensor.matmul(out, lhsT, probT[:, n % 2, j * P:(j + 1) * P],
                                           start=(j == 0), stop=(j == nb - 1))
                ins.then_inc(s_pv, 1)

            for n in range(U + 3):
                if n < U:
                    scores(n)
                if 2 <= n < U + 2:
                    turn(n - 2)
                if n >= 3:
                    values(n - 3)

        @block.vector
        def _(dve):
            st = env["dve_steps"].resume(dve)
            dve.wait_ge(S["cached_logf"], 16)
            clogf = R["logf"][:, NT * H:].rearrange("p (b j h) -> p b j h", b=DB, h=H)
            wst = R["wst"].rearrange("p (j b h) -> p j b h", j=9, h=H)
            st.link(nc.vector.tensor_copy(wst[:, JC], logf[:, PT:PT + 1, :].to_broadcast([P, DB, H])))
            st.link(nc.vector.tensor_copy(wst[:, JC - 2], clogf[:, :, JC - 1, :]))
            for j in range(JC - 3, -1, -1):
                st.link(nc.vector.tensor_tensor(wst[:, j], wst[:, j + 1], clogf[:, :, j + 1, :], ALU.add))
            st.link(nc.vector.tensor_tensor(wst[:, JC - 1], wst[:, 0], clogf[:, :, 0, :], ALU.add))
            dve.wait_ge(s_cum, 1)
            nc.vector.tensor_scalar(nfk, ps[0:H, 7, :], -1.0, None, ALU.mult).then_inc(s_nfk, 1)
            dve.wait_ge(s_sink, 16)

            def maxima(n):
                kind, h, i = units[n]
                w = width(kind, i)
                dve.wait_ge(s_s, n + 1)
                if kind == "fox":
                    own = ps[:, n % 3, w - P:w]
                    st.link(nc.vector.tensor_tensor(own, own, C("causal"), ALU.add))
                    nc.vector.tensor_reduce(nm[:, n:n + 1], ps[:, n % 3, 0:w], AX, ALU.max, negate=True).then_inc(s_nm, 1)
                    return
                slope = 2.0 ** (-8.0 * (h + 1) / H)
                if n >= 3:
                    dve.wait_ge(s_t, n - 2)
                st.link(nc.vector.scalar_tensor_tensor(prob[:, n % 3, 0:w], C("swa_dist")[:, 2 * P - w:], -slope,
                                                       ps[:, n % 3, 0:w], ALU.mult, ALU.add))
                st.link(nc.vector.tensor_reduce(mx[:, n:n + 1], prob[:, n % 3, 0:w], AX, ALU.max))
                nc.vector.tensor_scalar(nm[:, n:n + 1], mx[:, n:n + 1], sinks[:, h:h + 1], -1.0,
                                        ALU.max, ALU.mult).then_inc(s_nm, 1)

            def normalise(n):
                kind, h, i = units[n]
                w = width(kind, i)
                dve.wait_ge(s_e, n + 1)
                if kind == "swa":
                    dve.wait_ge(s_es, swa_before[n] + 1)
                    st.link(nc.vector.tensor_tensor(rs[:, n:n + 1], rs[:, n:n + 1], es[:, n:n + 1], ALU.add))
                st.link(nc.vector.reciprocal(ri[:, n:n + 1], rs[:, n:n + 1]))
                nc.vector.tensor_scalar(prob[:, n % 3, 0:w], prob[:, n % 3, 0:w], ri[:, n:n + 1], None,
                                        ALU.mult).then_inc(s_p, 1)

            def out(n):
                kind, h, i = units[n]
                r = h % 2 if kind == "fox" else h // GROUP
                part = slice(HD * r, HD * r + HD)
                dst = oaT[part, h // 2, :] if kind == "fox" else obT[part, h % GROUP, :]
                dve.wait_ge(s_pv, n + 1)
                nc.vector.tensor_copy(dst[:, i * P:(i + 1) * P], ps[part, 5 + n % 2, 0:P]).then_inc(s_o, 1)

            for n in range(U + 3):
                if n < U:
                    maxima(n)
                if 1 <= n < U + 1:
                    normalise(n - 1)
                if n >= 3:
                    out(n - 3)

        @block.scalar
        def _(act):
            act.wait_ge(s_sink, 16)
            for n in range(U + 2):
                if n < U:
                    kind, h, i = units[n]
                    w = width(kind, i)
                    act.wait_ge(s_nm, n + 1)
                    if kind == "fox" and n >= 3:
                        act.wait_ge(s_t, n - 2)
                    src = ps[:, n % 3, 0:w] if kind == "fox" else prob[:, n % 3, 0:w]
                    nc.scalar.activation(prob[:, n % 3, 0:w], src, ACT.Exp, bias=nm[:, n:n + 1],
                                         accum_out=rs[:, n:n + 1]).then_inc(s_e, 1)
                    if kind == "swa":
                        nc.scalar.activation(es[:, n:n + 1], sinks[:, h:h + 1], ACT.Exp,
                                             bias=nm[:, n:n + 1]).then_inc(s_es, 1)
                if n >= 2:
                    kind, h, i = units[n - 2]
                    act.wait_ge(s_t, n - 1)
                    if n >= 4:
                        act.wait_ge(s_pv, n - 3)
                    w = width(kind, i)
                    nc.scalar.copy(probT[:, n % 2, 0:w], ps[:, 3 + n % 2, 0:w]).then_inc(s_pt, 1)


def sample_stage(env):
    nc, a, ps, R, C, sem, kv = (env[k] for k in ("nc", "a", "ps", "R", "C", "sem", "kv"))
    qT, kT = carve(R["Q"], (4, TOK), (4, TOK))
    qbT, kbT = carve(R["qbT"], (GROUP, TOK)), R["kbT"]
    v, kvb = carve(R["v"], (NT, HW)), carve(R["kvb"], (NT, 2 * KW))
    oaT, obT = carve(R["oaT"], (4, TOK)), carve(R["obT"], (GROUP, TOK))
    wst = R["wst"].rearrange("p (j c) -> p j c", j=9)
    biasT = R["biasT"]
    NKEY = PAST + P
    kc, q_fox, q_swa, pick = carve(R["x"], (4, PAST), (4 * 160,), (P,), (P,))
    prob, probT, om, omb, sb_s, pbT, skT, skv0, skv1 = carve(
        R["work"], (NKEY,), (9, P), (HW,), (KW,), (2 * P,), (2, P), (P,), (2, KW), (2, KW))
    skv = [skv0, skv1]
    ring = [R["ring"][:, s * 4096:(s + 1) * 4096].rearrange("p (j n) -> p j n", j=JC) for s in range(4)]
    nmf, rsf, rif, mxb, nmb, rsb, esb, rib, sink, m3 = carve(R["small"], *[(1,)] * 9, (3,))
    s_sink, s_z, s_bias, s_biasT = env["s_sinks"], sem("c_zeros"), sem("c_bias_psum"), sem("c_bias_rows")
    s_skv = [sem("c_swa_cache_even"), sem("c_swa_cache_odd")]
    s_q = sem("c_queries")
    s_sh = sem("c_score_halves")
    s_s, s_sb, s_nm, s_nmb = sem("c_scores"), sem("c_swa_scores"), sem("c_neg_max"), sem("c_swa_neg_max")
    s_e, s_eb = sem("c_exp"), sem("c_swa_exp")
    s_tr = [sem("c_turned_bank0"), sem("c_turned_bank1")]
    s_fr = [sem("c_copied_by_act"), sem("c_copied_by_dve")]
    s_pv, s_pvb, s_om, s_omb = sem("c_pv"), sem("c_swa_pv"), sem("c_o_masked"), sem("c_swa_o_masked")
    s_f, s_fb, s_oa, s_ob = sem("c_folded"), sem("c_swa_folded"), sem("c_o_out"), sem("c_swa_o_out")
    s_v = sem("c_dve_steps")

    KEYS_FIRST, KEYS_LAST = range(4), range(4, 8)
    ORDER = [8, *KEYS_FIRST, 9, 10, 11, 12, *KEYS_LAST]
    ORDER_LAST = [8, 9, 10, 11, 12]

    class Turn:
        def __init__(self, i, u, r, last):
            j = 13 * u + (ORDER_LAST if last else ORDER).index(r)
            self.bank = j % 2
            self.before = i * 13 + 4 + j // 2

        def enter(self, pe):
            pe.wait_ge(s_fr[self.bank], self.before)

        def ready(self, eng):
            eng.wait_ge(s_tr[self.bank], self.before + 1)

        def copied(self, eng):
            eng.wait_ge(s_fr[self.bank], self.before + 1)

    def copy_out(bank, dst, src):
        ins = nc.scalar.copy(dst, src) if bank == 0 else nc.vector.tensor_copy(dst, src)
        ins.then_inc(s_fr[bank], 1)

    def key_cols(j):
        return kc[:, :, j * P:(j + 1) * P]

    def four(bank):
        return ps[:, bank, :].rearrange("p (c t) -> p c t", t=P)

    def copies(eng, bank, i, u, last, rs):
        for r in rs:
            t = Turn(i, u, r, last)
            if t.bank != bank:
                continue
            t.ready(eng)
            if r < 8:
                copy_out(bank, key_cols(r), four(bank))
            elif r == 8:
                copy_out(bank, skT, ps[:, bank, 0:P])
            elif r < 12:
                n = min(4, 9 - 4 * (r - 9))
                copy_out(bank, probT[:, 4 * (r - 9):4 * (r - 9) + n, :],
                         ps[:, bank, 0:n * P].rearrange("p (c t) -> p c t", t=P))
            else:
                copy_out(bank, pbT, ps[:, bank, 0:2 * P].rearrange("p (c t) -> p c t", t=P))

    def steps(eng, body):
        for u in range(2):
            body(0, u, first=True)
        with eng.Fori(1, DB // 2 - 1) as i:
            for u in range(2):
                body(i, u)
        for u in range(2):
            body(DB // 2 - 1, u, last=(u == 1))

    with nc.Block() as block:
        @block.sync
        def _(sp):
            with nc.allow_non_contiguous_dma(reason="a sink for each of 128 (head, query) rows"):
                sp.dma_start(sink, a["swa_sinks"].rearrange("l h -> (l h)")[:, None, None].to_broadcast([H, DN, 1])
                             ).then_inc(s_sink, 16)

            def small(i, u):
                for half, name in enumerate(("cache_swa_k", "cache_swa_v")):
                    rows = a[name][0].rearrange("b s h d -> b s (h d)")
                    b = 2 * i + u
                    src = rows[b] if isinstance(b, int) else rows[bass.ds(b, 1)].rearrange("a p n -> p (a n)")
                    sp.dma_start(skv[u][:, half, :], src).then_inc(s_skv[u], 16)

            for u in range(2):
                small(0, u)
            with sp.Fori(1, DB // 2) as i:
                for u in range(2):
                    b = 2 * i + u
                    sp.wait_ge(s_s, b - 1)
                    half_cache(sp, env, b, u, 0)
                    sp.wait_ge(s_pvb, b - 1)
                    small(i, u)
                    sp.wait_ge(s_pv, b - 1)
                    half_cache(sp, env, b, u, 1)
            sp.wait_ge(s_s, DB - 1)
            for c in range(2):
                gate_columns(sp, env, c)
            sp.wait_ge(s_pv, DB - 1)
            sp.dma_start(env["wa"], a["w_branch_a"][0].rearrange("(k p) n -> p k n", p=P)).then_inc(env["s_branch"], 16)
            sp.wait_ge(env["s_branch"], 16)
            sp.wait_ge(s_pv, DB)
            for g in range(KVH):
                sp.dma_start(env["wb"][g * HD:(g + 1) * HD], a["w_branch_b"][0].rearrange(
                    "(g i d) n -> g d i n", g=KVH, d=HD)[g]).then_inc(env["s_branch"], 16)

        @block.tensor
        def _(pe):
            for j in range(JC):
                out = ps[0:DB * H, 2 + j // 4, (j % 4) * P:(j % 4 + 1) * P]
                last = nc.tensor.matmul(out, wst[:, JC - 1, :], C("suffix"), start=True, stop=(j == JC - 1))
                if j < JC - 1:
                    last = nc.tensor.matmul(out, wst[:, j, :], C("ident"), start=False, stop=True)
            last = nc.tensor.matmul(ps[0:DB * H, 4, 0:P], wst[:, JC, :], C("same"), start=True, stop=True)
            last.then_inc(s_bias, 1)
            pe.wait_ge(kv[0], 16)
            for r in range(8):
                if r >= 2:
                    pe.wait_ge(s_fr[r % 2], r // 2)
                for c in range(4):
                    last = nc.tensor.transpose(ps[:, r % 2, c * P:(c + 1) * P], ring[0][:, r, c * P:(c + 1) * P],
                                               C("ident"))
                last.then_inc(s_tr[r % 2], 1)
            pe.wait_ge(s_biasT, 1)
            pe.wait_ge(s_z, 4)

            def body(i, u, first=False, last=False):
                b = 2 * i + u
                pe.wait_ge(s_q, b + 1)
                if first and u == 0:
                    for x in range(2):
                        pe.wait_ge(s_fr[x], 4)
                else:
                    for r in (6, 7):
                        prev = Turn(i if u else i - 1, 1 - u, r, False)
                        prev.copied(pe)
                if not (first and u == 0):
                    pe.wait_ge(s_e, b)
                for half in range(2):
                    out, cols = ps[:, 2 + half, :], slice(half * 512, half * 512 + 512)
                    nc.tensor.matmul(out, pick, biasT[:, cols], start=True, stop=False)
                    for c in range(4):
                        ins = nc.tensor.matmul(out, q_fox[:, c * P:(c + 1) * P], kc[:, c, cols], start=False, stop=(c == 3))
                    ins.then_inc(s_sh, 1)
                out = ps[:, 4, 0:P]
                nc.tensor.matmul(out, pick, biasT[:, PAST:NKEY], start=True, stop=False)
                for c in range(4):
                    ins = nc.tensor.matmul(out, q_fox[:, c * P:(c + 1) * P], kT[:, c, SEQ:TOK], start=False, stop=(c == 3))
                ins.then_inc(s_s, 1)
                nu = 1 - u

                def turn_keys(r):
                    t = Turn(i, u, r, False)
                    t.enter(pe)
                    for c in range(4):
                        ins = nc.tensor.transpose(ps[:, t.bank, c * P:(c + 1) * P], ring[nu][:, r, c * P:(c + 1) * P],
                                                  C("ident"))
                    ins.then_inc(s_tr[t.bank], 1)

                t = Turn(i, u, 8, last)
                t.enter(pe)
                pe.wait_ge(s_skv[u], 32 * (i + 1))
                nc.tensor.transpose(ps[:, t.bank, 0:P], skv[u][:, 0, :], C("ident")).then_inc(s_tr[t.bank], 1)
                t.copied(pe)
                if not (first and u == 0):
                    pe.wait_ge(s_nmb, b)
                nc.tensor.matmul(ps[:, 7, 0:P], q_swa, skT, start=True, stop=True)
                nc.tensor.matmul(ps[:, 7, P:2 * P], pick, C("others"), start=True, stop=False)
                nc.tensor.matmul(ps[:, 7, P:2 * P], q_swa, kbT[:, SEQ:TOK], start=False, stop=True).then_inc(s_sb, 1)
                if not last:
                    pe.wait_ge(kv[nu], 16 * ((i + 1) if u == 0 else (i + 2)))
                    for r in KEYS_FIRST:
                        turn_keys(r)
                pe.wait_ge(s_e, b + 1)
                for r in range(9, 12):
                    t = Turn(i, u, r, last)
                    t.enter(pe)
                    for c in range(min(4, 9 - 4 * (r - 9))):
                        k = 4 * (r - 9) + c
                        ins = nc.tensor.transpose(ps[:, t.bank, c * P:(c + 1) * P], prob[:, k * P:(k + 1) * P], C("ident"))
                    ins.then_inc(s_tr[t.bank], 1)
                t = Turn(i, u, 12, last)
                t.enter(pe)
                pe.wait_ge(s_eb, b + 1)
                for c in range(2):
                    ins = nc.tensor.transpose(ps[:, t.bank, c * P:(c + 1) * P], sb_s[:, c * P:(c + 1) * P], C("ident"))
                ins.then_inc(s_tr[t.bank], 1)
                if not (first and u == 0):
                    pe.wait_ge(s_oa, b)
                    pe.wait_ge(s_ob, b)
                for r in (10, 11):
                    Turn(i, u, r, last).copied(pe)
                pe.wait_ge(kv[2 + u], 16 * (i + 1))
                for k in range(9):
                    rhs = ring[2 + u][:, k, :] if k < JC else v[:, PT, :]
                    ins = nc.tensor.matmul(ps[:, 5, :], probT[:, k, :], rhs, start=(k == 0), stop=(k == 8))
                    if not last and k < len(KEYS_LAST):
                        turn_keys(KEYS_LAST[k])
                ins.then_inc(s_pv, 1)
                t.copied(pe)
                nc.tensor.matmul(ps[:, 6, 0:KW], pbT[:, 0, :], skv[u][:, 1, :], start=True, stop=False)
                nc.tensor.matmul(ps[:, 6, 0:KW], pbT[:, 1, :], kvb[:, PT, KW:2 * KW], start=False, stop=True).then_inc(s_pvb, 1)
                pe.wait_ge(s_om, b + 1)
                for c in range(4):
                    ins = nc.tensor.matmul(ps[:, 5, c * DN:(c + 1) * DN], om[:, c * P:(c + 1) * P], C("fold16"),
                                           start=True, stop=True)
                ins.then_inc(s_f, 1)
                pe.wait_ge(s_omb, b + 1)
                nc.tensor.matmul(ps[:, 6, 0:GROUP * DN], omb, C("fold64"), start=True, stop=True).then_inc(s_fb, 1)

            steps(pe, body)

        def at_request(ap, b):
            return ap[:, :, b * DN:(b + 1) * DN] if isinstance(b, int) else ap[:, :, bass.ds(b * DN, DN)]

        @block.vector
        def _(dve):
            st = Steps(dve, s_v)
            nc.vector.memset(q_fox, 0.0).then_inc(s_z, 1)
            nc.vector.memset(q_swa, 0.0).then_inc(s_z, 1)
            nc.vector.memset(pick, 0.0).then_inc(s_z, 1)
            nc.vector.memset(biasT[DB * H:P, :], 0.0).then_inc(s_z, 1)
            dve.wait_ge(s_bias, 1)
            st.link(nc.vector.tensor_copy(biasT[0:DB * H, 0:PAST], ps[0:DB * H, 2:4, :].rearrange("p a b -> p (a b)")))
            nc.vector.tensor_tensor(biasT[0:DB * H, PAST:NKEY], ps[0:DB * H, 4, 0:P], C("others", DB * H),
                                    ALU.add).then_inc(s_biasT, 1)
            dve.wait_ge(s_z, 4)

            def queries(b):
                diag = q_fox.rearrange("p (c w) -> p c w", w=160)
                for r in range(2):
                    part = slice(HD * r, HD * r + HD)
                    nc.vector.tensor_copy(diag[part, :, r * DN:(r + 1) * DN], at_request(qT[part, :, SEQ:TOK], b))
                    nc.vector.tensor_copy(q_swa[part, r * GROUP * DN:(r + 1) * GROUP * DN].rearrange("p (i n) -> p i n", n=DN),
                                          at_request(qbT[part, :, SEQ:TOK], b))
                heads = C("ident", DB * H)
                heads = heads[:, b * H:(b + 1) * H] if isinstance(b, int) else heads[:, bass.ds(b * H, H)]
                nc.vector.tensor_copy(pick[0:DB * H, :].rearrange("p (h n) -> p h n", n=DN),
                                      heads.unsqueeze(2).to_broadcast([DB * H, H, DN])).then_inc(s_q, 1)

            queries(0)
            for r in range(1, 8, 2):
                dve.wait_ge(s_tr[1], r // 2 + 1)
                copy_out(1, key_cols(r), four(1))

            def body(i, u, first=False, last=False):
                b = 2 * i + u

                def per_request(ap):
                    return ap.rearrange("p (b n) -> p b n", n=DN)

                def all_requests(name):
                    return C(name).unsqueeze(1).to_broadcast([P, DB, DN])

                for half in range(2):
                    dve.wait_ge(s_sh, 2 * b + half + 1)
                    nc.vector.tensor_reduce(m3[:, half:half + 1], ps[:, 2 + half, :], AX, ALU.max)
                dve.wait_ge(s_s, b + 1)
                st.link(nc.vector.tensor_tensor(per_request(ps[:, 4, 0:P]), per_request(ps[:, 4, 0:P]),
                                                all_requests("fox_new"), ALU.add))
                st.link(nc.vector.tensor_reduce(m3[:, 2:3], ps[:, 4, 0:P], AX, ALU.max))
                nc.vector.tensor_reduce(nmf, m3, AX, ALU.max, negate=True).then_inc(s_nm, 1)
                copies(dve, 1, i, u, last, [8])
                if not last:
                    copies(dve, 1, i, u, last, KEYS_FIRST)
                dve.wait_ge(s_sb, b + 1)
                st.link(nc.vector.tensor_tensor(sb_s[:, 0:P], ps[:, 7, 0:P], C("swa_old"), ALU.add))
                st.link(nc.vector.tensor_tensor(per_request(sb_s[:, P:2 * P]), per_request(ps[:, 7, P:2 * P]),
                                                all_requests("swa_new"), ALU.add))
                st.link(nc.vector.tensor_reduce(mxb, sb_s, AX, ALU.max))
                nc.vector.tensor_scalar(nmb, mxb, sink, -1.0, ALU.max, ALU.mult).then_inc(s_nmb, 1)
                if not last:
                    queries(b + 1)
                dve.wait_ge(s_e, b + 1)
                st.link(nc.vector.reciprocal(rif, rsf))
                copies(dve, 1, i, u, last, range(9, 12))
                dve.wait_ge(s_eb, b + 1)
                st.link(nc.vector.tensor_tensor(rsb, rsb, esb, ALU.add))
                st.link(nc.vector.reciprocal(rib, rsb))
                copies(dve, 1, i, u, last, [12])
                if not last:
                    copies(dve, 1, i, u, last, KEYS_LAST)
                dve.wait_ge(s_pv, b + 1)
                nc.vector.scalar_tensor_tensor(om, ps[:, 5, :], rif, C("headmask"), ALU.mult, ALU.mult).then_inc(s_om, 1)
                dve.wait_ge(s_pvb, b + 1)
                nc.vector.scalar_tensor_tensor(omb, ps[:, 6, 0:KW], rib, C("groupmask"), ALU.mult, ALU.mult).then_inc(s_omb, 1)
                dve.wait_ge(s_fb, b + 1)
                nc.vector.tensor_copy(at_request(obT[:, :, SEQ:TOK], b),
                                      ps[:, 6, 0:GROUP * DN].rearrange("p (i n) -> p i n", n=DN)).then_inc(s_ob, 1)

            base, per = st.n, 8

            def counted(i, u, first=False, last=False):
                st.loop((2 * i + u) * per + base)
                body(i, u, first, last)
                assert st.n == per

            dve.wait_ge(s_sink, 32)
            steps(dve, counted)

        @block.scalar
        def _(act):
            for r in range(0, 8, 2):
                act.wait_ge(s_tr[0], r // 2 + 1)
                copy_out(0, key_cols(r), four(0))
            act.wait_ge(s_sink, 32)

            def body(i, u, first=False, last=False):
                b = 2 * i + u
                copies(act, 0, i, u, last, [8])
                if not last:
                    act.wait_ge(s_s, b + 1)
                    copies(act, 0, i, u, last, KEYS_FIRST)
                act.wait_ge(s_nm, b + 1)
                nc.scalar.activation(prob, ps[:, 2:5, :].rearrange("p a b -> p (a b)")[:, 0:NKEY], ACT.Exp,
                                     bias=nmf, accum_out=rsf).then_inc(s_e, 1)
                act.wait_ge(s_nmb, b + 1)
                nc.scalar.activation(esb, sink, ACT.Exp, bias=nmb)
                nc.scalar.activation(sb_s, sb_s, ACT.Exp, bias=nmb, accum_out=rsb).then_inc(s_eb, 1)
                copies(act, 0, i, u, last, range(9, 13))
                if not last:
                    copies(act, 0, i, u, last, KEYS_LAST)
                act.wait_ge(s_f, b + 1)
                nc.scalar.copy(at_request(oaT[:, :, SEQ:TOK], b),
                               ps[:, 5, 0:4 * DN].rearrange("p (i n) -> p i n", n=DN)).then_inc(s_oa, 1)

            steps(act, body)


def half_cache(eng, env, b, u, half):
    a, R, kv = env["a"], env["R"], env["kv"]
    rows = a[("cache_fox_k", "cache_fox_v")[half]][0].rearrange("b (p j) h d -> b p (j h d)", j=JC)
    slot = 2 * half + u
    src = rows[b] if isinstance(b, int) else rows[bass.ds(b, 1)].rearrange("a p n -> p (a n)")
    eng.dma_start(R["ring"][:, slot * 4096:(slot + 1) * 4096], src).then_inc(kv[slot], 16)


def gate_columns(eng, env, c):
    w_in = env["a"]["w_in"][0].rearrange("(k p) n -> p k n", p=P)
    for h, o0 in enumerate((O_GA, O_GB)):
        eng.dma_start(env["sub"][2 * (c % 4) + h], w_in[:, :, o0 + c * P:o0 + (c + 1) * P]).then_inc(env["s_sub"][c % 4], 16)


def mix_stage(env):
    nc, a, ps, R, C, sem = (env[k] for k in ("nc", "a", "ps", "R", "C", "sem"))
    mod_d, h2_d, acc_d, tab_d = env["mod_d"], env["h2_d"], env["acc_d"], env["tab_d"]
    hT = carve(R["hT"], (KC, TOK))
    h2row = carve(R["hT"], (NT, D))
    oaT, obT = carve(R["oaT"], (4, TOK)), carve(R["obT"], (GROUP, TOK))
    mixT = carve(R["Q"], (KC, TOK))
    x = carve(R["x"], (NT, D))
    ring = R["ring"]
    sub, wa, wb = env["sub"], env["wa"], env["wb"]
    wo = [carve(ring[:, s * 4096:(s + 1) * 4096], (KC, 512)) for s in range(2)]
    h2T = carve(ring[:, 8192:], (KC, TOK))
    wsg = carve(ring[:, 0:4096], (2, KC, FE))
    wsd = carve(ring[:, 4096:6144], (2, D))
    sgate, prod = carve(R["work"], (2 * 2, TOK), (2, TOK))
    RR = env["RR"]
    hT_high, hT_low = carve(RR["x"], (KC, TOK)), carve(RR["hT"], (KC, TOK))
    w_high = [carve(RR[name][:, 0:2 * D], (2, KC, P)) for name in ("qbT", "v")]
    sub_low = [carve(RR["ring"][:, s * D:(s + 1) * D], (KC, P)) for s in range(8)]
    gate1 = carve(R["v"], (2, D))
    shift2 = [R["work"][:, 0:D], R["work"][:, 2 * D:3 * D]]
    scale2 = [R["work"][:, D:2 * D], R["work"][:, 3 * D:4 * D]]
    wr, br = carve(R["biasT"], (KC, NE), (NE,))
    tmpx = carve(R["obT"], (2, 512))
    tmpr = carve(R["oaT"], (2, D))
    stat, sums = carve(R["small"], (NT,), (2 * NT,))
    squares = R["qbT"][:, 2 * D:2 * D + 512]
    hs, hTs, sgs = (carve(R["wst"], (2, FE)), carve(R["kbT"], (2, FE)), carve(R["kvb"][:, 768:], (2, FE)))
    ysb = carve(R["v"], (2, D))
    sc, sel, gt, chosen, dest, selm, left = carve(R["oaT"], *[(NT, NE)] * 7)
    nblk, pend, pst = carve(R["kvb"], (NE,), (NE,), (NE,))
    gs, rank, top8, idxf, destk, gk = carve(
        R["obT"][:, D:], (NT, NG), (NT, NG), (NT, 8), (NT, TOPK), (NT, TOPK), (NT, TOPK))
    top2, above, ties, picked, scT, earlier = carve(
        R["Q"], (NT * NG, 8), (NT * NG, NG), (NT * NG, NG), (2 * 2 * TOPK, NE), (TOK,), (NT + 1, NE))
    junk, den, blk, one = carve(R["obT"][:, D + 512:], (NE,), (NT,), (1,), (1,))
    idx8 = R["obT"][:, D + 600:D + 640].bitcast(U32).rearrange("p (t k) -> p t k", k=TOPK)
    slot_no = R["obT"][:, D + 640:D + 680].bitcast(U32).rearrange("p (t k) -> p t k", k=TOPK)
    entry = R["obT"][:, D + 680:D + 760].rearrange("p (t k w) -> p t k w", k=TOPK, w=2)
    entry_u = R["obT"][:, D + 680:D + 760].bitcast(U32).rearrange("p (t k w) -> p t k w", k=TOPK, w=2)
    zero_rows = R["kvb"][:, 256:768]
    counts = env["counts"]

    s_wb = env["s_branch"]
    s_sub = env["s_sub"]
    s_wo = [sem("d_w_out0"), sem("d_w_out1")]
    s_x, s_wr, s_mod, s_wsg, s_wsd = sem("d_x_and_gate1"), sem("d_router_and_gate2"), sem("d_mod2"), sem("d_w_sh_gu"), sem("d_w_sh_down")
    s_high, s_low = sem("d_high_parts"), sem("d_low_parts")

    def split_no(c, r):
        return 2 * c + r + 1 + (KC if c else 0)

    s_mm, s_sig, s_mul, s_mix = sem("d_branch_psum"), sem("d_sigmoid"), sem("d_gated"), sem("d_mixed")
    s_out, s_x1, s_sq, s_var, s_rt = sem("d_out_psum"), sem("d_x1"), sem("d_sumsq"), sem("d_variance"), sem("d_root")
    s_h2, s_h2d = sem("d_h2_rows"), sem("d_h2_stored")
    s_t, s_ta, s_tv = sem("d_turned"), sem("d_h2T_by_act"), sem("d_h2T_by_dve")
    s_lg, s_sc, s_m, s_pos = sem("d_logits"), sem("d_scores"), sem("d_chosen"), sem("d_positions")
    s_gu, s_sg, s_hs, s_ht, s_hc = sem("d_sh_gu"), sem("d_sh_sigmoid"), sem("d_sh_hidden"), sem("d_sh_turned"), sem("d_sh_hT")
    s_y, s_ye, s_yd = sem("d_sh_y"), sem("d_sh_y_rows"), [sem("d_sh_stored0"), sem("d_sh_stored1")]
    s_blk, s_bt = sem("d_block_column"), sem("d_block_row")
    s_sp, s_tab, s_ent, s_scat = sem("d_spare_zeros"), sem("d_table_init"), sem("d_entries"), sem("d_scattered")
    s_tl = sem("d_table_loaded")

    with nc.Block() as block:
        @block.sync
        def _(sp):
            for c in range(2, 4):
                gate_columns(sp, env, c)
            for c in range(4, KC):
                sp.wait_ge(s_mm, 4 * (c - 4) + 4)
                gate_columns(sp, env, c)
            w_out = a["w_out"][0].rearrange("(k p) n -> p k n", p=P)
            sp.wait_ge(s_mm, 4 * 5 + 4)
            sp.dma_start(wo[0], w_out[:, :, 0:512]).then_inc(s_wo[0], 16)
            sp.wait_ge(s_mm, 4 * 7 + 4)
            sp.dma_start(wo[1], w_out[:, :, 512:D]).then_inc(s_wo[1], 16)
            sp.wait_ge(s_mix, KC)
            load_mod(sp, mod_d, R["work"][:, 0:2 * D], R["work"][:, 2 * D:4 * D], 3, 2, s_mod)
            sp.dma_start(tab_d, a["empty_table"]).then_inc(s_tab, 16)
            sp.wait_ge(s_out, NT)
            for h, name in enumerate(("w_sh_gate", "w_sh_up")):
                sp.dma_start(wsg[:, h], a[name][0].rearrange("(p k) f -> p k f", k=KC)).then_inc(s_wsg, 16)
            sp.wait_ge(s_out, 2 * NT)
            sp.dma_start(wsd, a["w_sh_down"][0].rearrange("(p j) n -> p j n", j=2)).then_inc(s_wsd, 16)
            for t in range(NT):
                sp.wait_ge(s_h2, t + 1)
                sp.dma_start(h2_d[t * P:(t + 1) * P, :], h2row[:, t, :]).then_inc(s_h2d, 16)
            sp.wait_ge(s_sp, 1)
            for half in range(2):
                sp.dma_start(acc_d[TOK:TOK + P, half * 512:(half + 1) * 512], zero_rows).then_inc(s_h2d, 16)
            for t in range(NT):
                if t == 2:
                    sp.wait_ge(s_h2d, 16 * (NT + 2))
                    sp.wait_ge(s_sc, 3)
                    sp.wait_ge(s_gu, NT)
                    for u in range(2):
                        e = sp.value_load(counts[0:1, 1 + u:2 + u], min_val=0, max_val=NE - 1)
                        load_gate_up(sp, env, u, e)
                        load_down(sp, env, u, e)
                sp.wait_ge(s_ye, 2 * t + 2)
                sp.dma_start(acc_d[t * P:(t + 1) * P, :], ysb[:, t % 2, :]).then_inc(s_yd[t % 2], 16)
            sp.wait_ge(s_yd[0], 48)
            sp.wait_ge(s_yd[1], 32)
            sp.wait_ge(s_h2d, 16 * (NT + 2))

        @block.tensor
        def _(pe):
            for c in range(KC):
                for r in range(4):
                    if c == 0 and r < 2:
                        pe.wait_ge(s_wb, 48 if r else 16)
                    if c >= 1:
                        if r < 2:
                            pe.wait_ge(s_mul, 2 * (c - 1) + r + 1)
                        else:
                            pe.wait_ge(s_sig, 2 * (c - 1) + r - 1)
                    if r >= 2:
                        pe.wait_ge(s_low, split_no(c, r - 2))
                    for half in range(2):
                        out, cols = ps[:, 2 * r + half, 0:HALF], slice(half * HALF, (half + 1) * HALF)
                        if r < 2:
                            for k in range(4):
                                lhsT, rhs = ((wa[:, k, c * P:(c + 1) * P], oaT[:, k, cols]),
                                             (wb[:, k, c * P:(c + 1) * P], obT[:, k, cols]))[r]
                                last = nc.tensor.matmul(out, lhsT, rhs, start=(k == 0), stop=(k == 3))
                            continue
                        high, low = w_high[c % 2][:, r - 2], sub_low[2 * (c % 4) + r - 2]
                        for k in range(KC):
                            if c == 0 and r == 2 and half == 0:
                                pe.wait_ge(s_low, 2 + k + 1)
                            last = split_product(nc, out, [((high[:, k, :], low[:, k, :]),
                                                            (hT_high[:, k, cols], hT_low[:, k, cols]))], k == 0, k == KC - 1)
                    last.then_inc(s_mm, 1)
            pe.wait_ge(s_mul, 2 * KC - 1)

            def turn(t):
                pe.wait_ge(s_h2, t + 1)
                for g in range(2):
                    n = 2 * t + g
                    if n >= 2:
                        pe.wait_ge(s_ta if g == 0 else s_tv, t)
                    for k in range(4):
                        last = nc.tensor.transpose(ps[:, 4 + g, k * P:(k + 1) * P],
                                                   h2row[:, t, (4 * g + k) * P:(4 * g + k + 1) * P], C("ident"))
                    last.then_inc(s_t, 1)

            for n in range(2 * NT):
                half, t = n // NT, n % NT
                if t == 0:
                    pe.wait_ge(s_wo[half], 16)
                if n >= 4:
                    pe.wait_ge(s_x1, n - 3)
                for k in range(KC):
                    if n == 0:
                        pe.wait_ge(s_mix, k + 1)
                    last = nc.tensor.matmul(ps[:, n % 4, :], mixT[:, k, t * P:(t + 1) * P], wo[half][:, k, :],
                                            start=(k == 0), stop=(k == KC - 1))
                last.then_inc(s_out, 1)
                if half == 1 and t >= 1:
                    turn(t - 1)
            pe.wait_ge(s_wr, 64)
            pe.wait_ge(s_ta, NT - 1)
            pe.wait_ge(s_tv, NT - 1)
            for k in range(KC):
                last = nc.tensor.matmul(ps[0:NE, 6, 0:SEQ], wr[:, k, :], h2T[:, k, 0:SEQ], start=(k == 0), stop=(k == KC - 1))
            last.then_inc(s_lg, 1)
            turn(NT - 1)
            pe.wait_ge(s_ta, NT)
            pe.wait_ge(s_tv, NT)
            for k in range(KC):
                last = nc.tensor.matmul(ps[0:NE, 7, 0:P], wr[:, k, :], h2T[:, k, SEQ:TOK], start=(k == 0), stop=(k == KC - 1))
            last.then_inc(s_lg, 1)
            pe.wait_ge(s_sc, 2)
            for t in range(NT):
                last = nc.tensor.transpose(ps[:, 5, t * NE:(t + 1) * NE], scT[0:NE, t * P:(t + 1) * P],
                                           C("ident", NE)[:, 0:NE])
            last.then_inc(s_t, 1)
            pe.wait_ge(s_x1, 2 * NT)
            pe.wait_ge(s_wsg, 32)
            for t in range(NT):
                if t == 2:
                    pe.wait_ge(s_m, 1)
                    nc.tensor.matmul(ps[:, 7, 0:(NT + 1) * NE], C("ones"), earlier.rearrange("p t e -> p (t e)"),
                                     start=True, stop=False)
                    nc.tensor.matmul(ps[:, 7, 0:NT * NE], C("tri_strict"), chosen.rearrange("p t e -> p (t e)"),
                                     start=False, stop=True).then_inc(s_pos, 1)
                for k in range(KC):
                    last = nc.tensor.matmul(ps[:, t, :], h2T[:, k, t * P:(t + 1) * P], wsg[:, :, k, :],
                                            start=(k == 0), stop=(k == KC - 1))
                last.then_inc(s_gu, 1)
            for t in range(NT):
                pe.wait_ge(s_hs, t + 1)
                if t >= 2:
                    pe.wait_ge(s_hc, t - 1)
                if t == 3:
                    pe.wait_ge(s_sc, 3)
                for j in range(2):
                    last = nc.tensor.transpose(ps[:, 5 + t % 2, j * P:(j + 1) * P], hs[:, t % 2, j * P:(j + 1) * P],
                                               C("ident"))
                last.then_inc(s_ht, 1)
                pe.wait_ge(s_hc, t + 1)
                pe.wait_ge(s_wsd, 16)
                for half in range(2):
                    n = 2 * t + half
                    if n < 4:
                        pe.wait_ge(s_hs, n + 1)
                    else:
                        pe.wait_ge(s_ye, n - 3)
                    for j in range(2):
                        last = nc.tensor.matmul(ps[:, n % 4, :], hTs[:, t % 2, j * P:(j + 1) * P],
                                                wsd[:, j, half * 512:(half + 1) * 512], start=(j == 0), stop=(j == 1))
                    last.then_inc(s_y, 1)
                if t == 1:
                    pe.wait_ge(s_blk, 1)
                    nc.tensor.matmul(ps[0:1, 6, 384:512], blk, C("ident"), start=True, stop=True).then_inc(s_bt, 1)

        @block.scalar
        def _(act):
            act.dma_start(wr, a["w_router"][0].rearrange("(p k) n -> p k n", k=KC)).then_inc(s_wr, 16)
            act.dma_start(br, a["router_bias"].to_broadcast([P, NE])).then_inc(s_wr, 16)

            def weights_high(c):
                act.wait_ge(s_sub[c % 4], 32 * (c // 4 + 1))
                if c >= 2:
                    act.wait_ge(s_mm, 4 * (c - 2) + 4)
                for r in range(2):
                    nc.scalar.copy(w_high[c % 2][:, r], sub[2 * (c % 4) + r]).then_inc(s_high, 1)

            weights_high(0)
            for k in range(KC):
                nc.scalar.copy(hT_high[:, k, :], hT[:, k, :]).then_inc(s_high, 1)
            for c in range(KC):
                if c + 1 < KC:
                    weights_high(c + 1)
                if c >= 2:
                    act.wait_ge(s_mul, 2 * (c - 1))
                for r in range(2):
                    act.wait_ge(s_mm, 4 * c + r + 3)
                    nc.scalar.activation(sgate[:, 2 * (c % 2) + r, :].rearrange("p (h t) -> p h t", t=HALF),
                                         ps[:, 4 + 2 * r:6 + 2 * r, 0:HALF], ACT.Sigmoid).then_inc(s_sig, 1)
            act.dma_start(gate1[:, 0, :], mod_d[0:1, 2 * D:3 * D].to_broadcast([P, D])).then_inc(s_x, 16)
            act.dma_start(x[:, 0:PT, :], a["x_prompt"][0].rearrange("(t p) d -> p t d", p=P)).then_inc(s_x, 16)
            act.dma_start(gate1[:, 1, :], mod_d[1:1 + DB, None, 2 * D:3 * D].to_broadcast([DB, DN, D])).then_inc(s_x, 16)
            act.dma_start(x[:, PT, :], a["x_sample"].rearrange("b n d -> (b n) d")).then_inc(s_x, 16)
            gate2 = carve(R["qbT"], (2, D))
            act.dma_start(gate2[:, 0, :], mod_d[0:1, 5 * D:6 * D].to_broadcast([P, D])).then_inc(s_wr, 16)
            act.dma_start(gate2[:, 1, :], mod_d[1:1 + DB, None, 5 * D:6 * D].to_broadcast([DB, DN, D])).then_inc(s_wr, 16)

            def turned(t):
                act.wait_ge(s_t, 2 * t + 1)
                nc.scalar.copy(h2T[:, 0:4, t * P:(t + 1) * P], ps[:, 4, :].rearrange("p (k t) -> p k t", t=P)).then_inc(s_ta, 1)

            for t in range(NT):
                act.wait_ge(s_x1, NT + t + 1)
                for half in range(2):
                    if 2 * t + half:
                        act.wait_ge(s_sq, 2 * t + half)
                    nc.scalar.activation(squares, x[:, t, half * 512:(half + 1) * 512], ACT.Square,
                                         accum_out=sums[:, 2 * t + half:2 * t + half + 1]).then_inc(s_sq, 1)
                if t >= 1:
                    turned(t - 1)
                act.wait_ge(s_var, t + 1)
                nc.scalar.activation(stat[:, t:t + 1], stat[:, t:t + 1], ACT.Sqrt).then_inc(s_rt, 1)
            turned(NT - 1)
            act.wait_ge(s_lg, 1)
            nc.scalar.activation(scT[0:NE, 0:SEQ], ps[0:NE, 6, 0:SEQ], ACT.Sigmoid).then_inc(s_sc, 1)
            act.wait_ge(s_lg, 2)
            nc.scalar.activation(scT[0:NE, SEQ:TOK], ps[0:NE, 7, 0:P], ACT.Sigmoid).then_inc(s_sc, 1)

            def sigmoid(t):
                act.wait_ge(s_gu, t + 1)
                if t >= 2:
                    act.wait_ge(s_hs, t - 1)
                nc.scalar.activation(sgs[:, t % 2, :], ps[:, t, 0:FE], ACT.Sigmoid).then_inc(s_sg, 1)

            def hidden(t):
                act.wait_ge(s_ht, t + 1)
                nc.scalar.copy(hTs[:, t % 2, :], ps[:, 5 + t % 2, 0:FE]).then_inc(s_hc, 1)

            def rows(t):
                for half in range(2):
                    n = 2 * t + half
                    act.wait_ge(s_y, n + 1)
                    if t >= 2 and half == 0:
                        act.wait_ge(s_yd[t % 2], 16 * (t // 2))
                    nc.scalar.copy(ysb[:, t % 2, half * 512:(half + 1) * 512], ps[:, n % 4, :]).then_inc(s_ye, 1)

            for t in range(2):
                sigmoid(t)
            for t in range(NT):
                if t + 2 < NT:
                    sigmoid(t + 2)
                hidden(t)
                rows(t)
                if t == 1:
                    act.wait_ge(s_bt, 1)
                    nc.scalar.copy(counts[0:1, 1:1 + P], ps[0:1, 6, 384:512]).then_inc(s_sc, 1)

        @block.vector
        def _(dve):
            st = env["dve_steps"].resume(dve)
            nc.vector.memset(zero_rows, 0.0).then_inc(s_sp, 1)

            def split(raw, high, low, count):
                dve.wait_ge(s_high, count)
                nc.vector.tensor_tensor(low, raw, high.bitcast(F32), ALU.subtract).then_inc(s_low, 1)

            def weights_low(c):
                for r in range(2):
                    split(sub[2 * (c % 4) + r], w_high[c % 2][:, r], sub_low[2 * (c % 4) + r], split_no(c, r))

            weights_low(0)
            for k in range(KC):
                split(hT[:, k, :], hT_high[:, k, :], hT_low[:, k, :], 2 + k + 1)
            for c in range(KC):
                u = c % 2
                if c + 1 < KC:
                    weights_low(c + 1)
                if c >= 2:
                    dve.wait_ge(s_mix, c - 1)
                for r in range(2):
                    out = mixT[:, c, :] if r == 0 else prod[:, u, :]
                    dve.wait_ge(s_mm, 4 * c + r + 1)
                    dve.wait_ge(s_sig, 2 * c + r + 1)
                    nc.vector.tensor_tensor(out.rearrange("p (h t) -> p h t", t=HALF),
                                            sgate[:, 2 * u + r, :].rearrange("p (h t) -> p h t", t=HALF),
                                            ps[:, 2 * r:2 * r + 2, 0:HALF], ALU.mult).then_inc(s_mul, 1)
            dve.wait_ge(s_x, 64)

            def turned(t):
                dve.wait_ge(s_t, 2 * t + 2)
                nc.vector.tensor_copy(h2T[:, 4:8, t * P:(t + 1) * P], ps[:, 5, :].rearrange("p (k t) -> p k t", t=P)).then_inc(s_tv, 1)

            for n in range(2 * NT):
                half, t = n // NT, n % NT
                cols = slice(half * 512, half * 512 + 512)
                dve.wait_ge(s_out, n + 1)
                w = int(t == PT)
                st.link(nc.vector.tensor_tensor(tmpx[:, n % 2, :], ps[:, n % 4, :], gate1[:, w, cols], ALU.mult))
                nc.vector.tensor_tensor(x[:, t, cols], x[:, t, cols], tmpx[:, n % 2, :], ALU.add).then_inc(s_x1, 1)
                if half == 0:
                    continue
                if t == 0:
                    dve.wait_ge(s_mod, 32)
                if t >= 1:
                    turned(t - 1)
                dve.wait_ge(s_sq, 2 * t + 2)
                st.link(nc.vector.tensor_tensor(stat[:, t:t + 1], sums[:, 2 * t:2 * t + 1],
                                                sums[:, 2 * t + 1:2 * t + 2], ALU.add))
                nc.vector.tensor_scalar(stat[:, t:t + 1], stat[:, t:t + 1], 1.0 / D, EPS, ALU.mult, ALU.add).then_inc(s_var, 1)
                dve.wait_ge(s_rt, t + 1)
                st.link(nc.vector.reciprocal(stat[:, t:t + 1], stat[:, t:t + 1]))
                st.link(nc.vector.scalar_tensor_tensor(tmpr[:, t % 2, :], x[:, t, :], stat[:, t:t + 1], scale2[w],
                                                       ALU.mult, ALU.mult))
                nc.vector.tensor_tensor(h2row[:, t, :].rearrange("q (k p) -> q p k", k=KC),
                                        tmpr[:, t % 2, :].rearrange("q (p k) -> q p k", k=KC),
                                        shift2[w].rearrange("q (p k) -> q p k", k=KC), ALU.add).then_inc(s_h2, 1)
            turned(NT - 1)

            for u in range(2):
                nc.vector.memset(ring[:, 14336 + u * D:14336 + (u + 1) * D], 0.0).then_inc(env["s_zeros"], 1)

            link = st.link
            nc.vector.memset(earlier[:, 0, :], 0.0)
            dve.wait_ge(s_t, 2 * NT + 1)
            dve.wait_ge(s_wr, 64)
            link(nc.vector.tensor_copy(sc, ps[:, 5, 0:NT * NE].rearrange("p (t e) -> p t e", e=NE)))
            link(nc.vector.tensor_tensor(sel, sc, br.unsqueeze(1).to_broadcast([P, NT, NE]), ALU.add))
            for t in range(NT):
                for g in range(NG):
                    last = nc.vector.max(top2[:, t * NG + g, :], sel[:, t, g * 8:(g + 1) * 8])
            link(last)
            flat = gs.rearrange("p t g -> p (t g)")
            link(nc.vector.tensor_tensor(flat, top2[:, :, 0], top2[:, :, 1], ALU.add))
            for t in range(NT):
                mine = gs[:, t, :].unsqueeze(2).to_broadcast([P, NG, NG])
                other = gs[:, t, :].unsqueeze(1).to_broadcast([P, NG, NG])
                nc.vector.tensor_tensor(above[:, t * NG:(t + 1) * NG, :], other, mine, ALU.is_gt)
                last = nc.vector.tensor_tensor(ties[:, t * NG:(t + 1) * NG, :], other, mine, ALU.is_equal)
            link(last)
            for t in range(NT):
                last = nc.vector.tensor_tensor(ties[:, t * NG:(t + 1) * NG, :], ties[:, t * NG:(t + 1) * NG, :],
                                               C("ties").rearrange("p (g j) -> p g j", j=NG), ALU.mult)
            link(last)
            link(nc.vector.tensor_tensor(above, above, ties, ALU.add))
            link(nc.vector.tensor_reduce(rank.rearrange("p t g -> p (t g)"), above, AX, ALU.add))
            link(nc.vector.tensor_scalar(gs, rank, float(TOPG), None, ALU.is_lt))
            link(nc.vector.tensor_scalar(rank, gs, -NEG, NEG, ALU.mult, ALU.add))
            by_group = selm.rearrange("p t (g j) -> p (t g) j", j=8)
            link(nc.vector.tensor_tensor(by_group, sel.rearrange("p t (g j) -> p (t g) j", j=8),
                                         flat.unsqueeze(2).to_broadcast([P, NT * NG, 8]), ALU.mult))
            link(nc.vector.tensor_tensor(by_group, by_group, rank.rearrange("p t g -> p (t g)").unsqueeze(2).to_broadcast(
                [P, NT * NG, 8]), ALU.add))
            for t in range(NT):
                last = nc.vector.max(top8[:, t, :], selm[:, t, :])
            link(last)
            for t in range(NT):
                last = nc.vector.match_replace(left[:, t, :], top8[:, t, :], selm[:, t, :], -3e38)
            link(last)
            link(nc.vector.tensor_scalar(chosen, left, -2e38, None, ALU.is_lt))
            for t in range(NT):
                ins = nc.vector.tensor_tensor(earlier[:, t + 1, :], earlier[:, t, :], chosen[:, t, :], ALU.add)
                if t + 1 < NT:
                    link(ins)
            ins.then_inc(s_m, 1)
            for t in range(NT):
                last = nc.vector.max_index(idx8[:, t, :], top8[:, t, :], selm[:, t, :])
            link(last)
            dve.wait_ge(s_m, 1)

            def hidden(t):
                dve.wait_ge(s_sg, t + 1)
                if t >= 2:
                    dve.wait_ge(s_ht, t - 1)
                link(nc.vector.tensor_tensor(sgs[:, t % 2, :], sgs[:, t % 2, :], ps[:, t, 0:FE], ALU.mult))
                nc.vector.tensor_tensor(hs[:, t % 2, :].rearrange("q (j p) -> q p j", j=2),
                                        sgs[:, t % 2, :].rearrange("q (p j) -> q p j", j=2),
                                        ps[:, t, FE:2 * FE].rearrange("q (p j) -> q p j", j=2), ALU.mult).then_inc(s_hs, 1)

            for t in range(2):
                hidden(t)
            link(nc.vector.tensor_tensor(gt, sc, chosen, ALU.mult))
            link(nc.vector.tensor_reduce(den, gt, AX, ALU.add))
            link(nc.vector.reciprocal(den, den))
            link(nc.vector.tensor_scalar(den, den, ROUTED_SCALE, None, ALU.mult))
            link(nc.vector.tensor_tensor(gt, gt, den.unsqueeze(2).to_broadcast([P, NT, NE]), ALU.mult))
            link(nc.vector.tensor_copy(idxf, idx8))
            dve.wait_ge(s_pos, 1)
            pos = ps[:, 7, 0:NT * NE].rearrange("p (t e) -> p t e", e=NE)
            cnt = ps[:, 7, NT * NE:(NT + 1) * NE]
            link(nc.vector.tensor_scalar(nblk, cnt, 0.0, None, ALU.is_gt))
            for j in range(1, NT):
                link(nc.vector.scalar_tensor_tensor(nblk, cnt, float(j * P), nblk, ALU.is_gt, ALU.add))
            link(nc.vector.memset(junk, 0.0))
            link(nc.vector.tensor_tensor_scan(pend, nblk, junk, 0.0, ALU.add, ALU.add))
            link(nc.vector.tensor_tensor(pst, pend, nblk, ALU.subtract))
            link(nc.vector.tensor_scalar(junk, pend, C("pcol"), 0.0, ALU.is_le, ALU.add, accum_out=blk))
            nc.vector.tensor_scalar(blk, blk, float(NE - 1), None, ALU.min).then_inc(s_blk, 1)
            dve.wait_ge(s_blk, 1)
            link(nc.vector.tensor_scalar(left[0:1, 0, 0:PAIRS], C("pairs2", 1), pend[0:1, NE - 1:NE], 0.0, ALU.is_lt,
                                         ALU.add, accum_out=one[0:1, :]))
            nc.vector.tensor_copy(counts[0:1, 0:1], one[0:1, :])
            link(nc.vector.tensor_scalar(left, pos, float(P), None, ALU.is_ge))
            for j in range(2, NT):
                link(nc.vector.scalar_tensor_tensor(left, pos, float(j * P), left, ALU.is_ge, ALU.add))
            link(nc.vector.tensor_scalar(dest, pos, float(SLOTS), None, ALU.mult))
            link(nc.vector.scalar_tensor_tensor(dest, left, float(1 - P * SLOTS), dest, ALU.mult, ALU.add))
            link(nc.vector.tensor_tensor(dest, dest, pst.unsqueeze(1).to_broadcast([P, NT, NE]), ALU.add))
            for t in range(NT):
                for k in range(TOPK):
                    for j, (src, dst) in enumerate(((dest, destk[:, t, k:k + 1]), (gt, entry[:, t, k, 1:2]))):
                        last = nc.vector.scalar_tensor_tensor(picked[:, (t % 2 * TOPK + k) * 2 + j, :], C("iota64"),
                                                              idxf[:, t, k:k + 1], src[:, t, :], ALU.is_equal, ALU.mult,
                                                              accum_out=dst)
                nc.vector.tensor_scalar(gk[:, t, :], C("pcol").to_broadcast([P, TOPK]), float(t * P), None, ALU.add)
                link(last)
                link(nc.vector.tensor_copy(slot_no[:, t, :], destk[:, t, :]))
                nc.vector.tensor_copy(entry_u[:, t, :, 0], gk[:, t, :]).then_inc(s_ent, 1)
                if 1 <= t < NT - 1:
                    hidden(t + 1)

        @block.gpsimd
        def _(pool):
            for c in range(KC):
                pool.wait_ge(s_mul, 2 * c + 2)
                nc.gpsimd.tensor_tensor(mixT[:, c, :], mixT[:, c, :], prod[:, c % 2, :], ALU.add).then_inc(s_mix, 1)
            pool.wait_ge(s_tab, 16)
            for t in range(NT):
                pool.wait_ge(s_ent, t + 1)
                for k in range(TOPK):
                    pool.indirect_dma_start(tab_d, bass.IndirectOffsetOnAxis(ap=slot_no[:, t, k:k + 1], axis=0),
                                            entry_u[:, t, k, :], None).then_inc(s_scat, 16)
            pool.wait_ge(s_scat, 16 * NT * TOPK)
            pool.dma_start(env["table"], tab_d.rearrange("(p b) w -> p (b w)", p=P)).then_inc(s_tl, 16)
            pool.wait_ge(s_tl, 16)


def load_gate_up(eng, env, u, e):
    a = env["a"]
    for h, name in enumerate(("w_exp_gate", "w_exp_up")):
        w = a[name][0].rearrange("e (p k) f -> e p (k f)", k=KC)
        eng.dma_start(env["wgu"][u][:, h].rearrange("p k f -> p (k f)"),
                      w[bass.ds(e, 1)].rearrange("a p n -> p (a n)")).then_inc(env["s_gate_up"][u], 16)


def load_down(eng, env, u, e):
    w = env["a"]["w_exp_down"][0].rearrange("e (p j) n -> e p (j n)", j=2)
    eng.dma_start(env["wd"][u].rearrange("p j n -> p (j n)"), w[bass.ds(e, 1)].rearrange("a p n -> p (a n)")
                  ).then_inc(env["s_down"][u], 16)


def expert_stage(env):
    nc, a, ps, R, C, sem = (env[k] for k in ("nc", "a", "ps", "R", "C", "sem"))
    h2_d, acc_d, counts = env["h2_d"], env["acc_d"], env["counts"]
    table = env["table"].rearrange("p (b w) -> p b w", w=2)
    ring = R["ring"]
    wgu = env["wgu"]
    wd = env["wd"]
    yb = carve(ring[:, 12288:14336], (2, D))
    xg = carve(ring[:, 14336:16384], (2, D))
    xT = carve(R["Q"], (2, D))
    hs, hT, sg = carve(R["Q"][:, 2 * D:], (2, FE), (2, FE), (2, FE))
    gidx = R["small"][:, 0:2].bitcast(U32)
    sidx = R["small"][:, 2:4].bitcast(U32)
    s_w = env["s_gate_up"]
    s_wd = env["s_down"]
    s_z, s_gi, s_si = env["s_zeros"], sem("e_gather_index"), sem("e_scatter_index")
    s_g = [sem("e_gathered_even"), sem("e_gathered_odd")]
    s_t, s_xa, s_xv = sem("e_turned"), sem("e_xT_by_act"), sem("e_xT_by_dve")
    s_gu, s_sg, s_v, s_hs = sem("e_gu"), sem("e_sigmoid"), sem("e_dve_steps"), sem("e_hidden")
    s_ht, s_hc, s_y, s_ya, s_yv, s_sc = (sem("e_hidden_turned"), sem("e_hT"), sem("e_y"), sem("e_y_by_act"),
                                         sem("e_y_by_dve"), sem("e_scattered"))

    def last_pair(eng):
        return eng.value_load(counts[0:1, 0:1], min_val=TOK * TOPK // P // 2 - 1, max_val=PAIRS - 2)

    def pairs(eng, body, m):
        for u in range(2):
            body(0, u, first=True)
        with eng.Fori(1, m + 1) as i:
            for u in range(2):
                body(i, u)

    with nc.Block() as block:
        @block.sync
        def _(sp):
            m = last_pair(sp)

            def body(i, u, first=False):
                b = 2 * i + u
                if first:
                    return
                e = sp.value_load(counts[0:1, bass.ds(b + 1, 1)], min_val=0, max_val=NE - 1)
                sp.wait_ge(s_gu, b - 1)
                load_gate_up(sp, env, u, e)
                sp.wait_ge(s_y, b - 1)
                load_down(sp, env, u, e)

            pairs(sp, body, m)

        @block.tensor
        def _(pe):
            m = last_pair(pe)

            def turn(i, u):
                pe.wait_ge(s_g[u], 16 * (i + 1))
                for g in range(2):
                    for k in range(4):
                        last = nc.tensor.transpose(ps[:, 2 + g, k * P:(k + 1) * P],
                                                   xg[:, u, (4 * g + k) * P:(4 * g + k + 1) * P], C("ident"))
                    last.then_inc(s_t, 1)

            def turn_hidden(b, u, wait_bank):
                pe.wait_ge(s_hs, b + 1)
                if wait_bank:
                    pe.wait_ge(s_hc, b)
                for j in range(2):
                    last = nc.tensor.transpose(ps[:, 4, j * P:(j + 1) * P], hs[:, u, j * P:(j + 1) * P], C("ident"))
                last.then_inc(s_ht, 1)

            def down(i, u, b, wait_bank):
                pe.wait_ge(s_hc, b + 1)
                pe.wait_ge(s_wd[u], 16 * (i + 1))
                if wait_bank:
                    pe.wait_ge(s_ya, b)
                    pe.wait_ge(s_yv, b)
                for half in range(2):
                    for j in range(2):
                        last = nc.tensor.matmul(ps[:, 5 + half, :], hT[:, u, j * P:(j + 1) * P],
                                                wd[u][:, j, half * 512:(half + 1) * 512], start=(j == 0), stop=(j == 1))
                last.then_inc(s_y, 1)

            def body(i, u, first=False):
                b = 2 * i + u
                pe.wait_ge(s_xa, b + 1)
                pe.wait_ge(s_xv, b + 1)
                pe.wait_ge(s_w[u], 32 * (i + 1))
                if not first:
                    pe.wait_ge(s_hs, b - 1)
                for k in range(KC):
                    last = nc.tensor.matmul(ps[:, u, :], xT[:, u, k * P:(k + 1) * P], wgu[u][:, :, k, :],
                                            start=(k == 0), stop=(k == KC - 1))
                last.then_inc(s_gu, 1)
                before = not (first and u == 0)
                if before:
                    turn_hidden(b - 1, 1 - u, not first)
                turn(i if u == 0 else i + 1, 1 - u)
                if before:
                    down(i if u == 1 else i - 1, 1 - u, b - 1, not first)

            turn(0, 0)
            pairs(pe, body, m)
            turn_hidden(2 * m + 1, 1, True)
            down(m, 1, 2 * m + 1, True)

        @block.scalar
        def _(act):
            m = last_pair(act)

            def tokens(b, u):
                act.wait_ge(s_t, 2 * b + 1)
                nc.scalar.copy(xT[:, u, 0:512], ps[:, 2, :]).then_inc(s_xa, 1)

            def rows(b, u, wait_buffer):
                act.wait_ge(s_y, b + 1)
                if wait_buffer:
                    act.wait_ge(s_sc, 16 * (b - 1))
                w = table[:, b, 1:2] if isinstance(b, int) else table[:, bass.ds(b, 1), 1:2].rearrange("p a w -> p (a w)")
                nc.scalar.activation(yb[:, u, 0:512], ps[:, 5, :], ACT.Copy, scale=w.bitcast(F32)).then_inc(s_ya, 1)

            def body(i, u, first=False):
                b = 2 * i + u
                act.wait_ge(s_gu, b + 1)
                nc.scalar.activation(sg[:, u, :], ps[:, u, 0:FE], ACT.Sigmoid).then_inc(s_sg, 1)
                tokens(b + 1, 1 - u)
                if not (first and u == 0):
                    rows(b - 1, 1 - u, not first)

            tokens(0, 0)
            pairs(act, body, m)
            rows(2 * m + 1, 1, True)

        @block.vector
        def _(dve):
            m = last_pair(dve)
            st = Steps(dve, s_v)

            def tokens(b, u):
                dve.wait_ge(s_t, 2 * b + 2)
                nc.vector.tensor_copy(xT[:, u, 512:D], ps[:, 3, :]).then_inc(s_xv, 1)

            def hidden_columns(b, u):
                dve.wait_ge(s_ht, b + 1)
                nc.vector.tensor_copy(hT[:, u, :], ps[:, 4, 0:FE]).then_inc(s_hc, 1)

            def rows(b, u, wait_buffer):
                dve.wait_ge(s_y, b + 1)
                if wait_buffer:
                    dve.wait_ge(s_sc, 16 * (b - 1))
                w = table[:, b, 1:2] if isinstance(b, int) else table[:, bass.ds(b, 1), 1:2].rearrange("p a w -> p (a w)")
                nc.vector.tensor_scalar(yb[:, u, 512:D], ps[:, 6, :], w.bitcast(F32), None, ALU.mult).then_inc(s_yv, 1)

            def body(i, u, first=False):
                b = 2 * i + u
                if not (first and u == 0):
                    hidden_columns(b - 1, 1 - u)
                dve.wait_ge(s_sg, b + 1)
                st.loop(b)
                st.link(nc.vector.tensor_tensor(sg[:, u, :], sg[:, u, :], ps[:, u, 0:FE], ALU.mult))
                nc.vector.tensor_tensor(hs[:, u, :].rearrange("q (j p) -> q p j", j=2),
                                        sg[:, u, :].rearrange("q (p j) -> q p j", j=2),
                                        ps[:, u, FE:2 * FE].rearrange("q (p j) -> q p j", j=2), ALU.mult).then_inc(s_hs, 1)
                tokens(b + 1, 1 - u)
                if not (first and u == 0):
                    rows(b - 1, 1 - u, not first)

            tokens(0, 0)
            pairs(dve, body, m)
            hidden_columns(2 * m + 1, 1)
            rows(2 * m + 1, 1, True)

        @block.gpsimd
        def _(pool):
            m = last_pair(pool)
            pool.wait_ge(s_z, 2)

            limit = pool.to_reg(TOK - 1)

            r_gathered, r_turned, r_rows, r_added = [pool.alloc_register(name) for name in (
                "gathered", "turned", "rows", "added")]

            def held(register, value):
                if isinstance(value, int):
                    return value
                pool.reg_mov(register, value)
                return register

            def index(dst, b, s):
                src = table[:, b, 0:1] if isinstance(b, int) else table[:, bass.ds(b, 1), 0:1].rearrange("p a w -> p (a w)")
                nc.gpsimd.tensor_copy(dst, src).then_inc(s, 1)

            def gather(u, b, reuse):
                done = held(r_gathered, b + 1)
                if reuse:
                    turned = held(r_turned, 2 * (b - 1))
                    pool.wait_ge(s_z, 2)
                    pool.wait_ge(s_t, turned)
                index(gidx[:, u:u + 1], b, s_gi)
                pool.wait_ge(s_z, 2)
                pool.wait_ge(s_gi, done)
                pool.indirect_dma_start(xg[:, u, :], None, h2_d, bass.IndirectOffsetOnAxis(ap=gidx[:, u:u + 1], axis=0),
                                        bounds_check=limit, oob_is_err=False).then_inc(s_g[u], 16)

            def scatter(u, b):
                done, added = held(r_rows, b + 1), held(r_added, 16 * b)
                pool.wait_ge(s_z, 2)
                if not (isinstance(b, int) and b == 0):
                    pool.wait_ge(s_sc, added)
                index(sidx[:, u:u + 1], b, s_si)
                pool.wait_ge(s_z, 2)
                pool.wait_ge(s_si, done)
                pool.wait_ge(s_ya, done)
                pool.wait_ge(s_yv, done)
                pool.indirect_dma_start(acc_d, bass.IndirectOffsetOnAxis(ap=sidx[:, u:u + 1], axis=0), yb[:, u, :], None,
                                        compute_op=ALU.add).then_inc(s_sc, 16)

            def body(i, u, first=False):
                b = 2 * i + u
                gather(u, b + 2, True)
                if not (first and u == 0):
                    scatter(1 - u, b - 1)

            gather(0, 0, False)
            gather(1, 1, False)
            pairs(pool, body, m)
            scatter(1, 2 * m + 1)
            pool.wait_ge(s_z, 2)
            pool.wait_ge(s_g[0], 16 * (m + 2))
            pool.wait_ge(s_z, 2)
            pool.wait_ge(s_g[1], 16 * (m + 2))
            pool.wait_ge(s_z, 2)
            pool.wait_ge(s_sc, 32 * m + 32)


def final_stage(env):
    nc, a, o, R, sem = (env[k] for k in ("nc", "a", "o", "R", "sem"))
    acc_d = env["acc_d"]
    x, gate2 = carve(R["x"], (NT, D)), carve(R["qbT"], (2, D))
    acc = carve(R["hT"], (NT, D))
    gain, sq = carve(R["Q"], (D,), (D,))
    ss = carve(R["small"], (NT,))
    s_a = [sem("f_gain_and_first_rows"), sem("f_other_rows")]
    s_x, s_act, s_dve, s_o = sem("f_x2"), sem("f_sumsq_and_root"), sem("f_mean_and_rows"), sem("f_stored")

    s_px = sem("f_pool_steps")
    FIRST_POOL = 3

    def residual(wait, eng, link, t):
        wait.wait_ge(s_a[min(t, 1)], 64 if t else 32)
        link(eng.tensor_tensor(acc[:, t, :], acc[:, t, :], gate2[:, int(t == PT), :], ALU.mult))
        eng.tensor_tensor(x[:, t, :], x[:, t, :], acc[:, t, :], ALU.add).then_inc(s_x if t < FIRST_POOL else s_px, 1)

    with nc.Block() as block:
        @block.sync
        def _(sp):
            for t in range(NT):
                sp.dma_start(acc[:, t, :], acc_d[t * P:(t + 1) * P, :]).then_inc(s_a[min(t, 1)], 16)
            for t in range(NT):
                sp.wait_ge(s_dve, 2 * t + 2)
                dst = o[0][0, t * P:(t + 1) * P, :] if t < PT else o[1].rearrange("b n d -> (b n) d")
                sp.dma_start(dst, acc[:, t, :]).then_inc(s_o, 16)
            sp.wait_ge(s_o, 16 * NT)

        @block.scalar
        def _(act):
            act.dma_start(gain, a["final_g"][None, :].to_broadcast([P, D])).then_inc(s_a[0], 16)
            for t in range(NT):
                if t < FIRST_POOL:
                    act.wait_ge(s_x, t + 1)
                else:
                    act.wait_ge(s_px, 2 * (t - FIRST_POOL) + 2)
                if t:
                    act.wait_ge(s_act, 2 * t)
                nc.scalar.activation(sq, x[:, t, :], ACT.Square, accum_out=ss[:, t:t + 1]).then_inc(s_act, 1)
                act.wait_ge(s_dve, 2 * t + 1)
                nc.scalar.activation(ss[:, t:t + 1], ss[:, t:t + 1], ACT.Sqrt).then_inc(s_act, 1)

        @block.vector
        def _(dve):
            st = env["dve_steps"].resume(dve)

            for t in range(NT):
                if t == 0:
                    residual(dve, nc.vector, st.link, 0)
                if t + 1 < FIRST_POOL:
                    residual(dve, nc.vector, st.link, t + 1)
                dve.wait_ge(s_act, 2 * t + 1)
                nc.vector.tensor_scalar(ss[:, t:t + 1], ss[:, t:t + 1], 1.0 / D, EPS, ALU.mult, ALU.add).then_inc(s_dve, 1)
                dve.wait_ge(s_act, 2 * t + 2)
                st.link(nc.vector.reciprocal(ss[:, t:t + 1], ss[:, t:t + 1]))
                nc.vector.scalar_tensor_tensor(acc[:, t, :], x[:, t, :], ss[:, t:t + 1], gain, ALU.mult,
                                               ALU.mult).then_inc(s_dve, 1)

        @block.gpsimd
        def _(pool):
            st = Steps(pool, s_px)
            for t in range(FIRST_POOL, NT):
                residual(pool, nc.gpsimd, st.link, t)
                st.n += 1


_INS = ['x_prompt', 'x_sample', 'cache_fox_k', 'cache_fox_v', 'cache_fox_logf', 'cache_swa_k', 'cache_swa_v',
        'c_prompt', 'c_sample', 'w_ada', 'b_ada', 'norm1_g', 'w_in', 'fox_b_f', 'w_branch_a', 'w_branch_b',
        'w_out', 'swa_sinks', 'norm2_g', 'w_router', 'router_bias', 'w_exp_gate', 'w_exp_up', 'w_exp_down',
        'w_sh_gate', 'w_sh_up', 'w_sh_down', 'final_g']
OUTS = [(1, SEQ, D), (DB, DN, D),
        (1, 1, SEQ, H, HD), (1, 1, SEQ, H, HD), (1, 1, SEQ, H), (1, 1, SINKW, KVH, HD), (1, 1, SINKW, KVH, HD),
        (1, DB, DN, H, HD), (1, DB, DN, H, HD), (1, DB, DN, H), (1, DB, SINKW, KVH, HD), (1, DB, SINKW, KVH, HD)]


def prepare(inputs, np):
    arrays = {n: np.ascontiguousarray(inputs[n]) for n in _INS}
    arrays["const"] = constants(np)
    empty = np.zeros((SLOTS * P, 2), np.uint32)
    empty[:, 0] = TOK + np.arange(SLOTS * P) // SLOTS
    arrays["empty_table"] = empty
    return arrays


def kernel(**inputs):
    import numpy as _np
    import concourse.bacc as _bacc
    from concourse import mybir as _mybir
    from concourse.bass_utils import run_bass_kernel_spmd as _run

    nc = _bacc.Bacc("TRN2", target_bir_lowering=False, num_devices=1)
    arrays = prepare(inputs, _np)
    a = {n: nc.dram_tensor("in_" + n, v.shape, _mybir.dt.from_np(v.dtype), kind="ExternalInput").ap()
         for n, v in arrays.items()}
    o = [nc.dram_tensor(f"out_{i}", s, _mybir.dt.float32, kind="ExternalOutput").ap() for i, s in enumerate(OUTS)]
    build(nc, a, o)
    r = _run(nc, [{"in_" + n: v for n, v in arrays.items()}], core_ids=[0])
    return tuple(r.results[0][f"out_{i}"] for i in range(len(OUTS)))
```
